# Optimizing a Trainium2 kernel written in Bass

```python
import jax, jax.numpy as jnp
from jax import lax
import numpy as np
import math

D_MODEL = 2048
BATCH = 1
SEQ = 256
DEPTH = 1

D_CONV = D_MODEL // 2
CONV_GROUPS = 16
CONV_WIDTH = 3
D_ATTN = D_MODEL - D_CONV
N_HEADS = 8
HEAD_DIM = D_ATTN // N_HEADS
D_MIX = D_CONV + D_ATTN
D_IN = 4 * D_CONV + 4 * D_ATTN
MOBA_BLOCK = 256
MOBA_TOPK = 3
Q_CHUNK = 64
EPS = 1e-6


def rms_norm(x, gain):
    xf = x.astype(jnp.float32)
    y = xf * lax.rsqrt(jnp.mean(xf * xf, axis=-1, keepdims=True) + EPS)
    return (y * gain.astype(jnp.float32)).astype(x.dtype)

def short_gated_conv(h, b_gate, c_gate, conv_w):
    seq = h.shape[1]
    u = c_gate * h
    u_pad = jnp.pad(u, ((0, 0), (CONV_WIDTH - 1, 0), (0, 0)))
    conv = u_pad[:, 0:seq] * conv_w[0]
    for tap in range(1, CONV_WIDTH):
        conv = conv + u_pad[:, tap:tap + seq] * conv_w[tap]
    return b_gate * conv

def moba_attention(q, k, v):
    bsz, n_heads, seq, hd = q.shape
    n_blocks = -(-seq // MOBA_BLOCK)
    pad = n_blocks * MOBA_BLOCK - seq
    k_pad = jnp.pad(k, ((0, 0), (0, 0), (0, pad), (0, 0)))
    v_pad = jnp.pad(v, ((0, 0), (0, 0), (0, pad), (0, 0)))
    k_blocks = k_pad.reshape(bsz, n_heads, n_blocks, MOBA_BLOCK, hd)
    v_blocks = v_pad.reshape(bsz, n_heads, n_blocks, MOBA_BLOCK, hd)
    k_mean = jnp.mean(k_blocks.astype(jnp.float32), axis=3)
    k_sel = min(MOBA_TOPK, n_blocks)
    scale = hd ** -0.5
    n_chunks = seq // Q_CHUNK
    q_chunks = q.reshape(bsz, n_heads, n_chunks, Q_CHUNK, hd).transpose(2, 0, 1, 3, 4)
    b_idx = jnp.arange(bsz)[:, None, None]
    h_idx = jnp.arange(n_heads)[None, :, None]
    block_ids = jnp.arange(n_blocks)
    slot_ids = jnp.arange(k_sel)
    key_offsets = jnp.arange(MOBA_BLOCK)

    def chunk_fn(args):
        ci, q_blk = args
        start = ci * Q_CHUNK
        own = start // MOBA_BLOCK
        q_pos = start + jnp.arange(Q_CHUNK)
        gate = jnp.einsum('bhqd,bhnd->bhqn', q_blk.astype(jnp.float32), k_mean)
        gate = jnp.where(block_ids < own, gate, -jnp.inf)
        _, sel = lax.top_k(gate, k_sel)
        sel_valid = slot_ids < own
        k_own = lax.dynamic_index_in_dim(k_blocks, own, axis=2, keepdims=False)
        v_own = lax.dynamic_index_in_dim(v_blocks, own, axis=2, keepdims=False)
        s_own = jnp.einsum('bhqd,bhkd->bhqk', q_blk, k_own).astype(jnp.float32) * scale
        k_pos = own * MOBA_BLOCK + key_offsets
        s_own = jnp.where(k_pos[None, :] <= q_pos[:, None], s_own, -jnp.inf)
        scores = []
        for slot in range(k_sel):
            k_g = k_blocks[b_idx, h_idx, sel[..., slot]]
            s = jnp.einsum('bhqd,bhqkd->bhqk', q_blk, k_g).astype(jnp.float32) * scale
            scores.append(jnp.where(sel_valid[slot], s, -jnp.inf))
        scores.append(s_own)
        probs = jax.nn.softmax(jnp.concatenate(scores, axis=-1), axis=-1).astype(v.dtype)
        out = jnp.einsum('bhqk,bhkd->bhqd', probs[..., k_sel * MOBA_BLOCK:], v_own)
        for slot in range(k_sel):
            v_g = v_blocks[b_idx, h_idx, sel[..., slot]]
            p_slot = probs[..., slot * MOBA_BLOCK:(slot + 1) * MOBA_BLOCK]
            out = out + jnp.einsum('bhqk,bhqkd->bhqd', p_slot, v_g)
        return out.astype(q.dtype)

    outs = lax.map(chunk_fn, (jnp.arange(n_chunks), q_chunks))
    return outs.transpose(1, 2, 0, 3, 4).reshape(bsz, n_heads, seq, hd)

def first_inputs(seed: int = 0) -> dict:
    key = jax.random.key(seed)
    ks = jax.random.split(key, 9)
    x = jax.random.normal(ks[0], (BATCH, SEQ, D_MODEL), jnp.float32)
    norm_gain = 1.0 + 0.1 * jax.random.normal(ks[1], (DEPTH, D_MODEL), jnp.float32)
    w_in = jax.random.normal(ks[2], (DEPTH, D_MODEL, D_IN), jnp.float32) * D_MODEL ** -0.5
    conv_w = jax.random.normal(ks[3], (DEPTH, CONV_WIDTH, D_CONV), jnp.float32) * CONV_WIDTH ** -0.5
    q_norm_gain = 1.0 + 0.1 * jax.random.normal(ks[4], (DEPTH, HEAD_DIM), jnp.float32)
    k_norm_gain = 1.0 + 0.1 * jax.random.normal(ks[5], (DEPTH, HEAD_DIM), jnp.float32)
    conv_out_gain = 1.0 + 0.1 * jax.random.normal(ks[6], (DEPTH, D_CONV), jnp.float32)
    attn_out_gain = 1.0 + 0.1 * jax.random.normal(ks[7], (DEPTH, D_ATTN), jnp.float32)
    w_out = jax.random.normal(ks[8], (DEPTH, D_MIX, D_MODEL), jnp.float32) * D_MIX ** -0.5
    return {"x": x, "norm_gain": norm_gain, "w_in": w_in, "conv_w": conv_w,
            "q_norm_gain": q_norm_gain, "k_norm_gain": k_norm_gain,
            "conv_out_gain": conv_out_gain, "attn_out_gain": attn_out_gain, "w_out": w_out}

def first_block(x, norm_gain, w_in, conv_w, q_norm_gain, k_norm_gain, conv_out_gain, attn_out_gain, w_out):
    bsz, seq, _ = x.shape
    split_points = [D_CONV, 2 * D_CONV, 3 * D_CONV, 4 * D_CONV,
                    4 * D_CONV + D_ATTN, 4 * D_CONV + 2 * D_ATTN, 4 * D_CONV + 3 * D_ATTN]
    for layer in range(DEPTH):
        h = rms_norm(x, norm_gain[layer])
        proj = jnp.einsum('bsd,de->bse', h, w_in[layer])
        h_conv, b_gate, c_gate, z_conv, q, k, v, z_attn = jnp.split(proj, split_points, axis=-1)
        y_conv = short_gated_conv(h_conv, b_gate, c_gate, conv_w[layer])
        y_conv = rms_norm(y_conv, conv_out_gain[layer]) * jax.nn.silu(z_conv)
        q = rms_norm(q.reshape(bsz, seq, N_HEADS, HEAD_DIM), q_norm_gain[layer]).transpose(0, 2, 1, 3)
        k = rms_norm(k.reshape(bsz, seq, N_HEADS, HEAD_DIM), k_norm_gain[layer]).transpose(0, 2, 1, 3)
        v = v.reshape(bsz, seq, N_HEADS, HEAD_DIM).transpose(0, 2, 1, 3)
        y_attn = moba_attention(q, k, v).transpose(0, 2, 1, 3).reshape(bsz, seq, D_ATTN)
        y_attn = rms_norm(y_attn, attn_out_gain[layer]) * jax.nn.silu(z_attn)
        y = jnp.concatenate([y_conv, y_attn], axis=-1)
        x = x + jnp.einsum('bse,ed->bsd', y, w_out[layer])
    return x


CONV_WIDTH_2 = D_MODEL // 2
CONV_KERNEL = 31
SSM_WIDTH = D_MODEL // 2
SSM_GROUP = 16
SSM_GROUPS = SSM_WIDTH // SSM_GROUP
SSM_STATE = 64
N_BRANCHES = 2
IN_WIDTH = 2 * CONV_WIDTH_2 + SSM_WIDTH + N_BRANCHES * D_MODEL
PEER_HEADS = 8
PEER_KEYS = 128
PEER_EXPERTS = PEER_KEYS * PEER_KEYS
PEER_QDIM = 256
PEER_HALF = PEER_QDIM // 2
PEER_TOPK = 16
PEER_TOKEN_BLOCK = 128
RMS_EPS = 1e-6
LN_EPS = 1e-5
DT_MIN = 1e-3
DT_MAX = 1e-1


def rmsnorm(x, g):
    xf = x.astype(jnp.float32)
    y = xf * lax.rsqrt(jnp.mean(xf * xf, axis=-1, keepdims=True) + RMS_EPS)
    return (y * g.astype(jnp.float32)).astype(x.dtype)

def layernorm(x, g, b):
    xf = x.astype(jnp.float32)
    mu = jnp.mean(xf, axis=-1, keepdims=True)
    var = jnp.mean(jnp.square(xf - mu), axis=-1, keepdims=True)
    y = (xf - mu) * lax.rsqrt(var + LN_EPS)
    return (y * g.astype(jnp.float32) + b.astype(jnp.float32)).astype(x.dtype)

def conformer_conv(a, w_dw, b_dw, ln_g, ln_b, w_pw):
    glu = a[..., :CONV_WIDTH_2] * jax.nn.sigmoid(a[..., CONV_WIDTH_2:])
    padded = jnp.pad(glu, ((0, 0), (CONV_KERNEL - 1, 0), (0, 0)))
    y = lax.conv_general_dilated(
        padded, w_dw.astype(glu.dtype)[:, None, :], window_strides=(1,), padding='VALID',
        dimension_numbers=('NWC', 'WIO', 'NWC'), feature_group_count=CONV_WIDTH_2)
    y = y + b_dw.astype(glu.dtype)
    y = jax.nn.silu(layernorm(y, ln_g, ln_b))
    return y @ w_pw

def s5_ssm(u, a_re, a_im, log_dt, b_re, b_im, c_re, c_im, d_skip, w_val, w_gate):
    bsz, seq, _ = u.shape
    uf = u.astype(jnp.float32)
    ug = uf.reshape(bsz, seq, SSM_GROUPS, SSM_GROUP)
    lam = lax.complex(a_re.astype(jnp.float32), a_im.astype(jnp.float32))
    dt = jnp.exp(log_dt.astype(jnp.float32))[:, None]
    lam_bar = jnp.exp(lam * dt)
    b_mat = lax.complex(b_re.astype(jnp.float32), b_im.astype(jnp.float32))
    b_bar = ((lam_bar - 1.0) / lam)[..., None] * b_mat
    bu = jnp.einsum('gph,bsgh->bsgp', b_bar, ug.astype(jnp.complex64))
    a_seq = jnp.broadcast_to(lam_bar[None, None], (1, seq, SSM_GROUPS, SSM_STATE))

    def combine(left, right):
        a_l, b_l = left
        a_r, b_r = right
        return a_r * a_l, a_r * b_l + b_r

    _, states = lax.associative_scan(combine, (a_seq, bu), axis=1)
    y = (jnp.einsum('ghp,bsgp->bsgh', c_re.astype(jnp.float32), jnp.real(states))
         - jnp.einsum('ghp,bsgp->bsgh', c_im.astype(jnp.float32), jnp.imag(states)))
    y = y.reshape(bsz, seq, SSM_WIDTH) + d_skip.astype(jnp.float32) * uf
    z = jax.nn.gelu(y).astype(u.dtype)
    return (z @ w_val) * jax.nn.sigmoid(z @ w_gate)

def peer(h, w_q, sub_keys, u_tab, v_tab):
    bsz, seq, d = h.shape
    tokens = h.reshape(bsz * seq // PEER_TOKEN_BLOCK, PEER_TOKEN_BLOCK, d)

    def block(xb):
        q = (xb @ w_q).reshape(PEER_TOKEN_BLOCK, PEER_HEADS, 2, PEER_HALF)
        s = jnp.einsum('thcd,hcnd->thcn', q, sub_keys).astype(jnp.float32)
        s_top, i_top = lax.top_k(s, PEER_TOPK)
        cand = s_top[:, :, 0, :, None] + s_top[:, :, 1, None, :]
        cand_idx = i_top[:, :, 0, :, None] * PEER_KEYS + i_top[:, :, 1, None, :]
        cand = cand.reshape(PEER_TOKEN_BLOCK, PEER_HEADS, PEER_TOPK * PEER_TOPK)
        cand_idx = cand_idx.reshape(PEER_TOKEN_BLOCK, PEER_HEADS, PEER_TOPK * PEER_TOPK)
        best, pos = lax.top_k(cand, PEER_TOPK)
        expert = jnp.take_along_axis(cand_idx, pos, axis=-1)
        gates = jax.nn.softmax(best, axis=-1).astype(xb.dtype)
        u_sel = u_tab[expert]
        v_sel = v_tab[expert]
        act = jax.nn.gelu(jnp.einsum('td,thkd->thk', xb, u_sel))
        return jnp.einsum('thk,thkd->td', gates * act, v_sel)

    out = lax.map(block, tokens)
    return out.reshape(bsz, seq, d)

def second_inputs(seed: int = 0) -> dict:
    key = jax.random.key(seed)
    ks = jax.random.split(key, 32)
    f32 = jnp.float32
    L, D = DEPTH, D_MODEL

    def nrm(k, shape, scale):
        return jax.random.normal(k, shape, f32) * scale

    n_idx = jnp.arange(SSM_STATE, dtype=f32)
    return {
        "x": nrm(ks[0], (BATCH, SEQ, D), 1.0),
        "norm_mix": 1.0 + nrm(ks[1], (L, D), 0.02),
        "w_in": nrm(ks[2], (L, D, IN_WIDTH), D ** -0.5),
        "b_gate": nrm(ks[3], (L, N_BRANCHES * D), 0.01),
        "conv_w_dw": nrm(ks[4], (L, CONV_KERNEL, CONV_WIDTH_2), CONV_KERNEL ** -0.5),
        "conv_b_dw": nrm(ks[5], (L, CONV_WIDTH_2), 0.01),
        "conv_ln_g": 1.0 + nrm(ks[6], (L, CONV_WIDTH_2), 0.02),
        "conv_ln_b": nrm(ks[7], (L, CONV_WIDTH_2), 0.01),
        "conv_w_out": nrm(ks[8], (L, CONV_WIDTH_2, D), CONV_WIDTH_2 ** -0.5),
        "ssm_a_re": -0.5 + nrm(ks[9], (L, SSM_GROUPS, SSM_STATE), 0.01),
        "ssm_a_im": math.pi * n_idx + nrm(ks[10], (L, SSM_GROUPS, SSM_STATE), 0.01),
        "ssm_log_dt": jax.random.uniform(ks[11], (L, SSM_GROUPS), f32, math.log(DT_MIN), math.log(DT_MAX)),
        "ssm_b_re": nrm(ks[12], (L, SSM_GROUPS, SSM_STATE, SSM_GROUP), (2.0 * SSM_GROUP) ** -0.5),
        "ssm_b_im": nrm(ks[13], (L, SSM_GROUPS, SSM_STATE, SSM_GROUP), (2.0 * SSM_GROUP) ** -0.5),
        "ssm_c_re": nrm(ks[14], (L, SSM_GROUPS, SSM_GROUP, SSM_STATE), (2.0 * SSM_STATE) ** -0.5),
        "ssm_c_im": nrm(ks[15], (L, SSM_GROUPS, SSM_GROUP, SSM_STATE), (2.0 * SSM_STATE) ** -0.5),
        "ssm_d": nrm(ks[16], (L, SSM_WIDTH), 1.0),
        "ssm_w_val": nrm(ks[17], (L, SSM_WIDTH, D), SSM_WIDTH ** -0.5),
        "ssm_w_gate": nrm(ks[18], (L, SSM_WIDTH, D), SSM_WIDTH ** -0.5),
        "w_out": nrm(ks[19], (L, D, D), D ** -0.5),
        "norm_ffn": 1.0 + nrm(ks[20], (L, D), 0.02),
        "peer_w_q": nrm(ks[21], (L, D, PEER_HEADS * PEER_QDIM), D ** -0.5),
        "peer_sub_keys": nrm(ks[22], (L, PEER_HEADS, 2, PEER_KEYS, PEER_HALF), PEER_HALF ** -0.5),
        "peer_u": nrm(ks[23], (L, PEER_EXPERTS, D), D ** -0.5),
        "peer_v": nrm(ks[24], (L, PEER_EXPERTS, D), PEER_HEADS ** -0.5),
        "norm_final": 1.0 + nrm(ks[25], (D,), 0.02),
    }

def second_block(x, norm_mix, w_in, b_gate, conv_w_dw, conv_b_dw, conv_ln_g, conv_ln_b, conv_w_out,
              ssm_a_re, ssm_a_im, ssm_log_dt, ssm_b_re, ssm_b_im, ssm_c_re, ssm_c_im, ssm_d,
              ssm_w_val, ssm_w_gate, w_out, norm_ffn, peer_w_q, peer_sub_keys, peer_u, peer_v,
              norm_final):
    bsz, seq, _ = x.shape
    for l in range(DEPTH):
        h = rmsnorm(x, norm_mix[l])
        proj = h @ w_in[l]
        conv_in = proj[..., :2 * CONV_WIDTH_2]
        ssm_in = proj[..., 2 * CONV_WIDTH_2:2 * CONV_WIDTH_2 + SSM_WIDTH]
        gate_in = proj[..., 2 * CONV_WIDTH_2 + SSM_WIDTH:]
        branch_conv = conformer_conv(conv_in, conv_w_dw[l], conv_b_dw[l], conv_ln_g[l], conv_ln_b[l], conv_w_out[l])
        branch_ssm = s5_ssm(ssm_in, ssm_a_re[l], ssm_a_im[l], ssm_log_dt[l], ssm_b_re[l], ssm_b_im[l],
                            ssm_c_re[l], ssm_c_im[l], ssm_d[l], ssm_w_val[l], ssm_w_gate[l])
        gates = jax.nn.sigmoid(gate_in + b_gate[l]).reshape(bsz, seq, N_BRANCHES, D_MODEL)
        merged = gates[:, :, 0, :] * branch_conv + gates[:, :, 1, :] * branch_ssm
        x = x + merged @ w_out[l]
        h = rmsnorm(x, norm_ffn[l])
        x = x + peer(h, peer_w_q[l], peer_sub_keys[l], peer_u[l], peer_v[l])
    return rmsnorm(x, norm_final)


def setup_inputs(seed=0):
    out = dict(first_inputs(seed))
    for name, value in second_inputs(seed + 1).items():
        if name != "x":
            out[name + "_2"] = value
    return out


def reference(
    x, norm_gain, w_in, conv_w, q_norm_gain, k_norm_gain, conv_out_gain, attn_out_gain, w_out,
    norm_mix_2, w_in_2, b_gate_2, conv_w_dw_2, conv_b_dw_2, conv_ln_g_2, conv_ln_b_2,
    conv_w_out_2, ssm_a_re_2, ssm_a_im_2, ssm_log_dt_2, ssm_b_re_2, ssm_b_im_2, ssm_c_re_2,
    ssm_c_im_2, ssm_d_2, ssm_w_val_2, ssm_w_gate_2, w_out_2, norm_ffn_2, peer_w_q_2,
    peer_sub_keys_2, peer_u_2, peer_v_2, norm_final_2,
):
    x = first_block(
        x, norm_gain, w_in, conv_w, q_norm_gain, k_norm_gain, conv_out_gain, attn_out_gain,
        w_out,
    )
    return second_block(
        x, norm_mix_2, w_in_2, b_gate_2, conv_w_dw_2, conv_b_dw_2, conv_ln_g_2, conv_ln_b_2,
        conv_w_out_2, ssm_a_re_2, ssm_a_im_2, ssm_log_dt_2, ssm_b_re_2, ssm_b_im_2, ssm_c_re_2,
        ssm_c_im_2, ssm_d_2, ssm_w_val_2, ssm_w_gate_2, w_out_2, norm_ffn_2, peer_w_q_2,
        peer_sub_keys_2, peer_u_2, peer_v_2, norm_final_2,
    )


_drawn_inputs = setup_inputs


def setup_inputs(seed=0):
    import zlib

    import numpy as np

    out = dict(_drawn_inputs(seed))
    spreads = {}
    factors = {'norm_mix_2': 3.772,
     'b_gate_2': 26.162,
     'conv_b_dw_2': 13.373,
     'conv_ln_g_2': 13.105,
     'conv_ln_b_2': 24.348,
     'ssm_a_re_2': 64.0,
     'ssm_a_im_2': 19.653,
     'ssm_log_dt_2': 20.602,
     'ssm_b_re_2': 31.662,
     'ssm_b_im_2': 31.44,
     'ssm_c_re_2': 32.6,
     'ssm_c_im_2': 30.749,
     'norm_final_2': 20.167,
     'norm_ffn_2': 13.841}
    for name, (base, spread) in spreads.items():
        noise = np.random.default_rng([zlib.crc32(name.encode()), seed]).standard_normal(out[name].shape)
        drawn = base * np.exp(spread * noise) if base else spread * noise
        out[name] = __import__('jax').numpy.asarray(drawn.astype(out[name].dtype))
    for name, factor in factors.items():
        out[name] = (out[name] * factor).astype(out[name].dtype)
    return out
```

```python
from contextlib import ExitStack, contextmanager

import concourse.bass as bass
import concourse.mybir as mybir

F32 = mybir.dt.float32
I32 = mybir.dt.int32
U32 = mybir.dt.uint32
ALU = mybir.AluOpType
ACT = mybir.ActivationFunctionType
AX_X = mybir.AxisListType.X

P = 128
T = 256
TT = T // P
D = 2048
KD = D // P
HALF = D // 2
KH = HALF // P
HEADS = 8
HEAD_DIM = P
EPS = 1e-6
LN_EPS = 1e-5

GROUPS, STATE, GCH = 64, 64, 16
PAIRS = GROUPS // 2
HPAIRS = PAIRS // 2
CHUNK = 16
CHUNKS = T // CHUNK
TAPS2 = 31

PEER_H, PEER_K, KEYS = 8, 16, 128
PICKS = PEER_H * PEER_K

RING = 4
SLAB = 4096
PSLOTS = 2
SQ = 4

TILE_IN = 0
TILE_OUT = TILE_IN + 64
TILE_IN2 = TILE_OUT + 16
TILE_VG = TILE_IN2 + 56
TILE_CV = TILE_VG + 32
TILE_OUT2 = TILE_CV + 16
TILE_WQ = TILE_OUT2 + 16
RND_IN, RND_OUT, RND_IN2, RND_VG, RND_CV, RND_OUT2, RND_WQ = 0, 8, 10, 17, 19, 20, 22

Q0, K0, V0, ZA0, HC0, BG0, CG0, ZC0 = range(0, 64, 8)
GLU0, SIG0, SSM0, GA0, GB0, CONV0 = 0, 8, 16, 24, 40, 56
VAL0, VSIG0 = 8, 12
SUBK0, SUBT0 = 40, 16
TOPK0 = 48

C_NORM, C_MIX, C_FFN, C_COUT, C_AOUT, C_CONV, C_QG, C_KG = 0, 16, 32, 48, 56, 64, 88, 89
C_GATE, C_CB, C_LNG, C_LNB, C_SKIP = 128, 160, 168, 176, 184
C_TAP = 256

MAGIC = 12582912.0


class Chain:

    def __init__(self, eng, sem):
        self.eng, self.sem, self.n, self.base = eng, sem, 0, 0

    def step(self, ins):
        ins.then_inc(self.sem, 1)
        self.n += 1

    def wait(self):
        self.eng.wait_ge(self.sem, self.base + self.n)

    def do(self, ins):
        self.step(ins)
        self.wait()

    @contextmanager
    def loop(self, start, end, steps):
        before = self.n
        with self.eng.Fori(start, end) as i:
            self.base, self.n = i * steps + (before - start * steps), 0
            yield i
            assert self.n == steps, (self.n, steps)
        self.base, self.n = 0, before + (end - start) * steps


def build(nc, d):
    ctx = ExitStack()
    with ctx:
        def sb(name, shape, dt=F32):
            return ctx.enter_context(nc.sbuf_tensor(name, shape, dt))

        def sem(name):
            return ctx.enter_context(nc.semaphore(name))

        ring = sb("weight_ring", [P, RING, SLAB])
        slots = sb("slots", [P, 64, T])
        x_t = sb("residual_t", [P, KD, T])
        h_t = sb("normed_t", [P, KD, T])
        work = sb("work", [P, 8192])
        norm_ws = sb("norm_ws", [P, 2048])
        ident = sb("ident", [P, P])
        ones = sb("ones", [P, P])
        params = sb("params", [P, 512])
        lam_f = sb("lam_f", [P, 4, PAIRS])
        powers = sb("powers", [P, 2, CHUNK, PAIRS])
        small = sb("small", [P, 64])
        pick_stage = sb("pick_stage", [P, 16], U32)
        ps = ctx.enter_context(nc.psum_tensor("ps", [P, 8, 512], F32))

        slots_f = slots[:, :, :].rearrange("p a b -> p (a b)")
        ring_f = ring[:, :, :].rearrange("p a b -> p (a b)")
        x_f = x_t[:, :, :].rearrange("p a b -> p (a b)")
        h_f = h_t[:, :, :].rearrange("p a b -> p (a b)")

        def slot(s, n=1):
            if isinstance(s, int):
                return slots_f[:, s * T:(s + n) * T]
            return slots_f[:, bass.ds(s * T, n * T)]

        sdev, rstd = norm_ws[:, 0:512], norm_ws[:, 512:1024]
        sq = norm_ws[:, 1024:2048].rearrange("p (a b) -> p a b", a=SQ)
        eps_c, ln_eps_c = small[:, 0:1], small[:, 1:2]
        att_nmax, att_max, att_sum, att_rsum = small[:, 2:4], small[:, 4:6], small[:, 6:8], small[:, 8:10]
        out_ss, out_sd, out_rs = small[:, 10:12], small[:, 12:14], small[:, 14:16]
        head_max, head_sum, head_rs = small[:, 16:24], small[:, 24:32], small[:, 32:40]

        x_tok0 = work[:, 0:4096].rearrange("p (a b) -> p a b", a=TT)
        att_qk, att_v = work[:, 0:512], work[:, 512:768]
        att_vtok = work[:, 768:1024].rearrange("p (a b) -> p a b", a=2)
        att_s, att_p, att_pt = work[:, 1024:1408], work[:, 1408:1792], work[:, 1792:2176]
        b_nat = work[:, 2176:3200].rearrange("p (c r h) -> p c r h", c=2, r=PAIRS)
        mask = work[:, 3200:3584]
        b_diag = work[:, 4096:6144].rearrange("p (c r h) -> p c r h", c=2, r=PAIRS)
        c_diag = work[:, 6144:8192].rearrange("p (c a b) -> p c a b", c=2, a=KH)
        xs = work[:, :].rearrange("p (c r t) -> p c r t", c=2, r=HPAIRS)
        xs_j = work[:, :].rearrange("p (a j) -> p a j", j=CHUNK)
        xs_cj = work[:, :].rearrange("p (a k j) -> p a k j", k=CHUNKS, j=CHUNK)
        glu_pad = work[:, 0:KH * (T + TAPS2 - 1)].rearrange("p (a b) -> p a b", a=KH)
        h_tok = work[:, 0:4096].rearrange("p (a b) -> p a b", a=TT)
        y_tok = work[:, 4096:8192].rearrange("p (a b) -> p a b", a=TT)
        vec = slots_f[:, 60 * T:62 * T].rearrange("p (a b) -> p a b", a=4)
        bt = slots_f[:, 56 * T:64 * T].rearrange("p (c a b) -> p c a b", c=2, a=KH)
        ct = slots_f[:, 48 * T:56 * T].rearrange("p (c a b) -> p c a b", c=2, a=KH)
        subk = slots_f[:, SUBK0 * T:(SUBK0 + 8) * T].rearrange("p (a b) -> p a b", a=16)
        subt = slots_f[:, SUBT0 * T:(SUBT0 + 8) * T].rearrange("p (a b) -> p a b", a=16)
        key_s = x_f.rearrange("p (t a b) -> p t a b", t=TT, a=16)
        diag = x_f[:, 0:2048].rearrange("p (a b) -> p a b", a=16)
        gain_b = x_f[:, 2048:4096]
        tk = slots_f[:, TOPK0 * T:64 * T]
        tk_s, tk_if = tk[:, 0:256], tk[:, 256:512]
        tk_iu = tk[:, 512:768].bitcast(U32)
        tk_cand, tk_best = tk[:, 768:1024], tk[:, 1024:1152]
        tk_pos, tk_hi, tk_lo = (tk[:, 1152 + 128 * n:1280 + 128 * n].bitcast(U32) for n in range(3))
        tk_hif, tk_lof, tk_e1, tk_e2 = (tk[:, 1536 + 128 * n:1664 + 128 * n] for n in range(4))
        picks = tk[:, 2048:2304].bitcast(U32)
        gates, dots, pick_w = tk[:, 2304:2560], tk[:, 2560:2816], tk[:, 2816:3072]
        iota16 = tk[:, 3072:3088]
        zero_row = tk[:, 3088:3600]
        onehot = norm_ws[:, :]
        rows = [ring_f[:, n * D:(n + 1) * D] for n in range(8)] + [h_f[:, n * D:(n + 1) * D] for n in range(2)] \
            + [slots_f[:, n * D:(n + 1) * D] for n in range(6)]
        ROWS = len(rows)
        PE_ROWS = 12

        ps_p = ps[:, 0:PSLOTS, 0:T]
        ps_m = ps[:, 2:4, :]
        ps_n, ps_s, ps_pt, ps_o = ps[:, 4, :], ps[:, 5, 0:384], ps[:, 6, 0:384], ps[:, 7, 0:T]
        ps_v = ps[:, 0:4, :]

        x_in = [sem(f"x_in{t}") for t in range(TT)]
        slab_landed = [sem(f"slab_landed{b}") for b in range(RING)]
        vec_in, ssm_in, b_in, c_in, subk_in, gain_in = (sem(n) for n in ("vec_in", "ssm_in", "b_in", "c_in", "subk_in", "gain_in"))
        consts_ready, cdiag_cleared, mask_ready = sem("consts_ready"), sem("cdiag_cleared"), sem("mask_ready")
        consts_set, mask_set = sem("consts_set"), sem("mask_set")
        eps_ready = sem("eps_ready")
        proj_done, proj_freed = sem("proj_done"), sem("proj_freed")
        misc_done, misc_freed = sem("misc_done"), sem("misc_freed")
        squared, sq_summed = sem("squared"), sem("sq_summed")
        rooted, rstd_ready, h_scaled = sem("rooted"), sem("rstd_ready"), sem("h_scaled")
        dve_step = sem("dve_step")
        ssm_coef, bdiag_ready, powers_ready = sem("ssm_coef"), sem("bdiag_ready"), sem("powers_ready")
        head_squared, head_summed, qk_ready, v_copied, v_turned, v_ready = (
            sem(n) for n in ("head_squared", "head_summed", "qk_ready", "v_copied", "v_turned", "v_ready"))
        scores_done, nmax_ready, exp_ready, probs_ready, probs_turned, pt_ready, out_done, out_ready = (
            sem(n) for n in ("scores_done", "nmax_ready", "exp_ready", "probs_ready", "probs_turned", "pt_ready",
                             "out_done", "out_ready"))
        za_silu, yconv_raw, y_final = sem("za_silu"), sem("yconv_raw"), sem("y_final")
        scanned, ssm_sum, z_ready, conv_done, centred, ln_scaled, conv_act = (
            sem(n) for n in ("scanned", "ssm_sum", "z_ready", "conv_done", "centred", "ln_scaled", "conv_act"))
        val_gated, merged = sem("val_gated"), sem("merged")
        picks_ready, best_ready, best_exp, dots_ready, gelu_ready, w_ready, diag_ready = (
            sem(n) for n in ("picks_ready", "best_ready", "best_exp", "dots_ready", "gelu_ready", "w_ready", "diag_ready"))
        staged, zero_ready = [sem(f"staged{half}") for half in range(2)], sem("zero_ready")
        gathered = [sem(f"gathered{n}") for n in range(ROWS)]
        row_free = [sem(f"row_free{n}") for n in range(ROWS)]
        v_summed, v_read, y_ready, out_squared, out_rooted, normed, stored = (
            sem(n) for n in ("v_summed", "v_read", "y_ready", "out_squared", "out_rooted", "normed", "stored"))

        def freed(n):
            return n + PSLOTS

        M_X = 0
        M_VEC = M_X + 8
        M_LAM = M_VEC + 1
        M_BC = M_LAM + 1
        M_BU = [M_BC + 8, M_BC + 8 + 20]
        M_CY = [M_BU[0] + 16, M_BU[1] + 16]
        M_SUB = M_CY[1] + 4
        M_TOK = M_SUB + 4
        M_S = M_TOK + 16

        block = ctx.enter_context(nc.Block())

        @block.sync
        def _(sp):
            for t in range(TT):
                sp.dma_start(x_tok0[:, t, :], d["x"][0, t * P:(t + 1) * P, :]).then_inc(x_in[t], 16)
            w_in = d["w_in"][0].rearrange("(k p) n -> p k n", p=P)
            w_out = d["w_out"][0].rearrange("(k p) n -> p k n", p=P)
            w_in2 = d["w_in_2"][0].rearrange("(k p) n -> p k n", p=P)
            w_val = d["ssm_w_val_2"][0].rearrange("(k p) n -> p k n", p=P)
            w_gate = d["ssm_w_gate_2"][0].rearrange("(k p) n -> p k n", p=P)
            w_cv = d["conv_w_out_2"][0].rearrange("(k p) n -> p k n", p=P)
            w_out2 = d["w_out_2"][0].rearrange("(k p) n -> p k n", p=P)
            w_q = d["peer_w_q_2"][0].rearrange("(k p) n -> p k n", p=P)

            def slab(b, src):
                dst = ring[:, b, :].rearrange("p (k n) -> p k n", k=src.shape[1])
                sp.dma_start(dst, src).then_inc(slab_landed[b], 16)

            def col(w, c0, n=256):
                return w[:, :, c0:c0 + n] if isinstance(c0, int) else w[:, :, bass.ds(c0, n)]

            for b in range(RING):
                slab(b, col(w_in, 4 * HALF + 256 * b))
            for first, last, base in ((1, 4, 4 * HALF), (4, 8, -4 * HALF)):
                with sp.Fori(first, last) as i:
                    for b in range(RING):
                        sp.wait_ge(proj_done, i * 8 + (2 * b - 6))
                        slab(b, col(w_in, i * 1024 + (base + 256 * b)))
            for i in range(2):
                for b in range(RING):
                    sp.wait_ge(proj_done, TILE_OUT + 8 * i + 2 * b - 6)
                    slab(b, col(w_out, 1024 * i + 256 * b))
            for b in range(RING):
                sp.wait_ge(proj_done, TILE_IN2 + 2 * b - 6)
                slab(b, col(w_in2, 2 * HALF + 256 * b))
            for first, last, base in ((1, 3, -1024), (3, 7, 0)):
                with sp.Fori(first, last) as i:
                    for b in range(RING):
                        sp.wait_ge(proj_done, i * 8 + (TILE_IN2 + 2 * b - 6))
                        slab(b, col(w_in2, i * 1024 + (base + 256 * b)))
            for i in range(2):
                for b in range(RING):
                    sp.wait_ge(proj_done, TILE_VG + (2 * b - 6 if i == 0 else 4 * b + 4))
                    slab(b, col(w_gate if b % 2 else w_val, 512 * (2 * i + b // 2), 512))
            for b in range(RING):
                sp.wait_ge(proj_done, TILE_CV + 4 * b - 12)
                slab(b, col(w_cv, 512 * b, 512))
            for w, tile0 in ((w_out2, TILE_OUT2), (w_q, TILE_WQ)):
                for i in range(2):
                    for b in range(RING):
                        sp.wait_ge(proj_done, tile0 + (4 * b - 12 if w is w_out2 and i == 0 else 8 * i + 2 * b - 6))
                        slab(b, col(w, 1024 * i + 256 * b))
                if w is w_out2:
                    sp.wait_ge(merged, KD)
                    sp.dma_start(subk, d["peer_sub_keys_2"][0].rearrange("h c n e -> n (h c) e")).then_inc(subk_in, 16)
            sp.wait_ge(picks_ready, TT)
            sp.dma_start(gain_b, d["norm_final_2"].partition_broadcast(P)).then_inc(gain_in, 16)
            for t in range(TT):
                sp.wait_ge(normed, t + 1)
                sp.dma_start(d["out"][0, t * P:(t + 1) * P, :], y_tok[:, t, :]).then_inc(stored, 16)
            sp.wait_ge(stored, 16 * TT)

        @block.gpsimd
        def _(pool):
            nc.gpsimd.memset(ident[:, :], 0.0).then_inc(consts_set, 1)
            nc.gpsimd.memset(ones[:, :], 1.0).then_inc(consts_ready, 1)
            pool.wait_ge(consts_set, 1)
            nc.gpsimd.affine_select(out=ident[:, :], in_=ident[:, :], compare_op=ALU.not_equal, fill=1.0, base=0,
                                    pattern=[[-1, P]], channel_multiplier=1).then_inc(consts_ready, 1)
            nc.gpsimd.memset(c_diag, 0.0).then_inc(cdiag_cleared, 1)
            pool.wait_ge(misc_done, M_X + 8)
            nc.gpsimd.memset(mask, 0.0).then_inc(mask_set, 1)
            pool.wait_ge(mask_set, 1)
            for lo in (0, 2 * P):
                nc.gpsimd.affine_select(out=mask[:, lo:lo + P], in_=mask[:, lo:lo + P], compare_op=ALU.is_ge,
                                        fill=-3.0e38, base=0, pattern=[[-1, P]],
                                        channel_multiplier=1).then_inc(mask_ready, 1)

            pool.wait_ge(merged, KD)
            nc.gpsimd.iota(iota16, pattern=[[1, 16]], base=0, channel_multiplier=0,
                           allow_small_or_imprecise_dtypes=True).then_inc(zero_ready, 1)
            nc.gpsimd.memset(zero_row, 0.0).then_inc(zero_ready, 1)

            def gather(t, table, rnd, col0):
                for half in range(2):
                    mine = range(8 * half, 8 * half + 8)
                    for n in mine:
                        pool.wait_ge(row_free[n], rnd + 1)
                    nc.gpsimd.tensor_copy(pick_stage[:, 8 * half:8 * half + 8],
                                          picks[:, bass.ds(col0 + 8 * half, 8)]).then_inc(staged[half], 1)
                    pool.wait_ge(picks_ready, t + 1)
                    pool.wait_ge(staged[half], rnd + 1)
                    for n in mine:
                        nc.gpsimd.indirect_dma_start(
                            rows[n], None, table, bass.IndirectOffsetOnAxis(ap=pick_stage[:, n:n + 1], axis=0),
                        ).then_inc(gathered[n], 16)

            for n in range(ROWS):
                pool.sem_inc(row_free[n], 1)
            for t in range(TT):
                pool.wait_ge(picks_ready, t + 1)
                for v, table in ((0, d["peer_u_2"][0]), (1, d["peer_v_2"][0])):
                    with pool.Fori(0, 8) as i:
                        gather(t, table, i + (16 * t + 8 * v), i * 16 + t * PICKS)

        @block.tensor
        def _(pe):
            def tile(rnd, tile0, t, rhs, kts, order=None, rhs_ready=None):
                per = SLAB // kts // P
                b, n = t // per, t % per
                if n == 0:
                    pe.wait_ge(slab_landed[b], (rnd + 1) * 16)
                pe.wait_ge(proj_freed, tile0 + (t + 1))
                w = ring[:, b, :].rearrange("p (k n) -> p k n", k=kts)
                order = list(range(kts)) if order is None else order
                for k in order:
                    if rhs_ready is not None:
                        pe.wait_ge(rhs_ready[0], rhs_ready[1] + k + 1)
                    mm = nc.tensor.matmul(ps_p[:, t % PSLOTS, :], w[:, k, n * P:(n + 1) * P], rhs(k),
                                          start=(k == order[0]), stop=(k == order[-1]))
                mm.then_inc(proj_done, 1)

            def misc_bank(m, first):
                pe.wait_ge(misc_freed, m if first else m - 1)
                return ps_m[:, m % 2, :]

            def sum_square(n, count, q0, r):
                if n == 0 and r > 1:
                    pe.wait_ge(rooted, r - 1)
                pe.wait_ge(squared, q0 + n + 1)
                nc.tensor.matmul(ps_n[:, 0:T], ones[:, :], sq[:, n % SQ, :], start=(n == 0),
                                 stop=(n == count - 1), skip_group_check=True).then_inc(sq_summed, 1)

            normed_x = lambda k: h_t[:, k, :]

            pe.wait_ge(consts_ready, 2)
            for g in range(4):
                for t in range(TT):
                    m = M_X + TT * g + t
                    if g == 0:
                        pe.wait_ge(x_in[t], 16)
                    bank = misc_bank(m, m == 0) if m >= 2 else ps_m[:, m % 2, :]
                    for j in range(4):
                        k = 4 * g + j
                        tr = nc.tensor.transpose(bank[:, j * P:(j + 1) * P], x_tok0[:, t, k * P:(k + 1) * P], ident[:, :])
                    tr.then_inc(misc_done, 1)
            pe.wait_ge(vec_in, 16 * 14)
            bank = misc_bank(M_VEC, True)
            for j, n in enumerate((90, 64, 124, 124)):
                tr = nc.tensor.transpose(bank[:, j * P:j * P + n], vec[0:n, j, :], ident[0:n, 0:n])
            tr.then_inc(misc_done, 1)
            for n in range(KD):
                sum_square(n, KD, 0, 1)

            with pe.Fori(0, 3) as i:
                for t in range(8):
                    tile(i, i * 8, t, normed_x, KD, rhs_ready=(h_scaled, 0) if t == 0 else None)
            pe.wait_ge(ssm_coef, 1)
            bank = misc_bank(M_LAM, True)
            for j in range(4):
                tr = nc.tensor.transpose(bank[:, j * P:j * P + PAIRS], slot(56 + j // 2)[0:PAIRS, (j % 2) * P:(j % 2 + 1) * P],
                                         ident[0:PAIRS, 0:PAIRS])
            tr.then_inc(misc_done, 1)

            with pe.Fori(0, 4) as i:
                for e in range(2):
                    head = i * 2 + e
                    pe.wait_ge(rooted, head + 1)
                    pe.wait_ge(head_squared, head * 2 + 2)
                    nc.tensor.matmul(ps_n, ones[:, :], norm_ws[:, 1024:1536], start=True, stop=True).then_inc(head_summed, 1)
                    tile(i + 3, i * 8 + 24, 4 * e, normed_x, KD)
                    pe.wait_ge(v_copied, head + 1)
                    pe.wait_ge(out_ready, head + 1)
                    for j in range(2):
                        tr = nc.tensor.transpose(ps_o[:, j * P:(j + 1) * P], att_v[:, j * P:(j + 1) * P], ident[:, :])
                    tr.then_inc(v_turned, 1)
                    pe.wait_ge(qk_ready, head * 2 + 2)
                    nc.tensor.matmul(ps_s[:, 0:P], att_qk[:, 0:P], att_qk[:, T:T + P], start=True, stop=True)
                    nc.tensor.matmul(ps_s[:, P:3 * P], att_qk[:, P:T], att_qk[:, T:2 * T], start=True,
                                     stop=True).then_inc(scores_done, 1)
                    tile(i + 3, i * 8 + 24, 4 * e + 1, normed_x, KD)
                    pe.wait_ge(probs_ready, head * 2 + 2)
                    for j in range(3):
                        tr = nc.tensor.transpose(ps_pt[:, j * P:(j + 1) * P], att_p[:, j * P:(j + 1) * P], ident[:, :])
                    tr.then_inc(probs_turned, 1)
                    tile(i + 3, i * 8 + 24, 4 * e + 2, normed_x, KD)
                    pe.wait_ge(pt_ready, head + 1)
                    pe.wait_ge(v_ready, head + 1)
                    nc.tensor.matmul(ps_o, att_vtok[:, 0, :], att_pt[:, 0:T], start=True, stop=False)
                    nc.tensor.matmul(ps_o[:, P:T], att_vtok[:, 1, :], att_pt[:, T:T + P], start=False,
                                     stop=True).then_inc(out_done, 1)
                    tile(i + 3, i * 8 + 24, 4 * e + 3, normed_x, KD)

            for t in range(8):
                tile(7, 56, t, normed_x, KD)
                sum_square(t, KH, 16, 10)
            for n in range(KH):
                sum_square(n, KH, 24, 11)

            mixed = lambda k: slot(HC0 + k) if k < KH else slot(Q0 + k - KH)
            pe.wait_ge(y_final, 1)
            for t in range(16):
                if t == 0:
                    pe.wait_ge(y_final, 2)
                    pe.wait_ge(proj_freed, freed(TILE_OUT))
                tile(RND_OUT + t // 8, TILE_OUT + 8 * (t // 8), t % 8, mixed, KD, order=[*range(KH, KD), *range(KH)])
                if t >= 2:
                    sum_square(t - 2, KD, 32, 12)
                if t == 7:
                    pe.wait_ge(bdiag_ready, 1)
                    pe.wait_ge(c_in, 16 * 16)
                    for u in range(8):
                        bank = misc_bank(M_BC + u, u == 0)
                        c, half = (u // 2) % 2, u % 2
                        for j in range(4):
                            a = 4 * half + j
                            src = b_diag[:, c, 4 * a:4 * a + 4, :].rearrange("p r h -> p (r h)") if u < 4 else c_diag[:, c, a, :]
                            tr = nc.tensor.transpose(bank[:, j * P:(j + 1) * P], src, ident[:, :])
                        tr.then_inc(misc_done, 1)
            for n in (14, 15):
                sum_square(n, KD, 32, 12)

            pe.wait_ge(proj_freed, freed(TILE_IN2))
            for t in range(8):
                tile(RND_IN2, TILE_IN2, t, normed_x, KD, rhs_ready=(h_scaled, KD) if t == 0 else None)

            def ssm_inputs(half):
                pe.wait_ge(proj_freed, freed(TILE_IN2 + 8))
                for n in range(HPAIRS):
                    pr = HPAIRS * half + n
                    a, j = pr // 4, pr % 4
                    bank = misc_bank(M_BU[half] + n, n == 0)
                    for c in range(2):
                        mm = nc.tensor.matmul(bank[:, c * T:(c + 1) * T], bt[32 * j:32 * j + 32, c, a, :],
                                              slot(SSM0 + a)[32 * j:32 * j + 32, :], start=True, stop=True)
                    mm.then_inc(misc_done, 1)

            def ssm_outputs(half):
                pe.wait_ge(scanned, half + 1)
                for n in range(4):
                    a = 4 * half + n
                    bank = misc_bank(M_CY[half] + n, n == 0)
                    for j in range(4):
                        for c in range(2):
                            mm = nc.tensor.matmul(bank[32 * j:32 * j + 32, 0:T], ct[:, c, a, 32 * j:32 * j + 32],
                                                  xs[:, c, 4 * n + j, :], start=(c == 0), stop=(c == 1))
                    mm.then_inc(misc_done, 1)

            pe.wait_ge(misc_freed, M_BC + 8)
            ssm_inputs(0)
            with pe.Fori(1, 3) as i:
                for t in range(8):
                    tile(i + RND_IN2, i * 8 + TILE_IN2, t, normed_x, KD)
            ssm_outputs(0)
            ssm_inputs(1)
            with pe.Fori(3, 5) as i:
                for t in range(8):
                    tile(i + RND_IN2, i * 8 + TILE_IN2, t, normed_x, KD)
            ssm_outputs(1)
            with pe.Fori(5, 7) as i:
                for t in range(8):
                    tile(i + RND_IN2, i * 8 + TILE_IN2, t, normed_x, KD)

            ssm_z = lambda k: slot(SSM0 + k)
            pe.wait_ge(z_ready, KH)
            for i in range(2):
                for t in range(16):
                    tile(RND_VG + i, TILE_VG + 16 * i, t, ssm_z, KH)
                if i == 0:
                    pe.wait_ge(conv_done, 1)
                    pe.wait_ge(rooted, 12)
                    for n in range(KH):
                        mm = nc.tensor.matmul(ps_n[:, 0:T], ones[:, :], slot(CONV0 + n), start=(n == 0), stop=(n == KH - 1))
                    mm.then_inc(centred, 1)
                    for n in range(KH):
                        sum_square(n, KH, 48, 14)

            conv_y = lambda k: slot(CONV0 + k)
            pe.wait_ge(proj_freed, freed(TILE_CV))
            for t in range(16):
                tile(RND_CV, TILE_CV, t, conv_y, KH, rhs_ready=(conv_act, 0) if t == 0 else None)

            merge = lambda k: slot(GA0 + k)
            for t in range(16):
                tile(RND_OUT2 + t // 8, TILE_OUT2 + 8 * (t // 8), t % 8, merge, KD,
                     rhs_ready=(merged, 0) if t == 0 else None)
                if t >= 2:
                    sum_square(t - 2, KD, 56, 15)
                if t == 7:
                    pe.wait_ge(subk_in, 16)
                    for u in range(4):
                        bank = misc_bank(M_SUB + u, u == 0)
                        for j in range(4):
                            tr = nc.tensor.transpose(bank[:, j * P:(j + 1) * P], subk[:, 4 * u + j, :], ident[:, :])
                        tr.then_inc(misc_done, 1)
            for n in (14, 15):
                sum_square(n, KD, 56, 15)

            def key_scores(u):
                for t in range(TT):
                    bank = misc_bank(M_S + TT * u + t, u == 0 and t == 0)
                    for j in range(4):
                        hc = 4 * u + j
                        mm = nc.tensor.matmul(bank[:, j * P:(j + 1) * P], slot(hc)[:, t * P:(t + 1) * P],
                                              subt[:, hc, :], start=True, stop=True)
                    mm.then_inc(misc_done, 1)

            pe.wait_ge(proj_freed, freed(TILE_WQ))
            for t in range(8):
                tile(RND_WQ, TILE_WQ, t, normed_x, KD, rhs_ready=(h_scaled, 2 * KD) if t == 0 else None)
            for u in range(16):
                bank = misc_bank(M_TOK + u, u == 0)
                src, t, g = (x_t, h_t)[u // 8], (u // 4) % 2, u % 4
                for j in range(4):
                    tr = nc.tensor.transpose(bank[:, j * P:(j + 1) * P], src[:, 4 * g + j, t * P:(t + 1) * P], ident[:, :])
                tr.then_inc(misc_done, 1)
            for u in range(2):
                pe.wait_ge(proj_freed, freed(TILE_WQ + 4 * u + 4))
                key_scores(u)
            for t in range(8):
                tile(RND_WQ + 1, TILE_WQ + 8, t, normed_x, KD)
            for u in range(2, 4):
                pe.wait_ge(proj_freed, freed(TILE_WQ + 4 * u + 4))
                key_scores(u)

            pe.wait_ge(zero_ready, 2)
            pe.wait_ge(misc_freed, M_S + 8)
            for t in range(TT):
                if t > 0:
                    pe.wait_ge(v_read, t)
                for c in range(4):
                    nc.tensor.matmul(ps_v[:, c, :], zero_row[:, 0:P], zero_row, start=True, stop=False, skip_group_check=True)
                with pe.Fori(0, 8) as i:
                    for n in range(PE_ROWS):
                        pe.wait_ge(diag_ready, i * PE_ROWS + (8 * PE_ROWS * t + n + 1))
                        pe.wait_ge(gathered[n], (i + (16 * t + 9)) * 16)
                        for c in range(4):
                            mm = nc.tensor.matmul(ps_v[:, c, :], diag[:, n, :], rows[n][:, c * 512:(c + 1) * 512],
                                                  start=False, stop=False, skip_group_check=True)
                        mm.then_inc(row_free[n], 1)
                for c in range(4):
                    mm = nc.tensor.matmul(ps_v[:, c, :], zero_row[:, 0:P], zero_row, start=False, stop=True, skip_group_check=True)
                mm.then_inc(v_summed, 1)

        @block.scalar
        def _(act):
            def act_copy(dst, src):
                return nc.scalar.activation(dst, src, ACT.Copy)

            def row(j, r, src, n):
                act.dma_start(vec[r:r + n, j, :], src).then_inc(vec_in, 16)

            def rows_of(name, pat="(k p) -> k p"):
                return d[name][0].rearrange(pat, p=P)

            row(0, C_NORM, rows_of("norm_gain"), KD)
            row(0, C_MIX, rows_of("norm_mix_2"), KD)
            row(0, C_FFN, rows_of("norm_ffn_2"), KD)
            row(0, C_COUT, rows_of("conv_out_gain"), KH)
            row(0, C_AOUT, rows_of("attn_out_gain"), KH)
            row(0, C_CONV, rows_of("conv_w", "t (k p) -> (t k) p"), 3 * KH)
            row(0, C_QG, d["q_norm_gain"], 1)
            row(0, C_KG, d["k_norm_gain"], 1)
            row(1, 0, rows_of("b_gate_2"), 32)
            row(1, 32, rows_of("conv_b_dw_2"), KH)
            row(1, 40, rows_of("conv_ln_g_2"), KH)
            row(1, 48, rows_of("conv_ln_b_2"), KH)
            row(1, 56, rows_of("ssm_d_2"), KH)
            taps = rows_of("conv_w_dw_2", "t (k p) -> (t k) p")
            act.dma_start(vec[0:124, 2:4, :], taps.rearrange("(j r) p -> r j p", j=2)).then_inc(vec_in, 16)
            act.dma_start(slot(59)[0:PAIRS, 0:P], d["ssm_a_re_2"][0].rearrange("(r s) p -> r (s p)", s=2)).then_inc(ssm_in, 16)
            act.dma_start(slot(59)[0:PAIRS, P:T], d["ssm_a_im_2"][0].rearrange("(r s) p -> r (s p)", s=2)).then_inc(ssm_in, 16)
            act.dma_start(slot(62)[0:PAIRS, 0:2], d["ssm_log_dt_2"][0].rearrange("(r s) -> r s", s=2)).then_inc(ssm_in, 16)
            act.wait_ge(cdiag_cleared, 1)
            for c, name in enumerate(("ssm_c_re_2", "ssm_c_im_2")):
                src = d[name][0].rearrange("(a g) h p -> g h a p", g=8)
                for g in range(8):
                    act.dma_start(c_diag[GCH * g:GCH * g + GCH, c, :, STATE * (g % 2):STATE * (g % 2) + STATE],
                                  src[g]).then_inc(c_in, 16)
            act.wait_ge(misc_done, M_X + 8)
            for c, name in enumerate(("ssm_b_re_2", "ssm_b_im_2")):
                act.dma_start(b_nat[:, c, :, :], d[name][0].rearrange("(r s) p h -> (s p) r h", s=2)).then_inc(b_in, 16)

            act.wait_ge(eps_ready, 2)

            def square(n, q0, src):
                if q0 + n >= SQ:
                    act.wait_ge(sq_summed, q0 if n < SQ else q0 + n - SQ + 1)
                nc.scalar.activation(sq[:, n % SQ, :], src, ACT.Square).then_inc(squared, 1)

            def root(r, q_end, width, eps=eps_c):
                act.wait_ge(sq_summed, q_end)
                if r > 1:
                    act.wait_ge(rstd_ready, r - 1)
                nc.scalar.activation(sdev[:, 0:T], ps_n[:, 0:T], ACT.Sqrt, bias=eps, scale=1.0 / width).then_inc(rooted, 1)

            def read_out(tile0, n, dst, func=ACT.Copy, **kw):
                act.wait_ge(proj_done, tile0 + (n + 1))
                return nc.scalar.activation(dst, ps_p[:, n % PSLOTS, :], func, **kw).then_inc(proj_freed, 1)

            for n in range(KD):
                act.wait_ge(misc_freed, M_X + TT * (n // 4 + 1))
                square(n, 0, x_t[:, n, :])
            root(1, KD, D)

            with act.Fori(0, 3) as i:
                for t in range(8):
                    read_out(i * 8, t, slot(i * 8 + t))
            act.wait_ge(proj_freed, freed(24))
            with act.Fori(0, 4) as i:
                for e in range(2):
                    head = i * 2 + e
                    act.wait_ge(sq_summed, KD)
                    nc.scalar.activation(sq[:, 0, :], slot(head + Q0), ACT.Square).then_inc(head_squared, 1)
                    nc.scalar.activation(sq[:, 1, :], slot(head + K0), ACT.Square).then_inc(head_squared, 1)
                    act_copy(att_v, slot(head + V0)).then_inc(v_copied, 1)
                    act.wait_ge(head_summed, head + 1)
                    act.wait_ge(rstd_ready, head + 1)
                    nc.scalar.activation(sdev, ps_n, ACT.Sqrt, bias=eps_c, scale=1.0 / HEAD_DIM).then_inc(rooted, 1)
                    read_out(i * 8 + 24, 4 * e, slot(i * 8 + (24 + 4 * e)))
                    for j, (lo, hi) in enumerate(((0, P), (P, 3 * P))):
                        act.wait_ge(nmax_ready, head + 1)
                        nc.scalar.activation(att_p[:, lo:hi], att_s[:, lo:hi], ACT.Exp, bias=att_nmax[:, j:j + 1],
                                             scale=HEAD_DIM ** -0.5, accum_out=att_sum[:, j:j + 1]).then_inc(exp_ready, 1)
                    read_out(i * 8 + 24, 4 * e + 1, slot(i * 8 + (25 + 4 * e)))
                    act.wait_ge(probs_turned, head + 1)
                    act_copy(att_pt, ps_pt).then_inc(pt_ready, 1)
                    read_out(i * 8 + 24, 4 * e + 2, slot(i * 8 + (26 + 4 * e)))
                    act.wait_ge(proj_freed, freed(24))
                    act.wait_ge(out_done, head + 1)
                    act_copy(slot(head + Q0), ps_o).then_inc(out_ready, 1)
                    read_out(i * 8 + 24, 4 * e + 3, slot(i * 8 + (27 + 4 * e)))
            act.wait_ge(proj_freed, freed(32))
            act.wait_ge(out_ready, HEADS + 1)
            for t in range(8):
                square(t, 16, slot(Q0 + t))
                read_out(56, t, slot(ZC0 + t), ACT.Silu)
            nc.scalar.activation(slot(ZA0, KH), slot(ZA0, KH), ACT.Silu).then_inc(za_silu, 1)
            root(10, 24, HALF)
            act.wait_ge(yconv_raw, 1)
            for n in range(KH):
                square(n, 24, slot(HC0 + n))
            root(11, 32, HALF)

            def out_squares(tile0, q0, first_bank, banks, bank_out, wait_slots):
                for n in range(KD):
                    act.wait_ge(proj_freed, freed(tile0 + n + 1))
                    square(n, q0, x_t[:, n, :])
                    if n == 7:
                        for u in range(banks):
                            act.wait_ge(misc_done, first_bank + u + 1)
                            dst, scale = bank_out(u)
                            nc.scalar.activation(dst, ps_m[:, (first_bank + u) % 2, :], ACT.Copy, scale=scale).then_inc(misc_freed, 1)

            def ssm_matrix(u):
                c, half = (u // 2) % 2, u % 2
                dst = (bt if u < 4 else ct)[:, c, 4 * half:4 * half + 4, :].rearrange("p a b -> p (a b)")
                return dst, (-1.0 if u >= 4 and c == 1 else 1.0)

            out_squares(TILE_OUT, 32, M_BC, 8, ssm_matrix, None)
            root(12, 48, D)

            for t in range(8):
                read_out(TILE_IN2, t, slot(SSM0 + t))

            def ssm_inputs(half):
                for n in range(HPAIRS):
                    m = M_BU[half] + n
                    act.wait_ge(misc_done, m + 1)
                    act_copy(xs[:, :, n, :], ps_m[:, m % 2, :].rearrange("p (c t) -> p c t", c=2)).then_inc(misc_freed, 1)

            def ssm_gelu(half):
                for n in range(4):
                    act.wait_ge(ssm_sum, 4 * half + n + 1)
                    nc.scalar.activation(slot(SSM0 + 4 * half + n), slot(SSM0 + 4 * half + n),
                                         ACT.Gelu_apprx_tanh).then_inc(z_ready, 1)

            ssm_inputs(0)
            for t in range(8):
                read_out(TILE_IN2 + 8, t, slot(GLU0 + t))
            for t in range(8):
                read_out(TILE_IN2 + 16, t, slot(SIG0 + t), ACT.Sigmoid)

            def gate_tiles(first):
                with act.Fori(0, 2) as i:
                    for t in range(8):
                        n = first + t
                        read_out(i * 8 + (TILE_IN2 + 24 + first), t, slot(i * 8 + (GA0 + n)), ACT.Sigmoid,
                                 bias=params[:, bass.ds(i * 8 + (C_GATE + n), 1)])

            ssm_inputs(1)
            ssm_gelu(0)
            gate_tiles(0)
            ssm_gelu(1)
            gate_tiles(16)

            def value_tiles(g):
                for t in range(8):
                    if t == 0 and g > 0:
                        act.wait_ge(val_gated, g)
                    if t == 0 and g == 0:
                        act.wait_ge(conv_done, 1)
                    read_out(TILE_VG + 8 * g, t, slot(VAL0 + t), ACT.Copy if t < 4 else ACT.Sigmoid)

            value_tiles(0)
            value_tiles(1)
            act.wait_ge(centred, 1)
            act.wait_ge(rstd_ready, 12)
            nc.scalar.activation(sdev[:, 0:T], ps_n[:, 0:T], ACT.Copy, scale=1.0 / HALF).then_inc(rooted, 1)
            act.wait_ge(centred, 2)
            for n in range(KH):
                square(n, 48, slot(CONV0 + n))
            root(14, 56, HALF, ln_eps_c)
            for n in range(KH):
                act.wait_ge(ln_scaled, n + 1)
                nc.scalar.activation(slot(CONV0 + n), slot(CONV0 + n), ACT.Silu,
                                     bias=params[:, C_LNB + n:C_LNB + n + 1]).then_inc(conv_act, 1)
            value_tiles(2)
            value_tiles(3)

            def keys_out(u):
                return subt[:, 4 * u:4 * u + 4, :].rearrange("p a b -> p (a b)"), 1.0

            out_squares(TILE_OUT2, 56, M_SUB, 4, keys_out, None)
            root(15, 72, D)

            for t in range(8):
                read_out(TILE_WQ, t, slot(t))
            for u in range(16):
                act.wait_ge(misc_done, M_TOK + u + 1)
                dst, t, g = (y_tok, h_tok)[u // 8], (u // 4) % 2, u % 4
                act_copy(dst[:, t, 512 * g:512 * g + 512], ps_m[:, (M_TOK + u) % 2, :]).then_inc(misc_freed, 1)

            def scores_out(u):
                for t in range(TT):
                    m = M_S + TT * u + t
                    act.wait_ge(misc_done, m + 1)
                    act_copy(key_s[:, t, 4 * u:4 * u + 4, :].rearrange("p a b -> p (a b)"), ps_m[:, m % 2, :]).then_inc(misc_freed, 1)

            scores_out(0)
            scores_out(1)
            for t in range(8):
                read_out(TILE_WQ + 8, t, slot(8 + t))
            scores_out(2)
            scores_out(3)

            def softmax_exp(t):
                act.wait_ge(best_ready, t + 1)
                nc.scalar.activation(gates[:, t * P:(t + 1) * P], gates[:, t * P:(t + 1) * P], ACT.Exp).then_inc(best_exp, 1)

            softmax_exp(0)
            for t in range(TT):
                act.wait_ge(dots_ready, (t + 1) * PICKS)
                nc.scalar.activation(pick_w[:, t * P:(t + 1) * P], dots[:, t * P:(t + 1) * P], ACT.Gelu_apprx_tanh).then_inc(gelu_ready, 1)
                act.wait_ge(w_ready, t + 1)
                with act.Fori(0, 8) as i:
                    for n in range(PE_ROWS):
                        act.wait_ge(row_free[n], i + (16 * t + 9))
                        nc.scalar.activation(diag[:, n, :], ident[:, :], ACT.Copy,
                                             scale=pick_w[:, bass.ds(i * 16 + (t * P + n), 1)]).then_inc(diag_ready, 1)
                if t == 0:
                    softmax_exp(1)
                act.wait_ge(y_ready, t + 1)
                nc.scalar.activation(onehot, y_tok[:, t, :], ACT.Square, accum_out=out_ss[:, t:t + 1]).then_inc(out_squared, 1)
                act.wait_ge(out_squared, t + 1)
                nc.scalar.activation(out_sd[:, t:t + 1], out_ss[:, t:t + 1], ACT.Sqrt, bias=eps_c, scale=1.0 / D).then_inc(out_rooted, 1)

        @block.vector
        def _(dve):
            own = Chain(dve, dve_step)
            v = nc.vector
            v.memset(eps_c, EPS).then_inc(eps_ready, 1)
            v.memset(ln_eps_c, LN_EPS).then_inc(eps_ready, 1)
            v.memset(ps_p, 0.0).then_inc(proj_freed, PSLOTS)
            v.memset(ps_o, 0.0).then_inc(out_ready, 1)

            for g in range(4):
                for t in range(TT):
                    m = M_X + TT * g + t
                    dve.wait_ge(misc_done, m + 1)
                    v.tensor_copy(x_t[:, 4 * g:4 * g + 4, t * P:(t + 1) * P],
                                  ps_m[:, m % 2, :].rearrange("p (a b) -> p a b", a=4)).then_inc(misc_freed, 1)
            dve.wait_ge(misc_done, M_VEC + 1)
            bank = ps_m[:, M_VEC % 2, :]
            own.step(v.tensor_copy(params[:, 0:90], bank[:, 0:90]))
            own.step(v.tensor_copy(params[:, 128:192], bank[:, 128:192]))
            own.step(v.tensor_copy(params[:, C_TAP:C_TAP + 124], bank[:, 256:380]))
            v.tensor_copy(params[:, C_TAP + 124:C_TAP + 248], bank[:, 384:508]).then_inc(misc_freed, 1)
            dve.wait_ge(misc_freed, M_VEC + 1)

            def invert_root(r):
                dve.wait_ge(rooted, r)
                v.reciprocal(rstd[:, 0:T], sdev[:, 0:T]).then_inc(rstd_ready, 1)
                dve.wait_ge(rstd_ready, r)

            def scale_residual(r, c0):
                invert_root(r)
                with dve.Fori(0, KD) as k:
                    v.scalar_tensor_tensor(out=h_f[:, bass.ds(k * T, T)], in0=x_f[:, bass.ds(k * T, T)],
                                           scalar=params[:, bass.ds(k + c0, 1)], in1=rstd[:, 0:T],
                                           op0=ALU.mult, op1=ALU.mult).then_inc(h_scaled, 1)

            scale_residual(1, C_NORM)

            dve.wait_ge(ssm_in, 16 * 3)
            buf = slots_f[0:PAIRS, 56 * T:63 * T].rearrange("p (a b) -> p a b", b=P)
            lam_re, lam_im, fac_re, fac_im = (buf[:, n, :] for n in range(4))
            a_re, a_im, t0, t1, t2, t3 = (buf[:, n, :] for n in (6, 7, 4, 5, 8, 9))
            t4, t5 = buf[:, 10, :], buf[:, 11, :]
            log_dt, dt = buf[:, 12, 0:2], buf[:, 12, 2:4]
            u0, u1, u2, u3 = (buf[:, 12, 8 + 8 * n:10 + 8 * n] for n in range(4))

            def scal(out, in0, s1, s2, op0, op1):
                own.do(v.tensor_scalar(out, in0, s1, s2, op0, op1))

            def stt(out, in0, s, in1, op0, op1):
                own.do(v.scalar_tensor_tensor(out=out, in0=in0, scalar=s, in1=in1, op0=op0, op1=op1))

            def tt(out, a, b, op):
                own.do(v.tensor_tensor(out, a, b, op))

            def exp(x, n, r, p, s):
                scal(r, x, -174.0, 176.0, ALU.max, ALU.min)
                scal(n, r, 1.4426950408889634, MAGIC, ALU.mult, ALU.add)
                scal(n, n, -MAGIC, None, ALU.add, ALU.bypass)
                stt(r, n, -0.693359375, r, ALU.mult, ALU.add)
                stt(r, n, 2.12194440e-4, r, ALU.mult, ALU.add)
                scal(p, r, 1.0 / 5040, None, ALU.mult, ALU.bypass)
                for c in (1.0 / 720, 1.0 / 120, 1.0 / 24, 1.0 / 6, 0.5, 1.0):
                    stt(p, p, c, r, ALU.add, ALU.mult)
                scal(p, p, 1.0, None, ALU.add, ALU.bypass)
                scal(r, n, 0.5, MAGIC, ALU.mult, ALU.add)
                scal(r, r, -MAGIC, None, ALU.add, ALU.bypass)
                tt(n, n, r, ALU.subtract)
                for half in (r, n):
                    scal(s.bitcast(I32), half, 127.0, 8388608.0, ALU.add, ALU.mult)
                    tt(p, p, s, ALU.mult)

            exp(log_dt, u0, u1, dt, u2)
            for s in range(2):
                own.do(v.tensor_scalar(t0[:, s * STATE:(s + 1) * STATE], a_re[:, s * STATE:(s + 1) * STATE],
                                       dt[:, s:s + 1], None, ALU.mult))
            exp(t0, t1, t2, t3, t4)
            for s in range(2):
                own.do(v.tensor_scalar(t0[:, s * STATE:(s + 1) * STATE], a_im[:, s * STATE:(s + 1) * STATE],
                                       dt[:, s:s + 1], None, ALU.mult))
            scal(t1, t0, 0.6366197723675814, MAGIC, ALU.mult, ALU.add)
            scal(t1, t1, -MAGIC, None, ALU.add, ALU.bypass)
            for c in (1.5703125, 4.837512969970703e-4, 7.549789948768648e-8):
                stt(t0, t1, -c, t0, ALU.mult, ALU.add)
            scal(t2, t1, 0.25, -0.375, ALU.mult, ALU.add)
            scal(t2, t2, MAGIC, None, ALU.add, ALU.bypass)
            scal(t2, t2, -MAGIC, None, ALU.add, ALU.bypass)
            stt(t1, t2, -4.0, t1, ALU.mult, ALU.add)
            tt(t2, t0, t0, ALU.mult)
            scal(t4, t2, 1.0 / 362880, None, ALU.mult, ALU.bypass)
            for c in (-1.0 / 5040, 1.0 / 120, -1.0 / 6):
                stt(t4, t4, c, t2, ALU.add, ALU.mult)
            stt(t4, t4, 1.0, t0, ALU.add, ALU.mult)
            scal(t5, t2, -1.0 / 3628800, None, ALU.mult, ALU.bypass)
            for c in (1.0 / 40320, -1.0 / 720, 1.0 / 24, -0.5):
                stt(t5, t5, c, t2, ALU.add, ALU.mult)
            scal(t5, t5, 1.0, None, ALU.add, ALU.bypass)
            scal(t0, t1, 1.0, None, ALU.is_equal, ALU.bypass)
            stt(t0, t1, 3.0, t0, ALU.is_equal, ALU.add)
            scal(t2, t0, -1.0, 1.0, ALU.mult, ALU.add)
            tt(lam_re, t0, t4, ALU.mult)
            tt(fac_re, t2, t5, ALU.mult)
            tt(lam_re, lam_re, fac_re, ALU.add)
            tt(lam_im, t0, t5, ALU.mult)
            tt(fac_im, t2, t4, ALU.mult)
            tt(lam_im, lam_im, fac_im, ALU.add)
            scal(t2, t1, 2.0, None, ALU.is_ge, ALU.bypass)
            scal(t2, t2, -2.0, 1.0, ALU.mult, ALU.add)
            tt(lam_im, lam_im, t2, ALU.mult)
            scal(t2, t1, 1.0, None, ALU.is_equal, ALU.bypass)
            stt(t2, t1, 2.0, t2, ALU.is_equal, ALU.add)
            scal(t2, t2, -2.0, 1.0, ALU.mult, ALU.add)
            tt(lam_re, lam_re, t2, ALU.mult)
            tt(lam_re, lam_re, t3, ALU.mult)
            tt(lam_im, lam_im, t3, ALU.mult)
            tt(t0, a_re, a_re, ALU.mult)
            tt(t1, a_im, a_im, ALU.mult)
            tt(t0, t0, t1, ALU.add)
            own.do(v.reciprocal(t1, t0))
            scal(t2, lam_re, -1.0, None, ALU.add, ALU.bypass)
            tt(t3, t2, a_re, ALU.mult)
            tt(t4, lam_im, a_im, ALU.mult)
            tt(t3, t3, t4, ALU.add)
            tt(fac_re, t3, t1, ALU.mult)
            tt(t3, lam_im, a_re, ALU.mult)
            tt(t4, t2, a_im, ALU.mult)
            tt(t3, t3, t4, ALU.subtract)
            v.tensor_tensor(fac_im, t3, t1, ALU.mult).then_inc(ssm_coef, 1)

            dve.wait_ge(misc_done, M_LAM + 1)
            v.tensor_copy(lam_f[:, :, :], ps_m[:, M_LAM % 2, :].rearrange("p (a b) -> p a b", a=4)[:, :, 0:PAIRS]).then_inc(misc_freed, 1)
            dve.wait_ge(misc_freed, M_LAM + 1)
            pw = att_qk[:, 0:256], att_qk[:, 256:512]
            dve.wait_ge(misc_done, M_X + 8)
            for c in range(2):
                own.step(v.tensor_copy(powers[:, c, 0, :], lam_f[:, c, :]))
            own.wait()
            n = 1
            while n < CHUNK:
                re, im = powers[:, 0, 0:n, :], powers[:, 1, 0:n, :]
                by_re, by_im = (powers[:, c, n - 1, :].unsqueeze(1).broadcast_to([P, n, PAIRS]) for c in range(2))
                s0, s1 = (p[:, 0:n * PAIRS].rearrange("p (a b) -> p a b", a=n) for p in pw)
                for c, (p, q, op) in enumerate(((by_re, by_im, ALU.subtract), (by_im, by_re, ALU.add))):
                    own.step(v.tensor_tensor(s0, re, p, ALU.mult))
                    own.do(v.tensor_tensor(s1, im, q, ALU.mult))
                    own.do(v.tensor_tensor(powers[:, c, n:2 * n, :], s0, s1, op))
                n *= 2
            dve.wait_ge(b_in, 32)
            own.do(v.memset(b_diag, 0.0))
            f_re, f_im = (lam_f[:, 2 + c, :].unsqueeze(2).broadcast_to([P, PAIRS, GCH]) for c in range(2))
            pw3 = att_qk.rearrange("p (a b) -> p a b", b=GCH)
            pw4 = work[:, 1024:1536].rearrange("p (a b) -> p a b", b=GCH)
            for c, (p, q, op) in enumerate(((f_re, f_im, ALU.subtract), (f_im, f_re, ALU.add))):
                own.step(v.tensor_tensor(pw3, b_nat[:, 0, :, :], p, ALU.mult))
                own.do(v.tensor_tensor(pw4, b_nat[:, 1, :, :], q, ALU.mult))
                for s in range(2):
                    half = slice(s * STATE, (s + 1) * STATE)
                    own.step(v.tensor_tensor(b_diag[half, c, :, s * GCH:(s + 1) * GCH], pw3[half], pw4[half], op))
                own.wait()
            v.tensor_copy(small[:, 40:41], small[:, 0:1]).then_inc(bdiag_ready, 1)

            dve.wait_ge(mask_ready, 2)
            with dve.Fori(0, 4) as i:
                for e in range(2):
                    head = i * 2 + e
                    dve.wait_ge(rooted, head + 2)
                    v.reciprocal(rstd, sdev).then_inc(rstd_ready, 1)
                    dve.wait_ge(rstd_ready, head + 2)
                    for c, (s0, gain) in enumerate(((Q0, C_QG), (K0, C_KG))):
                        v.scalar_tensor_tensor(out=att_qk[:, c * T:(c + 1) * T], in0=slot(head + s0),
                                               scalar=params[:, gain:gain + 1], in1=rstd[:, c * T:(c + 1) * T],
                                               op0=ALU.mult, op1=ALU.mult).then_inc(qk_ready, 1)
                    dve.wait_ge(v_turned, head + 1)
                    v.tensor_copy(att_vtok, ps_o.rearrange("p (a b) -> p a b", a=2)).then_inc(v_ready, 1)
                    dve.wait_ge(scores_done, head + 1)
                    own_at = head * 4 + own.n
                    v.tensor_tensor(att_s, ps_s, mask, ALU.add).then_inc(dve_step, 1)
                    dve.wait_ge(dve_step, own_at + 1)
                    v.tensor_reduce(att_max[:, 0:1], att_s[:, 0:P], AX_X, ALU.max).then_inc(dve_step, 1)
                    v.tensor_reduce(att_max[:, 1:2], att_s[:, P:3 * P], AX_X, ALU.max).then_inc(dve_step, 1)
                    dve.wait_ge(dve_step, own_at + 3)
                    v.tensor_scalar(att_nmax, att_max, -HEAD_DIM ** -0.5, None, ALU.mult).then_inc(nmax_ready, 1)
                    dve.wait_ge(exp_ready, head * 2 + 2)
                    v.reciprocal(att_rsum, att_sum).then_inc(dve_step, 1)
                    dve.wait_ge(dve_step, own_at + 4)
                    for j, (lo, hi) in enumerate(((0, P), (P, 3 * P))):
                        v.tensor_scalar(att_p[:, lo:hi], att_p[:, lo:hi], att_rsum[:, j:j + 1], None,
                                        ALU.mult).then_inc(probs_ready, 1)
            own.n += 4 * HEADS

            dve.wait_ge(proj_freed, freed(56))
            own.do(v.tensor_tensor(slot(CG0, KH), slot(CG0, KH), slot(HC0, KH), ALU.mult))
            for tap in (2, 1, 0):
                lag = 2 - tap
                for n in range(KH):
                    w = params[:, C_CONV + tap * KH + n:C_CONV + tap * KH + n + 1]
                    u, y = slot(CG0 + n), slot(HC0 + n)
                    if lag == 0:
                        ins = v.tensor_scalar(y, u, w, None, ALU.mult)
                    else:
                        ins = v.scalar_tensor_tensor(out=y[:, lag:T], in0=u[:, 0:T - lag], scalar=w, in1=y[:, lag:T],
                                                     op0=ALU.mult, op1=ALU.add)
                    own.step(ins)
                own.wait()
            v.tensor_tensor(slot(HC0, KH), slot(HC0, KH), slot(BG0, KH), ALU.mult).then_inc(yconv_raw, 1)

            def norm_branch(r, s0, c0):
                invert_root(r)
                for n in range(KH):
                    own.step(v.scalar_tensor_tensor(out=slot(s0 + n), in0=slot(s0 + n), scalar=params[:, c0 + n:c0 + n + 1],
                                                    in1=rstd[:, 0:T], op0=ALU.mult, op1=ALU.mult))
                own.wait()

            norm_branch(10, Q0, C_AOUT)
            dve.wait_ge(za_silu, 1)
            v.tensor_tensor(slot(Q0, KH), slot(Q0, KH), slot(ZA0, KH), ALU.mult).then_inc(y_final, 1)
            norm_branch(11, HC0, C_COUT)
            dve.wait_ge(proj_freed, freed(64))
            v.tensor_tensor(slot(HC0, KH), slot(HC0, KH), slot(ZC0, KH), ALU.mult).then_inc(y_final, 1)

            def add_residual(tile0):
                for n in range(KD):
                    dve.wait_ge(proj_done, tile0 + n + 1)
                    v.tensor_tensor(x_t[:, n, :], x_t[:, n, :], ps_p[:, n % PSLOTS, :], ALU.add).then_inc(proj_freed, 1)

            add_residual(TILE_OUT)
            scale_residual(12, C_MIX)

            s1, s2 = norm_ws[:, 1024:1536], norm_ws[:, 1536:2048]

            def scan(half):
                dve.wait_ge(misc_freed, M_BU[half] + 16)
                pairs = slice(HPAIRS * half, HPAIRS * half + HPAIRS)

                def power(c, j, width):
                    p = powers[:, c, j, pairs].unsqueeze(1).unsqueeze(3)
                    return p.broadcast_to([P, 2, HPAIRS, width])

                def cross(at, by, width):
                    w1, w2 = (s[:, 0:2 * HPAIRS * width].rearrange("p (c r k) -> p c r k", c=2, r=HPAIRS) for s in (s1, s2))
                    return w1, w2

                lam1 = [power(c, 0, CHUNKS) for c in range(2)]
                w1, w2 = cross(None, None, CHUNKS)
                flat = lambda w: w.rearrange("p c r k -> p (c r k)")
                with own.loop(1, CHUNK, 5) as j:
                    before = xs_j[:, :, bass.ds(j - 1, 1)].rearrange("p (c r k) o -> p c r (k o)", c=2, r=HPAIRS)
                    here = xs_j[:, :, bass.ds(j, 1)].rearrange("p a o -> p (a o)")
                    n = HPAIRS * CHUNKS
                    own.step(v.tensor_tensor(w1, before, lam1[0], ALU.mult))
                    own.do(v.tensor_tensor(w2, before, lam1[1], ALU.mult))
                    own.do(v.tensor_tensor(here, here, flat(w1), ALU.add))
                    own.step(v.tensor_tensor(here[:, 0:n], here[:, 0:n], flat(w2)[:, n:2 * n], ALU.subtract))
                    own.do(v.tensor_tensor(here[:, n:2 * n], here[:, n:2 * n], flat(w2)[:, 0:n], ALU.add))
                lam16 = [power(c, CHUNK - 1, 1) for c in range(2)]
                w1, w2 = cross(None, None, 1)
                with own.loop(1, CHUNKS, 5) as k:
                    before = xs_cj[:, :, bass.ds(k - 1, 1), CHUNK - 1:CHUNK].rearrange("p (c r) k j -> p c r (k j)", c=2)
                    here = xs_cj[:, :, bass.ds(k, 1), CHUNK - 1:CHUNK].rearrange("p a k j -> p (a k j)")
                    n = HPAIRS
                    own.step(v.tensor_tensor(w1, before, lam16[0], ALU.mult))
                    own.do(v.tensor_tensor(w2, before, lam16[1], ALU.mult))
                    own.do(v.tensor_tensor(here, here, flat(w1), ALU.add))
                    own.step(v.tensor_tensor(here[:, 0:n], here[:, 0:n], flat(w2)[:, n:2 * n], ALU.subtract))
                    own.do(v.tensor_tensor(here[:, n:2 * n], here[:, n:2 * n], flat(w2)[:, 0:n], ALU.add))
                w1, w2 = cross(None, None, CHUNKS - 1)
                carry = xs_cj[:, :, 0:CHUNKS - 1, CHUNK - 1].rearrange("p (c r) k -> p c r k", c=2)
                with own.loop(0, CHUNK - 1, 5) as j:
                    lam = [powers[:, c, bass.ds(j, 1), pairs].rearrange("p o r -> p (o r)").unsqueeze(1).unsqueeze(3)
                           .broadcast_to([P, 2, HPAIRS, CHUNKS - 1]) for c in range(2)]
                    here = xs_cj[:, :, 1:CHUNKS, bass.ds(j, 1)].rearrange("p (c r) k o -> p c r (k o)", c=2)
                    own.step(v.tensor_tensor(w1, carry, lam[0], ALU.mult))
                    own.do(v.tensor_tensor(w2, carry, lam[1], ALU.mult))
                    own.do(v.tensor_tensor(here, here, w1, ALU.add))
                    own.step(v.tensor_tensor(here[:, 0], here[:, 0], w2[:, 1], ALU.subtract))
                    own.do(v.tensor_tensor(here[:, 1], here[:, 1], w2[:, 0], ALU.add))
                v.tensor_copy(small[:, 41 + half:42 + half], small[:, 0:1]).then_inc(scanned, 1)

            def skip_sum(half):
                for n in range(4):
                    a, m = 4 * half + n, M_CY[half] + n
                    dve.wait_ge(misc_done, m + 1)
                    own.do(v.scalar_tensor_tensor(out=slot(SSM0 + a), in0=slot(SSM0 + a), scalar=params[:, C_SKIP + a:C_SKIP + a + 1],
                                                  in1=ps_m[:, m % 2, 0:T], op0=ALU.mult, op1=ALU.add))
                    v.tensor_copy(small[:, 44:45], small[:, 0:1]).then_inc(ssm_sum, 1)
                    v.tensor_copy(small[:, 45:46], small[:, 0:1]).then_inc(misc_freed, 1)

            scan(0)
            skip_sum(0)
            scan(1)
            skip_sum(1)

            dve.wait_ge(misc_done, M_CY[1] + 4)
            dve.wait_ge(proj_freed, freed(TILE_IN2 + 24))
            own.step(v.memset(glu_pad[:, :, 0:TAPS2 - 1], 0.0))
            own.do(v.tensor_tensor(glu_pad[:, :, TAPS2 - 1:], slots[:, GLU0:GLU0 + KH, :], slots[:, SIG0:SIG0 + KH, :], ALU.mult))
            for n in range(KH):
                last = TAPS2 - 1
                w = params[:, C_TAP + last * KH + n:C_TAP + last * KH + n + 1]
                own.step(v.tensor_scalar(slot(CONV0 + n), glu_pad[:, n, last:last + T], w, params[:, C_CB + n:C_CB + n + 1],
                                         ALU.mult, ALU.add))
            with own.loop(0, TAPS2 - 1, KH) as tap:
                own.wait()
                for n in range(KH):
                    own.step(v.scalar_tensor_tensor(out=slot(CONV0 + n), in0=glu_pad[:, n, bass.ds(tap, T)],
                                                    scalar=params[:, bass.ds(tap * KH + (C_TAP + n), 1)], in1=slot(CONV0 + n),
                                                    op0=ALU.mult, op1=ALU.add))
            own.wait()
            v.tensor_copy(small[:, 43:44], small[:, 0:1]).then_inc(conv_done, 1)

            def gate_values(g):
                dve.wait_ge(proj_freed, freed(TILE_VG + 8 * g + 8))
                own.do(v.tensor_tensor(slot(VAL0, 4), slot(VAL0, 4), slot(VSIG0, 4), ALU.mult))
                v.tensor_tensor(slot(GB0 + 4 * g, 4), slot(GB0 + 4 * g, 4), slot(VAL0, 4), ALU.mult).then_inc(val_gated, 1)

            gate_values(0)
            gate_values(1)
            dve.wait_ge(rooted, 13)
            conv = slots[:, CONV0:CONV0 + KH, :]
            own.do(v.tensor_tensor(conv, conv, sdev[:, 0:T].unsqueeze(1).broadcast_to([P, KH, T]), ALU.subtract))
            v.tensor_copy(small[:, 46:47], small[:, 0:1]).then_inc(centred, 1)
            v.tensor_copy(small[:, 47:48], small[:, 0:1]).then_inc(rstd_ready, 1)
            invert_root(14)
            for n in range(KH):
                v.scalar_tensor_tensor(out=slot(CONV0 + n), in0=slot(CONV0 + n), scalar=params[:, C_LNG + n:C_LNG + n + 1],
                                       in1=rstd[:, 0:T], op0=ALU.mult, op1=ALU.mult).then_inc(ln_scaled, 1)
            gate_values(2)
            gate_values(3)
            dve.wait_ge(val_gated, 4)
            for n in range(KD):
                dve.wait_ge(proj_done, TILE_CV + n + 1)
                v.tensor_tensor(slot(GA0 + n), slot(GA0 + n), ps_p[:, n % PSLOTS, :], ALU.mult).then_inc(proj_freed, 1)
                dve.wait_ge(proj_freed, freed(TILE_CV + n + 1))
                v.tensor_tensor(slot(GA0 + n), slot(GA0 + n), slot(GB0 + n), ALU.add).then_inc(merged, 1)

            add_residual(TILE_OUT2)
            scale_residual(15, C_FFN)

            s4 = tk_s.rearrange("p (h c k) -> p h c k", h=PEER_H, c=2)

            def best16(src, val, idx):
                n = range(len(src))
                for half in range(2):
                    at = slice(8 * half, 8 * half + 8)
                    for m in n:
                        own.step(v.max(val[m][:, at], src[m]))
                    own.wait()
                    for m in n:
                        own.step(v.max_index(idx[m][:, at], val[m][:, at], src[m]))
                    if half == 0:
                        for m in n:
                            own.step(v.match_replace(src[m], val[m][:, at], src[m], -3.0e38))
                    own.wait()

            def head_picks(t, h):
                dve.wait_ge(misc_freed, M_S + TT * (h // 2 + 1))
                own.wait()
                two = range(2)
                best16([key_s[:, t, 2 * h + c, :] for c in two], [tk_s[:, (2 * h + c) * 16:(2 * h + c + 1) * 16] for c in two],
                       [tk_iu[:, (2 * h + c) * 16:(2 * h + c + 1) * 16] for c in two])
                own.do(v.tensor_tensor(tk_cand.rearrange("p (a b) -> p a b", a=16),
                                       s4[:, h, 0, :].unsqueeze(2).broadcast_to([P, 16, 16]),
                                       s4[:, h, 1, :].unsqueeze(1).broadcast_to([P, 16, 16]), ALU.add))
                best16([tk_cand], [tk_best[:, h * 16:(h + 1) * 16]], [tk_pos[:, h * 16:(h + 1) * 16]])

            def experts(t):
                cols = slice(t * P, (t + 1) * P)
                by_head = lambda a: a.rearrange("p (h k) -> p h k", h=PEER_H)
                own.wait()
                dve.wait_ge(zero_ready, 1)
                g = by_head(gates[:, cols])
                v.tensor_tensor(g, by_head(tk_best), by_head(tk_best)[:, :, 0:1].broadcast_to([P, PEER_H, PEER_K]),
                                ALU.subtract).then_inc(best_ready, 1)
                own.step(v.tensor_scalar(tk_hi, tk_pos, 4, None, ALU.logical_shift_right))
                own.step(v.tensor_scalar(tk_lo, tk_pos, 15, None, ALU.bitwise_and))
                own.do(v.tensor_copy(tk_if, tk_iu))
                own.step(v.tensor_copy(tk_hif, tk_hi))
                own.do(v.tensor_copy(tk_lof, tk_lo))
                i4 = tk_if.rearrange("p (h c k) -> p h c k", h=PEER_H, c=2)
                hot = onehot.rearrange("p (n a) -> p n a", a=16)
                hot4 = onehot.rearrange("p (h k a) -> p h k a", h=PEER_H, k=PEER_K)
                for c, (pos, e) in enumerate(((tk_hif, tk_e1), (tk_lof, tk_e2))):
                    own.do(v.tensor_tensor(hot, pos.unsqueeze(2).broadcast_to([P, PICKS, 16]),
                                           iota16.unsqueeze(1).broadcast_to([P, PICKS, 16]), ALU.is_equal))
                    own.do(v.tensor_tensor(hot4, hot4, i4[:, :, c, :].unsqueeze(2).broadcast_to([P, PEER_H, PEER_K, 16]), ALU.mult))
                    own.do(v.tensor_reduce(e, hot, AX_X, ALU.add))
                v.scalar_tensor_tensor(out=picks[:, cols], in0=tk_e1, scalar=float(KEYS), in1=tk_e2, op0=ALU.mult,
                                       op1=ALU.add).then_inc(picks_ready, 1)
                dve.wait_ge(best_exp, t + 1)
                own.do(v.tensor_reduce(head_sum, g, AX_X, ALU.add))
                own.do(v.reciprocal(head_rs, head_sum))
                own.do(v.tensor_tensor(g, g, head_rs.unsqueeze(2).broadcast_to([P, PEER_H, PEER_K]), ALU.mult))

            for h in range(PEER_H):
                head_picks(0, h)
            experts(0)

            def dot_rows(t):
                with dve.Fori(0, 8) as i:
                    for n in range(ROWS):
                        dve.wait_ge(gathered[n], (i + (16 * t + 1)) * 16)
                        v.scalar_tensor_tensor(out=rows[n], in0=rows[n], scalar=1.0, in1=h_tok[:, t, :], op0=ALU.mult,
                                               op1=ALU.mult, accum_out=dots[:, bass.ds(i * 16 + (t * P + n), 1)]).then_inc(row_free[n], 1)
                for n in range(ROWS):
                    dve.wait_ge(row_free[n], 16 * t + 9)
                v.tensor_copy(small[:, 48:49], small[:, 0:1]).then_inc(dots_ready, PICKS)
                dve.wait_ge(gelu_ready, t + 1)
                cols = slice(t * P, (t + 1) * P)
                v.tensor_tensor(pick_w[:, cols], pick_w[:, cols], gates[:, cols], ALU.mult).then_inc(w_ready, 1)
                dve.wait_ge(w_ready, t + 1)

            def add_rows(t, i):
                for n in range(PE_ROWS, ROWS):
                    dve.wait_ge(gathered[n], (i + (16 * t + 9)) * 16)
                    at = i * 16 + (t * P + n)
                    w = pick_w[:, at:at + 1] if isinstance(at, int) else pick_w[:, bass.ds(at, 1)]
                    v.scalar_tensor_tensor(out=y_tok[:, t, :], in0=rows[n], scalar=w, in1=y_tok[:, t, :],
                                           op0=ALU.mult, op1=ALU.add).then_inc(row_free[n], 1)
                    dve.wait_ge(row_free[n], i + (16 * t + 10))

            def finish(t):
                dve.wait_ge(v_summed, t + 1)
                own.do(v.tensor_tensor(y_tok[:, t, :].rearrange("p (c n) -> p c n", c=4), y_tok[:, t, :].rearrange("p (c n) -> p c n", c=4),
                                       ps_v, ALU.add))
                v.tensor_copy(small[:, 49:50], small[:, 0:1]).then_inc(v_read, 1)
                v.tensor_copy(small[:, 50:51], small[:, 0:1]).then_inc(y_ready, 1)
                dve.wait_ge(out_rooted, t + 1)
                own.do(v.reciprocal(out_rs[:, t:t + 1], out_sd[:, t:t + 1]))
                dve.wait_ge(gain_in, 16)
                v.scalar_tensor_tensor(out=y_tok[:, t, :], in0=y_tok[:, t, :], scalar=out_rs[:, t:t + 1], in1=gain_b,
                                       op0=ALU.mult, op1=ALU.mult).then_inc(normed, 1)

            dve.wait_ge(misc_freed, M_S + 8)
            dot_rows(0)
            for i in range(8):
                if i == 7:
                    experts(1)
                for h in ((0, 1) if i == 0 else (i + 1,) if i < 7 else ()):
                    head_picks(1, h)
                add_rows(0, i)
            finish(0)
            dot_rows(1)
            with dve.Fori(0, 8) as i:
                add_rows(1, i)
            finish(1)


_INPUTS = [
    "x", "norm_gain", "w_in", "conv_w", "q_norm_gain", "k_norm_gain", "conv_out_gain", "attn_out_gain", "w_out",
    "norm_mix_2", "w_in_2", "b_gate_2", "conv_w_dw_2", "conv_b_dw_2", "conv_ln_g_2", "conv_ln_b_2", "conv_w_out_2",
    "ssm_a_re_2", "ssm_a_im_2", "ssm_log_dt_2", "ssm_b_re_2", "ssm_b_im_2", "ssm_c_re_2", "ssm_c_im_2", "ssm_d_2",
    "ssm_w_val_2", "ssm_w_gate_2", "w_out_2", "norm_ffn_2", "peer_w_q_2", "peer_sub_keys_2", "peer_u_2", "peer_v_2",
    "norm_final_2",
]


def kernel(**inputs):
    import numpy as np
    import concourse.bacc as bacc
    from concourse.bass_utils import run_bass_kernel_spmd

    nc = bacc.Bacc("TRN2", target_bir_lowering=False, num_devices=1)
    arrays, aps = {}, {}
    for name in _INPUTS:
        a = np.ascontiguousarray(inputs[name])
        arrays[f"in_{name}"] = a
        aps[name] = nc.dram_tensor(f"in_{name}", a.shape, mybir.dt.from_np(a.dtype), kind="ExternalInput").ap()
    aps["out"] = nc.dram_tensor("out_y", (1, T, D), F32, kind="ExternalOutput").ap()
    build(nc, aps)
    result = run_bass_kernel_spmd(nc, [arrays], core_ids=[0])
    return result.results[0]["out_y"]
```

```python
from contextlib import ExitStack, contextmanager

import concourse.bass as bass
import concourse.mybir as mybir

F32 = mybir.dt.float32
F32R = mybir.dt.float32r
I32 = mybir.dt.int32
U32 = mybir.dt.uint32
ALU = mybir.AluOpType
ACT = mybir.ActivationFunctionType
AX_X = mybir.AxisListType.X

P = 128
T = 256
TT = T // P
D = 2048
KD = D // P
HALF = D // 2
KH = HALF // P
HEADS = 8
HEAD_DIM = P
EPS = 1e-6
LN_EPS = 1e-5

GROUPS, STATE, GCH = 64, 64, 16
PAIRS = GROUPS // 2
HPAIRS = PAIRS // 2
CHUNK = 16
CHUNKS = T // CHUNK
TAPS2 = 31

PEER_H, PEER_K, KEYS = 8, 16, 128
SCORE_AFTER = [4, 5, 6, 8, 10, 12, 14, 15]
PICKS = PEER_H * PEER_K

SLAB = 2048
SBUF2 = 2
PSLOTS = 2
SQ = 4

TILE_IN = 0
TILE_OUT = TILE_IN + 64
TILE_IN2 = TILE_OUT + 16
TILE_VG = TILE_IN2 + 56
TILE_CV = TILE_VG + 32
TILE_OUT2 = TILE_CV + 16
TILE_WQ = TILE_OUT2 + 16
SLAB_IN = 0
SLAB_OUT = SLAB_IN + 64
SLAB_IN2 = SLAB_OUT + 16
SLAB_VG = SLAB_IN2 + 56
SLAB_CV = SLAB_VG + 16
SLAB_OUT2 = SLAB_CV + 8
SLAB_WQ = SLAB_OUT2 + 16
SLABS = SLAB_WQ + 16
G_IN, G_MIX, G_IN2, G_Z, G_CV, G_MERGE, G_Q = 0, 8, 10, 18, 20, 24, 32

Q0, K0, V0, ZA0, HC0, BG0, CG0, ZC0 = range(0, 64, 8)
GLU0, SIG0, SSM0, GA0, GB0, CONV0 = 0, 8, 16, 24, 40, 56
VAL0 = 8
H0 = 24
SUBK0, SUBT0 = 40, 16
TOPK0 = 48

C_NORM, C_MIX, C_FFN, C_COUT, C_AOUT, C_CONV, C_QG, C_KG = 0, 16, 32, 48, 56, 64, 88, 89
C_GATE, C_CB, C_LNG, C_LNB, C_SKIP = 128, 160, 168, 176, 184
C_TAP = 256

LN_MEAN, LN_VAR = 24, 29

MAGIC = 12582912.0


class Chain:

    def __init__(self, eng, sem):
        self.eng, self.sem, self.n, self.base = eng, sem, 0, 0

    def step(self, ins):
        ins.then_inc(self.sem, 1)
        self.n += 1

    def wait(self, but=0):
        self.eng.wait_ge(self.sem, self.base + (self.n - but))

    def do(self, ins):
        self.step(ins)
        self.wait()

    @contextmanager
    def loop(self, start, end, steps):
        before = self.n
        with self.eng.Fori(start, end) as i:
            self.base, self.n = i * steps + (before - start * steps), 0
            yield i
            assert self.n == steps, (self.n, steps)
        self.base, self.n = 0, before + (end - start) * steps


def build(nc, d):
    ctx = ExitStack()
    with ctx:
        def sb(name, shape, dt=F32):
            return ctx.enter_context(nc.sbuf_tensor(name, shape, dt))

        def sem(name):
            return ctx.enter_context(nc.semaphore(name))

        w_raw = sb("weight_raw", [P, SBUF2, SLAB])
        w_hi = sb("weight_hi", [P, SBUF2, SLAB], F32R)
        w_lo = sb("weight_lo", [P, SBUF2, SLAB], F32R)
        slots = sb("slots", [P, 64, T])
        x_t = sb("residual_t", [P, KD, T])
        a_hi = sb("operand_hi", [P, KD, T], F32R)
        a_lo = sb("operand_lo", [P, KD, T], F32R)
        work = sb("work", [P, 8192])
        norm_ws = sb("norm_ws", [P, 2048])
        ident = sb("ident", [P, P])
        ones = sb("ones", [P, P])
        params = sb("params", [P, 512])
        lam_f = sb("lam_f", [P, 4, PAIRS])
        powers = sb("powers", [P, 2, CHUNK, PAIRS])
        small = sb("small", [P, 64])
        pick_stage = sb("pick_stage", [P, 8], U32)
        ps = ctx.enter_context(nc.psum_tensor("ps", [P, 8, 512], F32))

        slots_f = slots[:, :, :].rearrange("p a b -> p (a b)")
        x_f = x_t[:, :, :].rearrange("p a b -> p (a b)")
        h_t = slots[:, H0:H0 + KD, :]

        def slot(s, n=1):
            if isinstance(s, int):
                return slots_f[:, s * T:(s + n) * T]
            return slots_f[:, bass.ds(s * T, n * T)]

        sdev, rstd = norm_ws[:, 0:512], norm_ws[:, 512:1024]
        sq = norm_ws[:, 1024:2048].rearrange("p (a b) -> p a b", a=SQ)
        eps_c, ln_eps_c = small[:, 0:1], small[:, 1:2]
        att_nmax, att_max, att_sum, att_rsum = small[:, 2:4], small[:, 4:6], small[:, 6:8], small[:, 8:10]
        out_ss, out_sd, out_rs = small[:, 10:12], small[:, 12:14], small[:, 14:16]
        head_max, head_sum, head_rs = small[:, 16:24], small[:, 24:32], small[:, 32:40]

        x_tok0 = work[:, 0:4096].rearrange("p (a b) -> p a b", a=TT)
        att_qk, att_v = work[:, 0:512], work[:, 512:768]
        att_vtok = work[:, 768:1024].rearrange("p (a b) -> p a b", a=2)
        att_s, att_p, att_pt = work[:, 1024:1408], work[:, 1408:1792], work[:, 1792:2176]
        b_nat = work[:, 2176:3200].rearrange("p (c r h) -> p c r h", c=2, r=PAIRS)
        mask = work[:, 3200:3584]
        b_diag = work[:, 4096:6144].rearrange("p (c r h) -> p c r h", c=2, r=PAIRS)
        c_diag = work[:, 6144:8192].rearrange("p (c a b) -> p c a b", c=2, a=KH)
        xs = work[:, :].rearrange("p (c r t) -> p c r t", c=2, r=HPAIRS)
        xs_j = work[:, :].rearrange("p (a j) -> p a j", j=CHUNK)
        xs_cj = work[:, :].rearrange("p (a k j) -> p a k j", k=CHUNKS, j=CHUNK)
        glu_pad = work[:, 0:KH * (T + TAPS2 - 1)].rearrange("p (a b) -> p a b", a=KH)
        h_tok = work[:, 0:4096].rearrange("p (a b) -> p a b", a=TT)
        y_tok = work[:, 4096:8192].rearrange("p (a b) -> p a b", a=TT)
        vec = slots_f[:, 60 * T:62 * T].rearrange("p (a b) -> p a b", a=4)
        bt = slots_f[:, 56 * T:64 * T].rearrange("p (c a b) -> p c a b", c=2, a=KH)
        ct = slots_f[:, 48 * T:56 * T].rearrange("p (c a b) -> p c a b", c=2, a=KH)
        subk = slots_f[:, SUBK0 * T:(SUBK0 + 8) * T].rearrange("p (a b) -> p a b", a=16)
        subt = slots_f[:, SUBT0 * T:(SUBT0 + 8) * T].rearrange("p (a b) -> p a b", a=16)
        key_s = x_f.rearrange("p (t a b) -> p t a b", t=TT, a=16)
        diag = x_f[:, 0:2048].rearrange("p (a b) -> p a b", a=16)
        gain_b = x_f[:, 2048:4096]
        tk = slots_f[:, TOPK0 * T:64 * T]
        tk_s, tk_if = tk[:, 0:256], tk[:, 256:512]
        tk_iu = tk[:, 512:768].bitcast(U32)
        tk_cand, tk_best = tk[:, 768:1024], tk[:, 1024:1152]
        tk_pos, tk_hi, tk_lo = (tk[:, 1152 + 128 * n:1280 + 128 * n].bitcast(U32) for n in range(3))
        tk_hif, tk_lof, tk_e1, tk_e2 = (tk[:, 1536 + 128 * n:1664 + 128 * n] for n in range(4))
        picks = tk[:, 2048:2304].bitcast(U32)
        gates, dots, pick_w = tk[:, 2304:2560], tk[:, 2560:2816], tk[:, 2816:3072]
        iota16 = tk[:, 3072:3088]
        zero_row = tk[:, 3088:3600]
        onehot = norm_ws[:, :]
        rows = [w_raw[:, n, :] for n in range(SBUF2)] + [slots_f[:, n * D:(n + 1) * D] for n in range(6)]
        ROWS = len(rows)
        ROUNDS = PICKS // ROWS
        PE_ROWS = 6

        ps_p = ps[:, 0:PSLOTS, 0:T]
        ps_m = ps[:, 2:4, :]
        ps_n, ps_s, ps_pt, ps_o = ps[:, 4, :], ps[:, 5, 0:384], ps[:, 6, 0:384], ps[:, 7, 0:T]
        ps_v = ps[:, 0:4, :]

        x_in = [sem(f"x_in{t}") for t in range(TT)]
        raw_landed = [sem(f"raw_landed{b}") for b in range(SBUF2)]
        hi_ready, lo_ready = sem("hi_ready"), sem("lo_ready")
        a_hi_ready, a_lo_ready = sem("a_hi_ready"), sem("a_lo_ready")
        vec_in, ssm_in, b_in, c_in, subk_in, gain_in = (sem(n) for n in ("vec_in", "ssm_in", "b_in", "c_in", "subk_in", "gain_in"))
        consts_ready, cdiag_cleared, mask_ready = sem("consts_ready"), sem("cdiag_cleared"), sem("mask_ready")
        consts_set, mask_set = sem("consts_set"), sem("mask_set")
        eps_ready = sem("eps_ready")
        proj_done, proj_freed = sem("proj_done"), sem("proj_freed")
        misc_done, misc_freed = sem("misc_done"), sem("misc_freed")
        squared, sq_summed = sem("squared"), sem("sq_summed")
        rooted, rstd_ready, h_scaled = sem("rooted"), sem("rstd_ready"), sem("h_scaled")
        dve_step = sem("dve_step")
        ssm_coef, bdiag_ready, powers_ready = sem("ssm_coef"), sem("bdiag_ready"), sem("powers_ready")
        head_squared, head_summed, qk_ready, v_copied, v_turned, v_ready = (
            sem(n) for n in ("head_squared", "head_summed", "qk_ready", "v_copied", "v_turned", "v_ready"))
        scores_done, nmax_ready, exp_ready, probs_ready, probs_turned, pt_ready, out_done, out_ready = (
            sem(n) for n in ("scores_done", "nmax_ready", "exp_ready", "probs_ready", "probs_turned", "pt_ready",
                             "out_done", "out_ready"))
        za_silu, yconv_raw, y_final = sem("za_silu"), sem("yconv_raw"), sem("y_final")
        scanned, ssm_sum, z_ready, glu_ready, conv_done, centred, ln_scaled, conv_act = (
            sem(n) for n in ("scanned", "ssm_sum", "z_ready", "glu_ready", "conv_done", "centred", "ln_scaled", "conv_act"))
        val_gated, merged = sem("val_gated"), sem("merged")
        picks_ready, best_ready, best_exp, dots_ready, gelu_ready, w_ready, diag_ready = (
            sem(n) for n in ("picks_ready", "best_ready", "best_exp", "dots_ready", "gelu_ready", "w_ready", "diag_ready"))
        staged, zero_ready = [sem(f"staged{half}") for half in range(2)], sem("zero_ready")
        gathered = [sem(f"gathered{n}") for n in range(ROWS)]
        row_free = [sem(f"row_free{n}") for n in range(ROWS)]
        v_summed, v_read, y_ready, out_squared, out_rooted, normed, stored = (
            sem(n) for n in ("v_summed", "v_read", "y_ready", "out_squared", "out_rooted", "normed", "stored"))

        def freed(n):
            return n + PSLOTS

        M_X = 0
        M_VEC = M_X + 8
        M_LAM = M_VEC + 1
        M_BC = M_LAM + 1
        M_BU = [M_BC + 8, M_BC + 8 + 20]
        M_CY = [M_BU[0] + 16, M_BU[1] + 16]
        M_SUB = M_CY[1] + 4
        M_TOK = M_SUB + 4
        M_S = M_TOK + 16

        block = ctx.enter_context(nc.Block())

        @block.sync
        def _(sp):
            for t in range(TT):
                sp.dma_start(x_tok0[:, t, :], d["x"][0, t * P:(t + 1) * P, :]).then_inc(x_in[t], 16)
            w_in = d["w_in"][0].rearrange("(k p) n -> p k n", p=P)
            w_out = d["w_out"][0].rearrange("(k p) n -> p k n", p=P)
            w_in2 = d["w_in_2"][0].rearrange("(k p) n -> p k n", p=P)
            w_val = d["ssm_w_val_2"][0].rearrange("(k p) n -> p k n", p=P)
            w_gate = d["ssm_w_gate_2"][0].rearrange("(k p) n -> p k n", p=P)
            w_cv = d["conv_w_out_2"][0].rearrange("(k p) n -> p k n", p=P)
            w_out2 = d["w_out_2"][0].rearrange("(k p) n -> p k n", p=P)
            w_q = d["peer_w_q_2"][0].rearrange("(k p) n -> p k n", p=P)

            def load(b, w, col, n, used):
                if used is not None:
                    sp.wait_ge(lo_ready, used)
                src = w[:, :, col:col + n] if isinstance(col, int) else w[:, :, bass.ds(col, n)]
                sp.dma_start(w_raw[:, b, :].rearrange("p (k n) -> p k n", n=n), src).then_inc(raw_landed[b], 16)

            def load_pairs(w, slab0, first, last, col0, n=P):
                with sp.Fori((slab0 + first) // 2, (slab0 + last) // 2) as j:
                    for b in range(2):
                        load(b, w, j * (2 * n) + (col0 + n * (b - slab0)), n, j * 4 + (2 * b - 2))

            for b in range(2):
                load(b, w_in, 4 * HALF + P * b, P, None)
            load_pairs(w_in, SLAB_IN, 2, 32, 4 * HALF)
            load_pairs(w_in, SLAB_IN, 32, 64, -4 * HALF)
            load_pairs(w_out, SLAB_OUT, 0, 16, 0)
            load_pairs(w_in2, SLAB_IN2, 0, 8, 2 * HALF)
            load_pairs(w_in2, SLAB_IN2, 8, 24, -KH * P)
            load_pairs(w_in2, SLAB_IN2, 24, 56, 0)
            with sp.Fori(0, 4) as g:
                for m, w in enumerate((w_val, w_gate)):
                    for b in range(2):
                        load(b, w, g * 512 + 256 * b, 256, g * 8 + 2 * (SLAB_VG + 2 * m + b - 1))
            load_pairs(w_cv, SLAB_CV, 0, 8, 0, 256)
            load_pairs(w_out2, SLAB_OUT2, 0, 4, 0)
            sp.wait_ge(merged, KD)
            sp.dma_start(subk, d["peer_sub_keys_2"][0].rearrange("h c n e -> n (h c) e")).then_inc(subk_in, 16)
            load_pairs(w_out2, SLAB_OUT2, 4, 16, 0)
            load_pairs(w_q, SLAB_WQ, 0, 16, 0)
            sp.wait_ge(picks_ready, TT)
            sp.dma_start(gain_b, d["norm_final_2"].partition_broadcast(P)).then_inc(gain_in, 16)
            for t in range(TT):
                sp.wait_ge(normed, t + 1)
                sp.dma_start(d["out"][0, t * P:(t + 1) * P, :], y_tok[:, t, :]).then_inc(stored, 16)
            sp.wait_ge(stored, 16 * TT)

        @block.gpsimd
        def _(pool):
            nc.gpsimd.memset(ident[:, :], 0.0).then_inc(consts_set, 1)
            nc.gpsimd.memset(ones[:, :], 1.0).then_inc(consts_ready, 1)
            pool.wait_ge(consts_set, 1)
            nc.gpsimd.affine_select(out=ident[:, :], in_=ident[:, :], compare_op=ALU.not_equal, fill=1.0, base=0,
                                    pattern=[[-1, P]], channel_multiplier=1).then_inc(consts_ready, 1)
            nc.gpsimd.memset(c_diag, 0.0).then_inc(cdiag_cleared, 1)

            def low_parts(first, last):
                with pool.Fori(first // 2, last // 2) as j:
                    for b in range(2):
                        for half in range(2):
                            at = slice(half * SLAB // 2, (half + 1) * SLAB // 2)
                            pool.wait_ge(hi_ready, j * 4 + (2 * b + half + 1))
                            nc.gpsimd.tensor_tensor(w_lo[:, b, at], w_raw[:, b, at], w_hi[:, b, at].bitcast(F32),
                                                    ALU.subtract).then_inc(lo_ready, 1)

            low_parts(0, 4)
            pool.wait_ge(misc_done, M_X + 8)
            nc.gpsimd.memset(mask, 0.0).then_inc(mask_set, 1)
            pool.wait_ge(mask_set, 1)
            for lo in (0, 2 * P):
                nc.gpsimd.affine_select(out=mask[:, lo:lo + P], in_=mask[:, lo:lo + P], compare_op=ALU.is_ge,
                                        fill=-3.0e38, base=0, pattern=[[-1, P]],
                                        channel_multiplier=1).then_inc(mask_ready, 1)

            low_parts(4, SLABS)
            pool.wait_ge(merged, KD)
            nc.gpsimd.iota(iota16, pattern=[[1, 16]], base=0, channel_multiplier=0,
                           allow_small_or_imprecise_dtypes=True).then_inc(zero_ready, 1)
            nc.gpsimd.memset(zero_row, 0.0).then_inc(zero_ready, 1)

            def gather(t, table, rnd, col0):
                for half in range(2):
                    mine = range(half * ROWS // 2, (half + 1) * ROWS // 2)
                    for n in mine:
                        pool.wait_ge(row_free[n], rnd + 1)
                    nc.gpsimd.tensor_copy(pick_stage[:, mine[0]:mine[-1] + 1],
                                          picks[:, bass.ds(col0 + mine[0], len(mine))]).then_inc(staged[half], 1)
                    pool.wait_ge(picks_ready, t + 1)
                    pool.wait_ge(staged[half], rnd + 1)
                    for n in mine:
                        nc.gpsimd.indirect_dma_start(
                            rows[n], None, table, bass.IndirectOffsetOnAxis(ap=pick_stage[:, n:n + 1], axis=0),
                        ).then_inc(gathered[n], 16)

            for n in range(ROWS):
                pool.sem_inc(row_free[n], 1)
            for t in range(TT):
                pool.wait_ge(picks_ready, t + 1)
                for v, table in ((0, d["peer_u_2"][0]), (1, d["peer_v_2"][0])):
                    with pool.Fori(0, ROUNDS) as i:
                        gather(t, table, i + (2 * t + v) * ROUNDS, i * ROWS + t * PICKS)

        @block.tensor
        def _(pe):
            def tile(slab0, tile0, t, kts, k0=0, order=None, ready=None):
                per = SLAB // kts // P
                b, n = (t // per) % SBUF2, t % per
                if n == 0:
                    pe.wait_ge(hi_ready, slab0 * 2 + (2 * (t // per) + 2))
                pe.wait_ge(proj_freed, tile0 + (t + 1))
                hi, lo = (w[:, b, :].rearrange("p (k n) -> p k n", k=kts)[:, :, n * P:(n + 1) * P] for w in (w_hi, w_lo))
                out = ps_p[:, t % PSLOTS, :]
                order = list(range(kts)) if order is None else order
                for k in order:
                    if ready is not None:
                        pe.wait_ge(a_lo_ready, ready(k) + 1)
                    nc.tensor.matmul(out, hi[:, k, :], a_hi[:, k0 + k, :], start=(k == order[0]), stop=False)
                    nc.tensor.matmul(out, hi[:, k, :], a_lo[:, k0 + k, :], start=False, stop=False)
                if n == 0:
                    pe.wait_ge(lo_ready, slab0 * 2 + (2 * (t // per) + 2))
                for k in order:
                    mm = nc.tensor.matmul(out, lo[:, k, :], a_hi[:, k0 + k, :], start=False, stop=(k == order[-1]))
                mm.then_inc(proj_done, 1)

            def misc_bank(m, first):
                pe.wait_ge(misc_freed, m if first else m - 1)
                return ps_m[:, m % 2, :]

            def sum_square(n, count, q0, r):
                if n == 0 and r > 1:
                    pe.wait_ge(rooted, r - 1)
                pe.wait_ge(squared, q0 + n + 1)
                nc.tensor.matmul(ps_n[:, 0:T], ones[:, :], sq[:, n % SQ, :], start=(n == 0),
                                 stop=(n == count - 1), skip_group_check=True).then_inc(sq_summed, 1)

            pe.wait_ge(consts_ready, 2)
            for g in range(4):
                for t in range(TT):
                    m = M_X + TT * g + t
                    if g == 0:
                        pe.wait_ge(x_in[t], 16)
                    bank = misc_bank(m, m == 0) if m >= 2 else ps_m[:, m % 2, :]
                    for j in range(4):
                        k = 4 * g + j
                        tr = nc.tensor.transpose(bank[:, j * P:(j + 1) * P], x_tok0[:, t, k * P:(k + 1) * P], ident[:, :])
                    tr.then_inc(misc_done, 1)
            pe.wait_ge(vec_in, 16 * 14)
            bank = misc_bank(M_VEC, True)
            for j, n in enumerate((90, 64, 124, 124)):
                tr = nc.tensor.transpose(bank[:, j * P:j * P + n], vec[0:n, j, :], ident[0:n, 0:n])
            tr.then_inc(misc_done, 1)
            for n in range(KD):
                sum_square(n, KD, 0, 1)

            with pe.Fori(0, 3) as i:
                for t in range(8):
                    tile(i * 8, i * 8, t, KD, ready=(lambda k: G_IN + k // 2) if t == 0 else None)
            pe.wait_ge(ssm_coef, 1)
            bank = misc_bank(M_LAM, True)
            for j in range(4):
                tr = nc.tensor.transpose(bank[:, j * P:j * P + PAIRS], slot(56 + j // 2)[0:PAIRS, (j % 2) * P:(j % 2 + 1) * P],
                                         ident[0:PAIRS, 0:PAIRS])
            tr.then_inc(misc_done, 1)

            with pe.Fori(0, 4) as i:
                for e in range(2):
                    head = i * 2 + e
                    pe.wait_ge(rooted, head + 1)
                    pe.wait_ge(head_squared, head * 2 + 2)
                    nc.tensor.matmul(ps_n, ones[:, :], norm_ws[:, 1024:1536], start=True, stop=True).then_inc(head_summed, 1)
                    tile(i * 8 + 24, i * 8 + 24, 4 * e, KD)
                    pe.wait_ge(v_copied, head + 1)
                    pe.wait_ge(out_ready, head + 1)
                    for j in range(2):
                        tr = nc.tensor.transpose(ps_o[:, j * P:(j + 1) * P], att_v[:, j * P:(j + 1) * P], ident[:, :])
                    tr.then_inc(v_turned, 1)
                    pe.wait_ge(qk_ready, head * 2 + 2)
                    nc.tensor.matmul(ps_s[:, 0:P], att_qk[:, 0:P], att_qk[:, T:T + P], start=True, stop=True)
                    nc.tensor.matmul(ps_s[:, P:3 * P], att_qk[:, P:T], att_qk[:, T:2 * T], start=True,
                                     stop=True).then_inc(scores_done, 1)
                    tile(i * 8 + 24, i * 8 + 24, 4 * e + 1, KD)
                    pe.wait_ge(probs_ready, head * 2 + 2)
                    for j in range(3):
                        tr = nc.tensor.transpose(ps_pt[:, j * P:(j + 1) * P], att_p[:, j * P:(j + 1) * P], ident[:, :])
                    tr.then_inc(probs_turned, 1)
                    tile(i * 8 + 24, i * 8 + 24, 4 * e + 2, KD)
                    pe.wait_ge(pt_ready, head + 1)
                    pe.wait_ge(v_ready, head + 1)
                    nc.tensor.matmul(ps_o, att_vtok[:, 0, :], att_pt[:, 0:T], start=True, stop=False)
                    nc.tensor.matmul(ps_o[:, P:T], att_vtok[:, 1, :], att_pt[:, T:T + P], start=False,
                                     stop=True).then_inc(out_done, 1)
                    tile(i * 8 + 24, i * 8 + 24, 4 * e + 3, KD)

            for t in range(8):
                tile(56, 56, t, KD)
                sum_square(t, KH, 16, 10)
            for n in range(KH):
                sum_square(n, KH, 24, 11)

            for t in range(16):
                if t == 0:
                    pe.wait_ge(proj_freed, freed(TILE_OUT))
                tile(SLAB_OUT, TILE_OUT, t, KD, order=[*range(KH, KD), *range(KH)],
                     ready=(lambda k: G_MIX + 1 - k // KH) if t == 0 else None)
                if t >= 2:
                    sum_square(t - 2, KD, 32, 12)
                if t == 7:
                    pe.wait_ge(bdiag_ready, 1)
                    pe.wait_ge(c_in, 16 * 16)
                    for u in range(8):
                        bank = misc_bank(M_BC + u, u == 0)
                        c, half = (u // 2) % 2, u % 2
                        for j in range(4):
                            a = 4 * half + j
                            src = b_diag[:, c, 4 * a:4 * a + 4, :].rearrange("p r h -> p (r h)") if u < 4 else c_diag[:, c, a, :]
                            tr = nc.tensor.transpose(bank[:, j * P:(j + 1) * P], src, ident[:, :])
                        tr.then_inc(misc_done, 1)
            for n in (14, 15):
                sum_square(n, KD, 32, 12)

            pe.wait_ge(proj_freed, freed(TILE_IN2))
            for t in range(8):
                tile(SLAB_IN2, TILE_IN2, t, KD, ready=(lambda k: G_IN2 + k // 2) if t == 0 else None)

            def ssm_inputs(half):
                pe.wait_ge(proj_freed, freed(TILE_IN2 + 8))
                for n in range(HPAIRS):
                    pr = HPAIRS * half + n
                    a, j = pr // 4, pr % 4
                    bank = misc_bank(M_BU[half] + n, n == 0)
                    for c in range(2):
                        mm = nc.tensor.matmul(bank[:, c * T:(c + 1) * T], bt[32 * j:32 * j + 32, c, a, :],
                                              slot(SSM0 + a)[32 * j:32 * j + 32, :], start=True, stop=True)
                    mm.then_inc(misc_done, 1)

            def ssm_outputs(half):
                pe.wait_ge(scanned, half + 1)
                for n in range(4):
                    a = 4 * half + n
                    bank = misc_bank(M_CY[half] + n, n == 0)
                    for j in range(4):
                        for c in range(2):
                            mm = nc.tensor.matmul(bank[32 * j:32 * j + 32, 0:T], ct[:, c, a, 32 * j:32 * j + 32],
                                                  xs[:, c, 4 * n + j, :], start=(c == 0), stop=(c == 1))
                    mm.then_inc(misc_done, 1)

            pe.wait_ge(misc_freed, M_BC + 8)
            ssm_inputs(0)

            def rounds(first, last):
                with pe.Fori(first, last) as i:
                    for t in range(4):
                        tile(i * 4 + SLAB_IN2, i * 4 + TILE_IN2, t, KD)

            rounds(2, 7)
            ssm_outputs(0)
            ssm_inputs(1)
            rounds(7, 12)
            ssm_outputs(1)
            rounds(12, 14)

            for t in range(32):
                tile(SLAB_VG, TILE_VG, t, KH, ready=(lambda k: G_Z + k // 4) if t == 0 else None)
                if t == LN_MEAN:
                    pe.wait_ge(conv_done, 1)
                    pe.wait_ge(rooted, 12)
                    for n in range(KH):
                        mm = nc.tensor.matmul(ps_n[:, 0:T], ones[:, :], slot(CONV0 + n), start=(n == 0), stop=(n == KH - 1))
                    mm.then_inc(centred, 1)
                if t == LN_VAR:
                    for n in range(KH):
                        sum_square(n, KH, 48, 14)

            pe.wait_ge(proj_freed, freed(TILE_CV))
            for t in range(16):
                tile(SLAB_CV, TILE_CV, t, KH, k0=KH, ready=(lambda k: G_CV + k // 2) if t == 0 else None)

            for t in range(16):
                tile(SLAB_OUT2, TILE_OUT2, t, KD, ready=(lambda k: G_MERGE + k // 2) if t == 0 else None)
                if t >= 2:
                    sum_square(t - 2, KD, 56, 15)
                if t == 11:
                    pe.wait_ge(subk_in, 16)
                    for u in range(4):
                        bank = misc_bank(M_SUB + u, u == 0)
                        for j in range(4):
                            tr = nc.tensor.transpose(bank[:, j * P:(j + 1) * P], subk[:, 4 * u + j, :], ident[:, :])
                        tr.then_inc(misc_done, 1)
            for n in (14, 15):
                sum_square(n, KD, 56, 15)

            def head_scores(h):
                pe.wait_ge(proj_freed, freed(TILE_WQ + 2 * h + 2))
                bank = misc_bank(M_S + h, h == 0)
                for t in range(TT):
                    for c in range(2):
                        mm = nc.tensor.matmul(bank[:, (2 * t + c) * P:(2 * t + c + 1) * P],
                                              slot(2 * h + c)[:, t * P:(t + 1) * P], subt[:, 2 * h + c, :], start=True, stop=True)
                mm.then_inc(misc_done, 1)

            pe.wait_ge(proj_freed, freed(TILE_WQ))
            for n in range(16):
                tile(SLAB_WQ, TILE_WQ, n, KD, ready=(lambda k: G_Q + k // 2) if n == 0 else None)
                for u in range(4 * n, 4 * n + 4 if n < 4 else 4 * n):
                    bank = misc_bank(M_TOK + u, u == 0)
                    src, t, g = (x_t, h_t)[u // 8], (u // 4) % 2, u % 4
                    for j in range(4):
                        tr = nc.tensor.transpose(bank[:, j * P:(j + 1) * P], src[:, 4 * g + j, t * P:(t + 1) * P], ident[:, :])
                    tr.then_inc(misc_done, 1)
                if n in SCORE_AFTER:
                    head_scores(SCORE_AFTER.index(n))

            pe.wait_ge(zero_ready, 2)
            pe.wait_ge(misc_freed, M_S + 8)
            for t in range(TT):
                if t > 0:
                    pe.wait_ge(v_read, t)
                for c in range(4):
                    nc.tensor.matmul(ps_v[:, c, :], zero_row[:, 0:P], zero_row, start=True, stop=False, skip_group_check=True)
                with pe.Fori(0, ROUNDS) as i:
                    for n in range(PE_ROWS):
                        pe.wait_ge(diag_ready, i * PE_ROWS + (ROUNDS * PE_ROWS * t + n + 1))
                        pe.wait_ge(gathered[n], (i + ((2 * t + 1) * ROUNDS + 1)) * 16)
                        for c in range(4):
                            mm = nc.tensor.matmul(ps_v[:, c, :], diag[:, n, :], rows[n][:, c * 512:(c + 1) * 512],
                                                  start=False, stop=False, skip_group_check=True)
                        mm.then_inc(row_free[n], 1)
                for c in range(4):
                    mm = nc.tensor.matmul(ps_v[:, c, :], zero_row[:, 0:P], zero_row, start=False, stop=True, skip_group_check=True)
                mm.then_inc(v_summed, 1)

        @block.scalar
        def _(act):
            def act_copy(dst, src):
                return nc.scalar.activation(dst, src, ACT.Copy)

            def row(j, r, src, n):
                act.dma_start(vec[r:r + n, j, :], src).then_inc(vec_in, 16)

            def rows_of(name, pat="(k p) -> k p"):
                return d[name][0].rearrange(pat, p=P)

            row(0, C_NORM, rows_of("norm_gain"), KD)
            row(0, C_MIX, rows_of("norm_mix_2"), KD)
            row(0, C_FFN, rows_of("norm_ffn_2"), KD)
            row(0, C_COUT, rows_of("conv_out_gain"), KH)
            row(0, C_AOUT, rows_of("attn_out_gain"), KH)
            row(0, C_CONV, rows_of("conv_w", "t (k p) -> (t k) p"), 3 * KH)
            row(0, C_QG, d["q_norm_gain"], 1)
            row(0, C_KG, d["k_norm_gain"], 1)
            row(1, 0, rows_of("b_gate_2"), 32)
            row(1, 32, rows_of("conv_b_dw_2"), KH)
            row(1, 40, rows_of("conv_ln_g_2"), KH)
            row(1, 48, rows_of("conv_ln_b_2"), KH)
            row(1, 56, rows_of("ssm_d_2"), KH)
            taps = rows_of("conv_w_dw_2", "t (k p) -> (t k) p")
            act.dma_start(vec[0:124, 2:4, :], taps.rearrange("(j r) p -> r j p", j=2)).then_inc(vec_in, 16)
            act.dma_start(slot(59)[0:PAIRS, 0:P], d["ssm_a_re_2"][0].rearrange("(r s) p -> r (s p)", s=2)).then_inc(ssm_in, 16)
            act.dma_start(slot(59)[0:PAIRS, P:T], d["ssm_a_im_2"][0].rearrange("(r s) p -> r (s p)", s=2)).then_inc(ssm_in, 16)
            act.dma_start(slot(62)[0:PAIRS, 0:2], d["ssm_log_dt_2"][0].rearrange("(r s) -> r s", s=2)).then_inc(ssm_in, 16)
            act.wait_ge(cdiag_cleared, 1)
            for c, name in enumerate(("ssm_c_re_2", "ssm_c_im_2")):
                src = d[name][0].rearrange("(a g) h p -> g h a p", g=8)
                for g in range(8):
                    act.dma_start(c_diag[GCH * g:GCH * g + GCH, c, :, STATE * (g % 2):STATE * (g % 2) + STATE],
                                  src[g]).then_inc(c_in, 16)
            act.wait_ge(misc_done, M_X + 8)
            for c, name in enumerate(("ssm_b_re_2", "ssm_b_im_2")):
                act.dma_start(b_nat[:, c, :, :], d[name][0].rearrange("(r s) p h -> (s p) r h", s=2)).then_inc(b_in, 16)

            act.wait_ge(eps_ready, 2)

            def square(n, q0, src):
                if q0 + n >= SQ:
                    act.wait_ge(sq_summed, q0 if n < SQ else q0 + n - SQ + 1)
                nc.scalar.activation(sq[:, n % SQ, :], src, ACT.Square).then_inc(squared, 1)

            def root(r, q_end, width, eps=eps_c):
                act.wait_ge(sq_summed, q_end)
                if r > 1:
                    act.wait_ge(rstd_ready, r - 1)
                nc.scalar.activation(sdev[:, 0:T], ps_n[:, 0:T], ACT.Sqrt, bias=eps, scale=1.0 / width).then_inc(rooted, 1)

            def read_out(tile0, n, dst, func=ACT.Copy, **kw):
                act.wait_ge(proj_done, tile0 + (n + 1))
                return nc.scalar.activation(dst, ps_p[:, n % PSLOTS, :], func, **kw).then_inc(proj_freed, 1)

            def high_part(slab, b, done=None):
                if done is not None:
                    act.wait_ge(proj_done, done)
                act.wait_ge(raw_landed[b], slab * 8 + (16 - 8 * b))
                for half in range(2):
                    at = slice(half * SLAB // 2, (half + 1) * SLAB // 2)
                    act_copy(w_hi[:, b, at], w_raw[:, b, at]).then_inc(hi_ready, 1)

            def next_high(slab0, tile0, n):
                per = 2 if isinstance(slab0, int) and SLAB_VG <= slab0 < SLAB_OUT2 else 1
                if not (isinstance(slab0, int) and slab0 + n // per + 2 >= SLABS):
                    high_part(slab0 + (n // per + 2), (n // per) % SBUF2, tile0 + (n + 1))

            def operand_high(k, src, n=2):
                act_copy(a_hi[:, k:k + n, :], src).then_inc(a_hi_ready, 1)

            def normed_high(q0):
                for g in range(KD // 2):
                    act.wait_ge(h_scaled, q0 + 2 * g + 2)
                    operand_high(2 * g, h_t[:, 2 * g:2 * g + 2, :])

            for n in range(KD):
                act.wait_ge(misc_freed, M_X + TT * (n // 4 + 1))
                square(n, 0, x_t[:, n, :])
            for b in range(SBUF2):
                high_part(b, b)
            root(1, KD, D)
            normed_high(0)

            with act.Fori(0, 3) as i:
                for t in range(8):
                    next_high(i * 8, i * 8, t)
                    read_out(i * 8, t, slot(i * 8 + t))
            act.wait_ge(proj_freed, freed(24))
            with act.Fori(0, 4) as i:
                for e in range(2):
                    head = i * 2 + e
                    act.wait_ge(sq_summed, KD)
                    nc.scalar.activation(sq[:, 0, :], slot(head + Q0), ACT.Square).then_inc(head_squared, 1)
                    nc.scalar.activation(sq[:, 1, :], slot(head + K0), ACT.Square).then_inc(head_squared, 1)
                    act_copy(att_v, slot(head + V0)).then_inc(v_copied, 1)
                    act.wait_ge(head_summed, head + 1)
                    act.wait_ge(rstd_ready, head + 1)
                    nc.scalar.activation(sdev, ps_n, ACT.Sqrt, bias=eps_c, scale=1.0 / HEAD_DIM).then_inc(rooted, 1)
                    next_high(i * 8 + 24, i * 8 + 24, 4 * e)
                    read_out(i * 8 + 24, 4 * e, slot(i * 8 + (24 + 4 * e)))
                    for j, (lo, hi) in enumerate(((0, P), (P, 3 * P))):
                        act.wait_ge(nmax_ready, head + 1)
                        nc.scalar.activation(att_p[:, lo:hi], att_s[:, lo:hi], ACT.Exp, bias=att_nmax[:, j:j + 1],
                                             scale=HEAD_DIM ** -0.5, accum_out=att_sum[:, j:j + 1]).then_inc(exp_ready, 1)
                    next_high(i * 8 + 24, i * 8 + 24, 4 * e + 1)
                    read_out(i * 8 + 24, 4 * e + 1, slot(i * 8 + (25 + 4 * e)))
                    act.wait_ge(probs_turned, head + 1)
                    act_copy(att_pt, ps_pt).then_inc(pt_ready, 1)
                    next_high(i * 8 + 24, i * 8 + 24, 4 * e + 2)
                    read_out(i * 8 + 24, 4 * e + 2, slot(i * 8 + (26 + 4 * e)))
                    act.wait_ge(proj_freed, freed(24))
                    act.wait_ge(out_done, head + 1)
                    act_copy(slot(head + Q0), ps_o).then_inc(out_ready, 1)
                    next_high(i * 8 + 24, i * 8 + 24, 4 * e + 3)
                    read_out(i * 8 + 24, 4 * e + 3, slot(i * 8 + (27 + 4 * e)))
            act.wait_ge(proj_freed, freed(32))
            act.wait_ge(out_ready, HEADS + 1)
            for t in range(8):
                square(t, 16, slot(Q0 + t))
                next_high(56, 56, t)
                read_out(56, t, slot(ZC0 + t), ACT.Silu)
            nc.scalar.activation(slot(ZA0, KH), slot(ZA0, KH), ACT.Silu).then_inc(za_silu, 1)
            root(10, 24, HALF)
            act.wait_ge(yconv_raw, 1)
            for n in range(KH):
                square(n, 24, slot(HC0 + n))
            root(11, 32, HALF)
            act.wait_ge(proj_done, TILE_OUT)
            for g, s0 in enumerate((Q0, HC0)):
                act.wait_ge(y_final, g + 1)
                operand_high(KH * (1 - g), slots[:, s0:s0 + KH, :], KH)

            def out_squares(slab0, tile0, q0, at, first_bank, banks, bank_out):
                for n in range(KD):
                    next_high(slab0, tile0, n)
                    act.wait_ge(proj_freed, freed(tile0 + n + 1))
                    square(n, q0, x_t[:, n, :])
                    if n == at:
                        for u in range(banks):
                            act.wait_ge(misc_done, first_bank + u + 1)
                            dst, scale = bank_out(u)
                            nc.scalar.activation(dst, ps_m[:, (first_bank + u) % 2, :], ACT.Copy, scale=scale).then_inc(misc_freed, 1)

            def ssm_matrix(u):
                c, half = (u // 2) % 2, u % 2
                dst = (bt if u < 4 else ct)[:, c, 4 * half:4 * half + 4, :].rearrange("p a b -> p (a b)")
                return dst, (-1.0 if u >= 4 and c == 1 else 1.0)

            out_squares(SLAB_OUT, TILE_OUT, 32, 7, M_BC, 8, ssm_matrix)
            root(12, 48, D)
            normed_high(KD)

            for t in range(8):
                next_high(SLAB_IN2, TILE_IN2, t)
                read_out(TILE_IN2, t, slot(SSM0 + t))

            def ssm_inputs(half):
                for n in range(HPAIRS):
                    m = M_BU[half] + n
                    act.wait_ge(misc_done, m + 1)
                    act_copy(xs[:, :, n, :], ps_m[:, m % 2, :].rearrange("p (c t) -> p c t", c=2)).then_inc(misc_freed, 1)

            def ssm_gelu(half):
                for n in range(4):
                    act.wait_ge(ssm_sum, 4 * half + n + 1)
                    nc.scalar.activation(slot(SSM0 + 4 * half + n), slot(SSM0 + 4 * half + n),
                                         ACT.Gelu_apprx_tanh).then_inc(z_ready, 1)

            ssm_inputs(0)
            for t in range(8):
                next_high(SLAB_IN2 + 8, TILE_IN2 + 8, t)
                read_out(TILE_IN2 + 8, t, slot(GLU0 + t))
            for t in range(8):
                next_high(SLAB_IN2 + 16, TILE_IN2 + 16, t)
                read_out(TILE_IN2 + 16, t, slot(SIG0 + t), ACT.Sigmoid)

            def gate_tiles(first, last):
                with act.Fori(first // 4, last // 4) as i:
                    for t in range(4):
                        next_high(i * 4 + (SLAB_IN2 + 24), i * 4 + (TILE_IN2 + 24), t)
                        read_out(i * 4 + (TILE_IN2 + 24), t, slot(i * 4 + (GA0 + t)), ACT.Sigmoid,
                                 bias=params[:, bass.ds(i * 4 + (C_GATE + t), 1)])

            gate_tiles(0, 4)
            ssm_inputs(1)
            ssm_gelu(0)
            gate_tiles(4, 24)
            ssm_gelu(1)
            gate_tiles(24, 32)
            act.wait_ge(z_ready, KH)
            for g in range(2):
                operand_high(4 * g, slots[:, SSM0 + 4 * g:SSM0 + 4 * g + 4, :], 4)

            def value_tiles(g, first=0, last=8):
                for t in range(first, last):
                    if t == 0 and g > 1:
                        act.wait_ge(val_gated, g - 1)
                    if t == 0 and g == 0:
                        act.wait_ge(glu_ready, 1)
                    if t % 2:
                        next_high(SLAB_VG + 4 * g, TILE_VG + 8 * g, t)
                    read_out(TILE_VG + 8 * g, t, slot(VAL0 * (1 - g % 2) + t), ACT.Copy if t < 4 else ACT.Sigmoid)

            value_tiles(0)
            value_tiles(1)
            value_tiles(2)
            value_tiles(3, 0, LN_MEAN - 23)
            act.wait_ge(centred, 1)
            act.wait_ge(rstd_ready, 12)
            nc.scalar.activation(sdev[:, 0:T], ps_n[:, 0:T], ACT.Copy, scale=1.0 / HALF).then_inc(rooted, 1)
            value_tiles(3, LN_MEAN - 23, LN_VAR - 25)
            act.wait_ge(centred, 2)
            for n in range(KH):
                square(n, 48, slot(CONV0 + n))
            value_tiles(3, LN_VAR - 25, 8)
            root(14, 56, HALF, ln_eps_c)
            for n in range(KH):
                act.wait_ge(ln_scaled, n + 1)
                nc.scalar.activation(slot(CONV0 + n), slot(CONV0 + n), ACT.Silu,
                                     bias=params[:, C_LNB + n:C_LNB + n + 1]).then_inc(conv_act, 1)
                if n % 2:
                    act.wait_ge(conv_act, n + 1)
                    operand_high(KH + n - 1, slots[:, CONV0 + n - 1:CONV0 + n + 1, :])
            for g in range(KD // 2):
                next_high(SLAB_CV, TILE_CV, 2 * g + 1)
                if g < KH // 2:
                    act.wait_ge(merged, 2 * g + 2)
                    operand_high(2 * g, slots[:, GA0 + 2 * g:GA0 + 2 * g + 2, :])
            for g in range(KH // 2, KD // 2):
                act.wait_ge(merged, 2 * g + 2)
                operand_high(2 * g, slots[:, GA0 + 2 * g:GA0 + 2 * g + 2, :])

            def keys_out(u):
                return subt[:, 4 * u:4 * u + 4, :].rearrange("p a b -> p (a b)"), 1.0

            out_squares(SLAB_OUT2, TILE_OUT2, 56, 11, M_SUB, 4, keys_out)
            root(15, 72, D)
            normed_high(2 * KD)

            def scores_out(h):
                m = M_S + h
                act.wait_ge(misc_done, m + 1)
                act_copy(x_f.rearrange("p (t a) -> p t a", t=TT)[:, :, 2 * h * KEYS:2 * (h + 1) * KEYS],
                         ps_m[:, m % 2, :].rearrange("p (t a) -> p t a", t=TT)).then_inc(misc_freed, 1)

            for n in range(16):
                next_high(SLAB_WQ, TILE_WQ, n)
                read_out(TILE_WQ, n, slot(n))
                for u in range(4 * n, 4 * n + 4 if n < 4 else 4 * n):
                    act.wait_ge(misc_done, M_TOK + u + 1)
                    dst, t, g = (y_tok, h_tok)[u // 8], (u // 4) % 2, u % 4
                    act_copy(dst[:, t, 512 * g:512 * g + 512], ps_m[:, (M_TOK + u) % 2, :]).then_inc(misc_freed, 1)
                if n in SCORE_AFTER:
                    scores_out(SCORE_AFTER.index(n))

            def softmax_exp(t):
                act.wait_ge(best_ready, t + 1)
                nc.scalar.activation(gates[:, t * P:(t + 1) * P], gates[:, t * P:(t + 1) * P], ACT.Exp).then_inc(best_exp, 1)

            softmax_exp(0)
            for t in range(TT):
                act.wait_ge(dots_ready, (t + 1) * PICKS)
                nc.scalar.activation(pick_w[:, t * P:(t + 1) * P], dots[:, t * P:(t + 1) * P], ACT.Gelu_apprx_tanh).then_inc(gelu_ready, 1)
                act.wait_ge(w_ready, t + 1)
                with act.Fori(0, ROUNDS) as i:
                    for n in range(PE_ROWS):
                        act.wait_ge(row_free[n], i + ((2 * t + 1) * ROUNDS + 1))
                        nc.scalar.activation(diag[:, n, :], ident[:, :], ACT.Copy,
                                             scale=pick_w[:, bass.ds(i * ROWS + (t * P + n), 1)]).then_inc(diag_ready, 1)
                if t == 0:
                    softmax_exp(1)
                act.wait_ge(y_ready, t + 1)
                nc.scalar.activation(onehot, y_tok[:, t, :], ACT.Square, accum_out=out_ss[:, t:t + 1]).then_inc(out_squared, 1)
                act.wait_ge(out_squared, t + 1)
                nc.scalar.activation(out_sd[:, t:t + 1], out_ss[:, t:t + 1], ACT.Sqrt, bias=eps_c, scale=1.0 / D).then_inc(out_rooted, 1)

        @block.vector
        def _(dve):
            own = Chain(dve, dve_step)
            v = nc.vector
            v.memset(eps_c, EPS).then_inc(eps_ready, 1)
            v.memset(ln_eps_c, LN_EPS).then_inc(eps_ready, 1)
            v.memset(ps_p, 0.0).then_inc(proj_freed, PSLOTS)
            v.memset(ps_o, 0.0).then_inc(out_ready, 1)

            for g in range(4):
                for t in range(TT):
                    m = M_X + TT * g + t
                    dve.wait_ge(misc_done, m + 1)
                    v.tensor_copy(x_t[:, 4 * g:4 * g + 4, t * P:(t + 1) * P],
                                  ps_m[:, m % 2, :].rearrange("p (a b) -> p a b", a=4)).then_inc(misc_freed, 1)
            dve.wait_ge(misc_done, M_VEC + 1)
            bank = ps_m[:, M_VEC % 2, :]
            own.step(v.tensor_copy(params[:, 0:90], bank[:, 0:90]))
            own.step(v.tensor_copy(params[:, 128:192], bank[:, 128:192]))
            own.step(v.tensor_copy(params[:, C_TAP:C_TAP + 124], bank[:, 256:380]))
            v.tensor_copy(params[:, C_TAP + 124:C_TAP + 248], bank[:, 384:508]).then_inc(misc_freed, 1)
            dve.wait_ge(misc_freed, M_VEC + 1)

            def invert_root(r):
                dve.wait_ge(rooted, r)
                v.reciprocal(rstd[:, 0:T], sdev[:, 0:T]).then_inc(rstd_ready, 1)
                dve.wait_ge(rstd_ready, r)

            def operand_low(group, k, src, n=2):
                dve.wait_ge(a_hi_ready, group + 1)
                v.tensor_tensor(a_lo[:, k:k + n, :], src, a_hi[:, k:k + n, :].bitcast(F32), ALU.subtract).then_inc(a_lo_ready, 1)

            def scale_residual(r, c0, group):
                invert_root(r)
                for g in range(KD // 2 + 1):
                    for k in range(2 * g, 2 * g + 2 if g < KD // 2 else 2 * g):
                        v.scalar_tensor_tensor(out=h_t[:, k, :], in0=x_t[:, k, :], scalar=params[:, k + c0:k + c0 + 1],
                                               in1=rstd[:, 0:T], op0=ALU.mult, op1=ALU.mult).then_inc(h_scaled, 1)
                    if g > 0:
                        operand_low(group + g - 1, 2 * g - 2, h_t[:, 2 * g - 2:2 * g, :])

            scale_residual(1, C_NORM, G_IN)

            dve.wait_ge(ssm_in, 16 * 3)
            buf = slots_f[0:PAIRS, 56 * T:63 * T].rearrange("p (a b) -> p a b", b=P)
            lam_re, lam_im, fac_re, fac_im = (buf[:, n, :] for n in range(4))
            a_re, a_im, t0, t1, t2, t3 = (buf[:, n, :] for n in (6, 7, 4, 5, 8, 9))
            t4, t5 = buf[:, 10, :], buf[:, 11, :]
            log_dt, dt = buf[:, 12, 0:2], buf[:, 12, 2:4]
            u0, u1, u2, u3 = (buf[:, 12, 8 + 8 * n:10 + 8 * n] for n in range(4))

            def scal(out, in0, s1, s2, op0, op1):
                own.do(v.tensor_scalar(out, in0, s1, s2, op0, op1))

            def stt(out, in0, s, in1, op0, op1):
                own.do(v.scalar_tensor_tensor(out=out, in0=in0, scalar=s, in1=in1, op0=op0, op1=op1))

            def tt(out, a, b, op):
                own.do(v.tensor_tensor(out, a, b, op))

            def exp(x, n, r, p, s):
                scal(r, x, -174.0, 176.0, ALU.max, ALU.min)
                scal(n, r, 1.4426950408889634, MAGIC, ALU.mult, ALU.add)
                scal(n, n, -MAGIC, None, ALU.add, ALU.bypass)
                stt(r, n, -0.693359375, r, ALU.mult, ALU.add)
                stt(r, n, 2.12194440e-4, r, ALU.mult, ALU.add)
                scal(p, r, 1.0 / 5040, None, ALU.mult, ALU.bypass)
                for c in (1.0 / 720, 1.0 / 120, 1.0 / 24, 1.0 / 6, 0.5, 1.0):
                    stt(p, p, c, r, ALU.add, ALU.mult)
                scal(p, p, 1.0, None, ALU.add, ALU.bypass)
                scal(r, n, 0.5, MAGIC, ALU.mult, ALU.add)
                scal(r, r, -MAGIC, None, ALU.add, ALU.bypass)
                tt(n, n, r, ALU.subtract)
                for half in (r, n):
                    scal(s.bitcast(I32), half, 127.0, 8388608.0, ALU.add, ALU.mult)
                    tt(p, p, s, ALU.mult)

            exp(log_dt, u0, u1, dt, u2)
            for s in range(2):
                own.do(v.tensor_scalar(t0[:, s * STATE:(s + 1) * STATE], a_re[:, s * STATE:(s + 1) * STATE],
                                       dt[:, s:s + 1], None, ALU.mult))
            exp(t0, t1, t2, t3, t4)
            for s in range(2):
                own.do(v.tensor_scalar(t0[:, s * STATE:(s + 1) * STATE], a_im[:, s * STATE:(s + 1) * STATE],
                                       dt[:, s:s + 1], None, ALU.mult))
            scal(t1, t0, 0.6366197723675814, MAGIC, ALU.mult, ALU.add)
            scal(t1, t1, -MAGIC, None, ALU.add, ALU.bypass)
            for c in (1.5703125, 4.837512969970703e-4, 7.549789948768648e-8):
                stt(t0, t1, -c, t0, ALU.mult, ALU.add)
            scal(t2, t1, 0.25, -0.375, ALU.mult, ALU.add)
            scal(t2, t2, MAGIC, None, ALU.add, ALU.bypass)
            scal(t2, t2, -MAGIC, None, ALU.add, ALU.bypass)
            stt(t1, t2, -4.0, t1, ALU.mult, ALU.add)
            tt(t2, t0, t0, ALU.mult)
            scal(t4, t2, 1.0 / 362880, None, ALU.mult, ALU.bypass)
            for c in (-1.0 / 5040, 1.0 / 120, -1.0 / 6):
                stt(t4, t4, c, t2, ALU.add, ALU.mult)
            stt(t4, t4, 1.0, t0, ALU.add, ALU.mult)
            scal(t5, t2, -1.0 / 3628800, None, ALU.mult, ALU.bypass)
            for c in (1.0 / 40320, -1.0 / 720, 1.0 / 24, -0.5):
                stt(t5, t5, c, t2, ALU.add, ALU.mult)
            scal(t5, t5, 1.0, None, ALU.add, ALU.bypass)
            scal(t0, t1, 1.0, None, ALU.is_equal, ALU.bypass)
            stt(t0, t1, 3.0, t0, ALU.is_equal, ALU.add)
            scal(t2, t0, -1.0, 1.0, ALU.mult, ALU.add)
            tt(lam_re, t0, t4, ALU.mult)
            tt(fac_re, t2, t5, ALU.mult)
            tt(lam_re, lam_re, fac_re, ALU.add)
            tt(lam_im, t0, t5, ALU.mult)
            tt(fac_im, t2, t4, ALU.mult)
            tt(lam_im, lam_im, fac_im, ALU.add)
            scal(t2, t1, 2.0, None, ALU.is_ge, ALU.bypass)
            scal(t2, t2, -2.0, 1.0, ALU.mult, ALU.add)
            tt(lam_im, lam_im, t2, ALU.mult)
            scal(t2, t1, 1.0, None, ALU.is_equal, ALU.bypass)
            stt(t2, t1, 2.0, t2, ALU.is_equal, ALU.add)
            scal(t2, t2, -2.0, 1.0, ALU.mult, ALU.add)
            tt(lam_re, lam_re, t2, ALU.mult)
            tt(lam_re, lam_re, t3, ALU.mult)
            tt(lam_im, lam_im, t3, ALU.mult)
            tt(t0, a_re, a_re, ALU.mult)
            tt(t1, a_im, a_im, ALU.mult)
            tt(t0, t0, t1, ALU.add)
            own.do(v.reciprocal(t1, t0))
            scal(t2, lam_re, -1.0, None, ALU.add, ALU.bypass)
            tt(t3, t2, a_re, ALU.mult)
            tt(t4, lam_im, a_im, ALU.mult)
            tt(t3, t3, t4, ALU.add)
            tt(fac_re, t3, t1, ALU.mult)
            tt(t3, lam_im, a_re, ALU.mult)
            tt(t4, t2, a_im, ALU.mult)
            tt(t3, t3, t4, ALU.subtract)
            v.tensor_tensor(fac_im, t3, t1, ALU.mult).then_inc(ssm_coef, 1)

            dve.wait_ge(misc_done, M_LAM + 1)
            v.tensor_copy(lam_f[:, :, :], ps_m[:, M_LAM % 2, :].rearrange("p (a b) -> p a b", a=4)[:, :, 0:PAIRS]).then_inc(misc_freed, 1)
            dve.wait_ge(misc_freed, M_LAM + 1)
            pw = att_qk[:, 0:256], att_qk[:, 256:512]
            dve.wait_ge(misc_done, M_X + 8)
            for c in range(2):
                own.step(v.tensor_copy(powers[:, c, 0, :], lam_f[:, c, :]))
            own.wait()
            n = 1
            while n < CHUNK:
                re, im = powers[:, 0, 0:n, :], powers[:, 1, 0:n, :]
                by_re, by_im = (powers[:, c, n - 1, :].unsqueeze(1).broadcast_to([P, n, PAIRS]) for c in range(2))
                s0, s1 = (p[:, 0:n * PAIRS].rearrange("p (a b) -> p a b", a=n) for p in pw)
                for c, (p, q, op) in enumerate(((by_re, by_im, ALU.subtract), (by_im, by_re, ALU.add))):
                    own.step(v.tensor_tensor(s0, re, p, ALU.mult))
                    own.do(v.tensor_tensor(s1, im, q, ALU.mult))
                    own.do(v.tensor_tensor(powers[:, c, n:2 * n, :], s0, s1, op))
                n *= 2
            dve.wait_ge(b_in, 32)
            own.do(v.memset(b_diag, 0.0))
            f_re, f_im = (lam_f[:, 2 + c, :].unsqueeze(2).broadcast_to([P, PAIRS, GCH]) for c in range(2))
            pw3 = att_qk.rearrange("p (a b) -> p a b", b=GCH)
            pw4 = work[:, 1024:1536].rearrange("p (a b) -> p a b", b=GCH)
            for c, (p, q, op) in enumerate(((f_re, f_im, ALU.subtract), (f_im, f_re, ALU.add))):
                own.step(v.tensor_tensor(pw3, b_nat[:, 0, :, :], p, ALU.mult))
                own.do(v.tensor_tensor(pw4, b_nat[:, 1, :, :], q, ALU.mult))
                for s in range(2):
                    half = slice(s * STATE, (s + 1) * STATE)
                    own.step(v.tensor_tensor(b_diag[half, c, :, s * GCH:(s + 1) * GCH], pw3[half], pw4[half], op))
                own.wait()
            v.tensor_copy(small[:, 40:41], small[:, 0:1]).then_inc(bdiag_ready, 1)

            dve.wait_ge(mask_ready, 2)
            with dve.Fori(0, 4) as i:
                for e in range(2):
                    head = i * 2 + e
                    dve.wait_ge(rooted, head + 2)
                    v.reciprocal(rstd, sdev).then_inc(rstd_ready, 1)
                    dve.wait_ge(rstd_ready, head + 2)
                    for c, (s0, gain) in enumerate(((Q0, C_QG), (K0, C_KG))):
                        v.scalar_tensor_tensor(out=att_qk[:, c * T:(c + 1) * T], in0=slot(head + s0),
                                               scalar=params[:, gain:gain + 1], in1=rstd[:, c * T:(c + 1) * T],
                                               op0=ALU.mult, op1=ALU.mult).then_inc(qk_ready, 1)
                    dve.wait_ge(v_turned, head + 1)
                    v.tensor_copy(att_vtok, ps_o.rearrange("p (a b) -> p a b", a=2)).then_inc(v_ready, 1)
                    dve.wait_ge(scores_done, head + 1)
                    own_at = head * 4 + own.n
                    v.tensor_tensor(att_s, ps_s, mask, ALU.add).then_inc(dve_step, 1)
                    dve.wait_ge(dve_step, own_at + 1)
                    v.tensor_reduce(att_max[:, 0:1], att_s[:, 0:P], AX_X, ALU.max).then_inc(dve_step, 1)
                    v.tensor_reduce(att_max[:, 1:2], att_s[:, P:3 * P], AX_X, ALU.max).then_inc(dve_step, 1)
                    dve.wait_ge(dve_step, own_at + 3)
                    v.tensor_scalar(att_nmax, att_max, -HEAD_DIM ** -0.5, None, ALU.mult).then_inc(nmax_ready, 1)
                    dve.wait_ge(exp_ready, head * 2 + 2)
                    v.reciprocal(att_rsum, att_sum).then_inc(dve_step, 1)
                    dve.wait_ge(dve_step, own_at + 4)
                    for j, (lo, hi) in enumerate(((0, P), (P, 3 * P))):
                        v.tensor_scalar(att_p[:, lo:hi], att_p[:, lo:hi], att_rsum[:, j:j + 1], None,
                                        ALU.mult).then_inc(probs_ready, 1)
            own.n += 4 * HEADS

            dve.wait_ge(proj_freed, freed(56))
            own.do(v.tensor_tensor(slot(CG0, KH), slot(CG0, KH), slot(HC0, KH), ALU.mult))
            for tap in (2, 1, 0):
                lag = 2 - tap
                for n in range(KH):
                    w = params[:, C_CONV + tap * KH + n:C_CONV + tap * KH + n + 1]
                    u, y = slot(CG0 + n), slot(HC0 + n)
                    if lag == 0:
                        ins = v.tensor_scalar(y, u, w, None, ALU.mult)
                    else:
                        ins = v.scalar_tensor_tensor(out=y[:, lag:T], in0=u[:, 0:T - lag], scalar=w, in1=y[:, lag:T],
                                                     op0=ALU.mult, op1=ALU.add)
                    own.step(ins)
                own.wait()
            v.tensor_tensor(slot(HC0, KH), slot(HC0, KH), slot(BG0, KH), ALU.mult).then_inc(yconv_raw, 1)

            def norm_branch(r, s0, c0):
                invert_root(r)
                for n in range(KH):
                    own.step(v.scalar_tensor_tensor(out=slot(s0 + n), in0=slot(s0 + n), scalar=params[:, c0 + n:c0 + n + 1],
                                                    in1=rstd[:, 0:T], op0=ALU.mult, op1=ALU.mult))
                own.wait()

            norm_branch(10, Q0, C_AOUT)
            dve.wait_ge(za_silu, 1)
            v.tensor_tensor(slot(Q0, KH), slot(Q0, KH), slot(ZA0, KH), ALU.mult).then_inc(y_final, 1)
            norm_branch(11, HC0, C_COUT)
            dve.wait_ge(proj_freed, freed(64))
            v.tensor_tensor(slot(HC0, KH), slot(HC0, KH), slot(ZC0, KH), ALU.mult).then_inc(y_final, 1)
            for g, s0 in enumerate((Q0, HC0)):
                operand_low(G_MIX + g, KH * (1 - g), slots[:, s0:s0 + KH, :], KH)

            def add_residual(tile0):
                for n in range(KD):
                    dve.wait_ge(proj_done, tile0 + n + 1)
                    v.tensor_tensor(x_t[:, n, :], x_t[:, n, :], ps_p[:, n % PSLOTS, :], ALU.add).then_inc(proj_freed, 1)

            add_residual(TILE_OUT)
            scale_residual(12, C_MIX, G_IN2)

            prod = [norm_ws[:, 1024 + 256 * n:1280 + 256 * n] for n in range(4)]

            def rotate(here, before, lam, width):
                p0, p1, p2, p3 = (p[:, 0:HPAIRS * width].rearrange("p (r k) -> p r k", r=HPAIRS) for p in prod)
                (re, im), (b_re, b_im), (l_re, l_im) = here, before, lam
                own.wait(1)
                own.step(v.tensor_tensor(p0, b_re, l_re, ALU.mult))
                own.step(v.tensor_tensor(p1, b_re, l_im, ALU.mult))
                own.wait(2)
                own.step(v.tensor_tensor(p2, b_im, l_im, ALU.mult))
                own.step(v.tensor_tensor(p3, b_im, l_re, ALU.mult))
                own.wait(3)
                own.step(v.tensor_tensor(re, re, p0, ALU.add))
                own.wait(3)
                own.step(v.tensor_tensor(im, im, p1, ALU.add))
                own.wait(1)
                own.step(v.tensor_tensor(re, re, p2, ALU.subtract))
                own.wait(1)
                own.step(v.tensor_tensor(im, im, p3, ALU.add))

            def scan(half):
                dve.wait_ge(misc_freed, M_BU[half] + 16)
                pairs = slice(HPAIRS * half, HPAIRS * half + HPAIRS)

                def power(j, width):
                    if isinstance(j, int):
                        p = [powers[:, c, j, pairs] for c in range(2)]
                    else:
                        p = [powers[:, c, bass.ds(j, 1), pairs].rearrange("p o r -> p (o r)") for c in range(2)]
                    return [x.unsqueeze(2).broadcast_to([P, HPAIRS, width]) for x in p]

                def token(j):
                    x = xs_j[:, :, bass.ds(j, 1)].rearrange("p (c r k) o -> p c r (k o)", c=2, r=HPAIRS)
                    return x[:, 0], x[:, 1]

                lam1 = power(0, CHUNKS)
                own.wait()
                with own.loop(1, CHUNK, 8) as j:
                    rotate(token(j), token(j - 1), lam1, CHUNKS)
                own.wait()
                lam16 = [powers[:, c, CHUNK - 1, pairs].unsqueeze(1).unsqueeze(3).broadcast_to([P, 2, HPAIRS, 1]) for c in range(2)]
                w1, w2 = (p[:, 0:2 * HPAIRS].rearrange("p (c r k) -> p c r k", c=2, r=HPAIRS) for p in prod[0:2])
                flat = lambda w: w.rearrange("p c r k -> p (c r k)")
                with own.loop(1, CHUNKS, 5) as k:
                    before = xs_cj[:, :, bass.ds(k - 1, 1), CHUNK - 1:CHUNK].rearrange("p (c r) k j -> p c r (k j)", c=2)
                    here = xs_cj[:, :, bass.ds(k, 1), CHUNK - 1:CHUNK].rearrange("p a k j -> p (a k j)")
                    n = HPAIRS
                    own.step(v.tensor_tensor(w1, before, lam16[0], ALU.mult))
                    own.do(v.tensor_tensor(w2, before, lam16[1], ALU.mult))
                    own.do(v.tensor_tensor(here, here, flat(w1), ALU.add))
                    own.step(v.tensor_tensor(here[:, 0:n], here[:, 0:n], flat(w2)[:, n:2 * n], ALU.subtract))
                    own.do(v.tensor_tensor(here[:, n:2 * n], here[:, n:2 * n], flat(w2)[:, 0:n], ALU.add))
                carry = xs_cj[:, :, 0:CHUNKS - 1, CHUNK - 1].rearrange("p (c r) k -> p c r k", c=2)
                with own.loop(0, CHUNK - 1, 8) as j:
                    here = xs_cj[:, :, 1:CHUNKS, bass.ds(j, 1)].rearrange("p (c r) k o -> p c r (k o)", c=2)
                    rotate((here[:, 0], here[:, 1]), (carry[:, 0], carry[:, 1]), power(j, CHUNKS - 1), CHUNKS - 1)
                own.wait()
                v.tensor_copy(small[:, 41 + half:42 + half], small[:, 0:1]).then_inc(scanned, 1)

            def skip_sum(half):
                for n in range(4):
                    a, m = 4 * half + n, M_CY[half] + n
                    dve.wait_ge(misc_done, m + 1)
                    own.do(v.scalar_tensor_tensor(out=slot(SSM0 + a), in0=slot(SSM0 + a), scalar=params[:, C_SKIP + a:C_SKIP + a + 1],
                                                  in1=ps_m[:, m % 2, 0:T], op0=ALU.mult, op1=ALU.add))
                    v.tensor_copy(small[:, 44:45], small[:, 0:1]).then_inc(ssm_sum, 1)
                    v.tensor_copy(small[:, 45:46], small[:, 0:1]).then_inc(misc_freed, 1)

            scan(0)
            skip_sum(0)
            scan(1)
            skip_sum(1)

            dve.wait_ge(misc_done, M_CY[1] + 4)
            dve.wait_ge(proj_freed, freed(TILE_IN2 + 24))
            own.step(v.memset(glu_pad[:, :, 0:TAPS2 - 1], 0.0))
            own.do(v.tensor_tensor(glu_pad[:, :, TAPS2 - 1:], slots[:, GLU0:GLU0 + KH, :], slots[:, SIG0:SIG0 + KH, :], ALU.mult))
            v.tensor_copy(small[:, 51:52], small[:, 0:1]).then_inc(glu_ready, 1)
            for n in range(KH):
                last = TAPS2 - 1
                w = params[:, C_TAP + last * KH + n:C_TAP + last * KH + n + 1]
                own.step(v.tensor_scalar(slot(CONV0 + n), glu_pad[:, n, last:last + T], w, params[:, C_CB + n:C_CB + n + 1],
                                         ALU.mult, ALU.add))

            def taps(first, last):
                with own.loop(first, last, KH) as tap:
                    for n in range(KH):
                        own.wait(KH - 1)
                        own.step(v.scalar_tensor_tensor(out=slot(CONV0 + n), in0=glu_pad[:, n, bass.ds(tap, T)],
                                                        scalar=params[:, bass.ds(tap * KH + (C_TAP + n), 1)], in1=slot(CONV0 + n),
                                                        op0=ALU.mult, op1=ALU.add))

            def gate_values(g):
                dve.wait_ge(proj_freed, freed(TILE_VG + 8 * g + 8))
                val = VAL0 * (1 - g % 2)
                own.do(v.tensor_tensor(slot(val, 4), slot(val, 4), slot(val + 4, 4), ALU.mult))
                v.tensor_tensor(slot(GB0 + 4 * g, 4), slot(GB0 + 4 * g, 4), slot(val, 4), ALU.mult).then_inc(val_gated, 1)

            taps(0, 10)
            for g in range(2):
                operand_low(G_Z + g, 4 * g, slots[:, SSM0 + 4 * g:SSM0 + 4 * g + 4, :], 4)
            taps(10, 17)
            gate_values(0)
            taps(17, 23)
            gate_values(1)
            taps(23, TAPS2 - 1)
            own.wait()
            v.tensor_copy(small[:, 43:44], small[:, 0:1]).then_inc(conv_done, 1)
            gate_values(2)
            dve.wait_ge(rooted, 13)
            conv = slots[:, CONV0:CONV0 + KH, :]
            own.do(v.tensor_tensor(conv, conv, sdev[:, 0:T].unsqueeze(1).broadcast_to([P, KH, T]), ALU.subtract))
            v.tensor_copy(small[:, 46:47], small[:, 0:1]).then_inc(centred, 1)
            v.tensor_copy(small[:, 47:48], small[:, 0:1]).then_inc(rstd_ready, 1)
            invert_root(14)
            for n in range(KH):
                v.scalar_tensor_tensor(out=slot(CONV0 + n), in0=slot(CONV0 + n), scalar=params[:, C_LNG + n:C_LNG + n + 1],
                                       in1=rstd[:, 0:T], op0=ALU.mult, op1=ALU.mult).then_inc(ln_scaled, 1)
            for g in range(KH // 2):
                operand_low(G_CV + g, KH + 2 * g, slots[:, CONV0 + 2 * g:CONV0 + 2 * g + 2, :])
            gate_values(3)
            dve.wait_ge(val_gated, 4)
            for n in range(KD):
                dve.wait_ge(proj_done, TILE_CV + n + 1)
                v.tensor_tensor(slot(GA0 + n), slot(GA0 + n), ps_p[:, n % PSLOTS, :], ALU.mult).then_inc(proj_freed, 1)
                dve.wait_ge(proj_freed, freed(TILE_CV + n + 1))
                v.tensor_tensor(slot(GA0 + n), slot(GA0 + n), slot(GB0 + n), ALU.add).then_inc(merged, 1)
                if n % 2 and 2 < n < KH + 2:
                    operand_low(G_MERGE + n // 2 - 1, n - 3, slots[:, GA0 + n - 3:GA0 + n - 1, :])
            for g in range(KH // 2, KD // 2):
                operand_low(G_MERGE + g, 2 * g, slots[:, GA0 + 2 * g:GA0 + 2 * g + 2, :])

            add_residual(TILE_OUT2)
            scale_residual(15, C_FFN, G_Q)

            s4 = tk_s.rearrange("p (h c k) -> p h c k", h=PEER_H, c=2)

            def best16(src, val, idx):
                n = range(len(src))
                for half in range(2):
                    at = slice(8 * half, 8 * half + 8)
                    for m in n:
                        own.step(v.max(val[m][:, at], src[m]))
                    own.wait()
                    for m in n:
                        own.step(v.max_index(idx[m][:, at], val[m][:, at], src[m]))
                    if half == 0:
                        for m in n:
                            own.step(v.match_replace(src[m], val[m][:, at], src[m], -3.0e38))
                    own.wait()

            def head_picks(t, h):
                dve.wait_ge(misc_freed, M_S + h + 1)
                own.wait()
                two = range(2)
                best16([key_s[:, t, 2 * h + c, :] for c in two], [tk_s[:, (2 * h + c) * 16:(2 * h + c + 1) * 16] for c in two],
                       [tk_iu[:, (2 * h + c) * 16:(2 * h + c + 1) * 16] for c in two])
                own.do(v.tensor_tensor(tk_cand.rearrange("p (a b) -> p a b", a=16),
                                       s4[:, h, 0, :].unsqueeze(2).broadcast_to([P, 16, 16]),
                                       s4[:, h, 1, :].unsqueeze(1).broadcast_to([P, 16, 16]), ALU.add))
                best16([tk_cand], [tk_best[:, h * 16:(h + 1) * 16]], [tk_pos[:, h * 16:(h + 1) * 16]])

            def experts(t):
                cols = slice(t * P, (t + 1) * P)
                by_head = lambda a: a.rearrange("p (h k) -> p h k", h=PEER_H)
                own.wait()
                dve.wait_ge(zero_ready, 1)
                g = by_head(gates[:, cols])
                v.tensor_tensor(g, by_head(tk_best), by_head(tk_best)[:, :, 0:1].broadcast_to([P, PEER_H, PEER_K]),
                                ALU.subtract).then_inc(best_ready, 1)
                own.step(v.tensor_scalar(tk_hi, tk_pos, 4, None, ALU.logical_shift_right))
                own.step(v.tensor_scalar(tk_lo, tk_pos, 15, None, ALU.bitwise_and))
                own.do(v.tensor_copy(tk_if, tk_iu))
                own.step(v.tensor_copy(tk_hif, tk_hi))
                own.do(v.tensor_copy(tk_lof, tk_lo))
                i4 = tk_if.rearrange("p (h c k) -> p h c k", h=PEER_H, c=2)
                hot = onehot.rearrange("p (n a) -> p n a", a=16)
                hot4 = onehot.rearrange("p (h k a) -> p h k a", h=PEER_H, k=PEER_K)
                for c, (pos, e) in enumerate(((tk_hif, tk_e1), (tk_lof, tk_e2))):
                    own.do(v.tensor_tensor(hot, pos.unsqueeze(2).broadcast_to([P, PICKS, 16]),
                                           iota16.unsqueeze(1).broadcast_to([P, PICKS, 16]), ALU.is_equal))
                    own.do(v.tensor_tensor(hot4, hot4, i4[:, :, c, :].unsqueeze(2).broadcast_to([P, PEER_H, PEER_K, 16]), ALU.mult))
                    own.do(v.tensor_reduce(e, hot, AX_X, ALU.add))
                v.scalar_tensor_tensor(out=picks[:, cols], in0=tk_e1, scalar=float(KEYS), in1=tk_e2, op0=ALU.mult,
                                       op1=ALU.add).then_inc(picks_ready, 1)
                dve.wait_ge(best_exp, t + 1)
                own.do(v.tensor_reduce(head_sum, g, AX_X, ALU.add))
                own.do(v.reciprocal(head_rs, head_sum))
                own.do(v.tensor_tensor(g, g, head_rs.unsqueeze(2).broadcast_to([P, PEER_H, PEER_K]), ALU.mult))

            for h in range(PEER_H):
                head_picks(0, h)
            experts(0)

            def dot_rows(t):
                with dve.Fori(0, ROUNDS) as i:
                    for n in range(ROWS):
                        dve.wait_ge(gathered[n], (i + (2 * t * ROUNDS + 1)) * 16)
                        v.scalar_tensor_tensor(out=rows[n], in0=rows[n], scalar=1.0, in1=h_tok[:, t, :], op0=ALU.mult,
                                               op1=ALU.mult, accum_out=dots[:, bass.ds(i * ROWS + (t * P + n), 1)]).then_inc(row_free[n], 1)
                for n in range(ROWS):
                    dve.wait_ge(row_free[n], (2 * t + 1) * ROUNDS + 1)
                v.tensor_copy(small[:, 48:49], small[:, 0:1]).then_inc(dots_ready, PICKS)
                dve.wait_ge(gelu_ready, t + 1)
                cols = slice(t * P, (t + 1) * P)
                v.tensor_tensor(pick_w[:, cols], pick_w[:, cols], gates[:, cols], ALU.mult).then_inc(w_ready, 1)
                dve.wait_ge(w_ready, t + 1)

            def add_rows(t, i):
                for n in range(PE_ROWS, ROWS):
                    dve.wait_ge(gathered[n], (i + ((2 * t + 1) * ROUNDS + 1)) * 16)
                    at = i * ROWS + (t * P + n)
                    w = pick_w[:, at:at + 1] if isinstance(at, int) else pick_w[:, bass.ds(at, 1)]
                    v.scalar_tensor_tensor(out=y_tok[:, t, :], in0=rows[n], scalar=w, in1=y_tok[:, t, :],
                                           op0=ALU.mult, op1=ALU.add).then_inc(row_free[n], 1)
                    dve.wait_ge(row_free[n], i + ((2 * t + 1) * ROUNDS + 2))

            def finish(t):
                dve.wait_ge(v_summed, t + 1)
                own.do(v.tensor_tensor(y_tok[:, t, :].rearrange("p (c n) -> p c n", c=4), y_tok[:, t, :].rearrange("p (c n) -> p c n", c=4),
                                       ps_v, ALU.add))
                v.tensor_copy(small[:, 49:50], small[:, 0:1]).then_inc(v_read, 1)
                v.tensor_copy(small[:, 50:51], small[:, 0:1]).then_inc(y_ready, 1)
                dve.wait_ge(out_rooted, t + 1)
                own.do(v.reciprocal(out_rs[:, t:t + 1], out_sd[:, t:t + 1]))
                dve.wait_ge(gain_in, 16)
                v.scalar_tensor_tensor(out=y_tok[:, t, :], in0=y_tok[:, t, :], scalar=out_rs[:, t:t + 1], in1=gain_b,
                                       op0=ALU.mult, op1=ALU.mult).then_inc(normed, 1)

            dve.wait_ge(misc_freed, M_S + 8)
            dot_rows(0)
            for i in range(ROUNDS):
                if i == ROUNDS - 1:
                    experts(1)
                if i < PEER_H:
                    head_picks(1, i)
                add_rows(0, i)
            finish(0)
            dot_rows(1)
            with dve.Fori(0, ROUNDS) as i:
                add_rows(1, i)
            finish(1)


_INPUTS = [
    "x", "norm_gain", "w_in", "conv_w", "q_norm_gain", "k_norm_gain", "conv_out_gain", "attn_out_gain", "w_out",
    "norm_mix_2", "w_in_2", "b_gate_2", "conv_w_dw_2", "conv_b_dw_2", "conv_ln_g_2", "conv_ln_b_2", "conv_w_out_2",
    "ssm_a_re_2", "ssm_a_im_2", "ssm_log_dt_2", "ssm_b_re_2", "ssm_b_im_2", "ssm_c_re_2", "ssm_c_im_2", "ssm_d_2",
    "ssm_w_val_2", "ssm_w_gate_2", "w_out_2", "norm_ffn_2", "peer_w_q_2", "peer_sub_keys_2", "peer_u_2", "peer_v_2",
    "norm_final_2",
]


def kernel(**inputs):
    import numpy as np
    import concourse.bacc as bacc
    from concourse.bass_utils import run_bass_kernel_spmd

    nc = bacc.Bacc("TRN2", target_bir_lowering=False, num_devices=1)
    arrays, aps = {}, {}
    for name in _INPUTS:
        a = np.ascontiguousarray(inputs[name])
        arrays[f"in_{name}"] = a
        aps[name] = nc.dram_tensor(f"in_{name}", a.shape, mybir.dt.from_np(a.dtype), kind="ExternalInput").ap()
    aps["out"] = nc.dram_tensor("out_y", (1, T, D), F32, kind="ExternalOutput").ap()
    build(nc, aps)
    result = run_bass_kernel_spmd(nc, [arrays], core_ids=[0])
    return result.results[0]["out_y"]
```

```python
from contextlib import ExitStack, contextmanager

import concourse.bass as bass
import concourse.mybir as mybir

F32 = mybir.dt.float32
F32R = mybir.dt.float32r
I32 = mybir.dt.int32
U32 = mybir.dt.uint32
ALU = mybir.AluOpType
ACT = mybir.ActivationFunctionType
AX_X = mybir.AxisListType.X

P = 128
T = 256
TT = T // P
D = 2048
KD = D // P
HALF = D // 2
KH = HALF // P
HEADS = 8
HEAD_DIM = P
EPS = 1e-6
LN_EPS = 1e-5

GROUPS, STATE, GCH = 64, 64, 16
PAIRS = GROUPS // 2
HPAIRS = PAIRS // 2
CHUNK = 16
CHUNKS = T // CHUNK
TAPS2 = 31

PEER_H, PEER_K, KEYS = 8, 16, 128
HEAD_PARTS = ((0, 4), (4, 7), (7, 8))
SCORE_AFTER = [4, 5, 6, 8, 10, 12, 14, 15]
PICKS = PEER_H * PEER_K

SLAB = 2048
SBUF2 = 2
PSLOTS = 2
SQ = 4

TILE_IN = 0
TILE_OUT = TILE_IN + 64
TILE_IN2 = TILE_OUT + 16
TILE_VG = TILE_IN2 + 56
TILE_CV = TILE_VG + 32
TILE_OUT2 = TILE_CV + 16
TILE_WQ = TILE_OUT2 + 16
SLAB_IN = 0
SLAB_OUT = SLAB_IN + 64
SLAB_IN2 = SLAB_OUT + 16
SLAB_VG = SLAB_IN2 + 56
SLAB_CV = SLAB_VG + 16
SLAB_OUT2 = SLAB_CV + 8
SLAB_WQ = SLAB_OUT2 + 16
SLABS = SLAB_WQ + 16
G_IN, G_MIX, G_IN2, G_Z, G_CV, G_MERGE, G_Q = 0, 8, 12, 20, 22, 26, 34

Q0, K0, V0, ZA0, HC0, BG0, CG0, ZC0 = range(0, 64, 8)
GLU0, SIG0, SSM0, GA0, GB0, CONV0 = 0, 8, 16, 24, 40, 56
MIX = ((Q0, KH, 1), (Q0 + 4, KH + 4, 1), (HC0, 0, 5), (HC0 + 4, 4, 9))
VAL0 = 8
H0 = 24
SUBK0, SUBT0 = 40, 16
TOPK0 = 48

C_NORM, C_MIX, C_FFN, C_COUT, C_AOUT, C_CONV, C_QG, C_KG = 0, 16, 32, 48, 56, 64, 88, 89
C_GATE, C_CB, C_LNG, C_LNB, C_SKIP = 128, 160, 168, 176, 184
C_TAP = 256

LN_MEAN, LN_VAR, LN_OUT = 22, 25, 29

MAGIC = 12582912.0


class Chain:

    def __init__(self, eng, sem):
        self.eng, self.sem, self.n, self.base = eng, sem, 0, 0

    def step(self, ins):
        ins.then_inc(self.sem, 1)
        self.n += 1

    def wait(self, but=0):
        self.eng.wait_ge(self.sem, self.base + (self.n - but))

    def do(self, ins):
        self.step(ins)
        self.wait()

    @contextmanager
    def loop(self, start, end, steps):
        before = self.n
        with self.eng.Fori(start, end) as i:
            self.base, self.n = i * steps + (before - start * steps), 0
            yield i
            assert self.n == steps, (self.n, steps)
        self.base, self.n = 0, before + (end - start) * steps


def build(nc, d):
    ctx = ExitStack()
    with ctx:
        def sb(name, shape, dt=F32):
            return ctx.enter_context(nc.sbuf_tensor(name, shape, dt))

        def sem(name):
            return ctx.enter_context(nc.semaphore(name))

        w_raw = sb("weight_raw", [P, SBUF2, SLAB])
        w_hi = sb("weight_hi", [P, SBUF2, SLAB], F32R)
        w_lo = sb("weight_lo", [P, SBUF2, SLAB], F32R)
        slots = sb("slots", [P, 64, T])
        x_t = sb("residual_t", [P, KD, T])
        a_hi = sb("operand_hi", [P, KD, T], F32R)
        a_lo = sb("operand_lo", [P, KD, T], F32R)
        work = sb("work", [P, 8192])
        norm_ws = sb("norm_ws", [P, 2048])
        ident = sb("ident", [P, P])
        ones = sb("ones", [P, P])
        params = sb("params", [P, 512])
        lam_f = sb("lam_f", [P, 4, PAIRS])
        powers = sb("powers", [P, 2, CHUNK, PAIRS])
        small = sb("small", [P, 64])
        pick_stage = sb("pick_stage", [P, 8], U32)
        ps = ctx.enter_context(nc.psum_tensor("ps", [P, 8, 512], F32))

        slots_f = slots[:, :, :].rearrange("p a b -> p (a b)")
        x_f = x_t[:, :, :].rearrange("p a b -> p (a b)")
        h_t = slots[:, H0:H0 + KD, :]

        def slot(s, n=1):
            if isinstance(s, int):
                return slots_f[:, s * T:(s + n) * T]
            return slots_f[:, bass.ds(s * T, n * T)]

        sdev, rstd = norm_ws[:, 0:512], norm_ws[:, 512:1024]
        sq_acc = norm_ws[:, 256:512]
        sq = norm_ws[:, 1024:2048].rearrange("p (a b) -> p a b", a=SQ)
        eps_c, ln_eps_c = small[:, 0:1], small[:, 1:2]
        att_nmax, att_max, att_sum, att_rsum = small[:, 2:4], small[:, 4:6], small[:, 6:8], small[:, 8:10]
        out_ss, out_sd, out_rs = small[:, 10:12], small[:, 12:14], small[:, 14:16]
        head_max, head_sum, head_rs = small[:, 16:24], small[:, 24:32], small[:, 32:40]

        x_tok0 = work[:, 0:4096].rearrange("p (a b) -> p a b", a=TT)
        att_qk, att_v = work[:, 0:512], work[:, 512:768]
        att_vtok = work[:, 768:1024].rearrange("p (a b) -> p a b", a=2)
        att_s, att_p, att_pt = work[:, 1024:1408], work[:, 1408:1792], work[:, 1792:2176]
        b_nat = work[:, 2176:3200].rearrange("p (c r h) -> p c r h", c=2, r=PAIRS)
        mask = work[:, 3200:3584]
        b_diag = work[:, 4096:6144].rearrange("p (c r h) -> p c r h", c=2, r=PAIRS)
        c_diag = work[:, 6144:8192].rearrange("p (c a b) -> p c a b", c=2, a=KH)
        xs = work[:, :].rearrange("p (c r t) -> p c r t", c=2, r=HPAIRS)
        xs_j = work[:, :].rearrange("p (a j) -> p a j", j=CHUNK)
        xs_cj = work[:, :].rearrange("p (a k j) -> p a k j", k=CHUNKS, j=CHUNK)
        glu_pad = work[:, 0:KH * (T + TAPS2 - 1)].rearrange("p (a b) -> p a b", a=KH)
        h_tok = work[:, 0:4096].rearrange("p (a b) -> p a b", a=TT)
        y_tok = work[:, 4096:8192].rearrange("p (a b) -> p a b", a=TT)
        vec = slots_f[:, 60 * T:62 * T].rearrange("p (a b) -> p a b", a=4)
        bt = slots_f[:, 56 * T:64 * T].rearrange("p (c a b) -> p c a b", c=2, a=KH)
        ct = slots_f[:, 48 * T:56 * T].rearrange("p (c a b) -> p c a b", c=2, a=KH)
        subk = slots_f[:, SUBK0 * T:(SUBK0 + 8) * T].rearrange("p (a b) -> p a b", a=16)
        subt = slots_f[:, SUBT0 * T:(SUBT0 + 8) * T].rearrange("p (a b) -> p a b", a=16)
        key_s = x_f.rearrange("p (t a b) -> p t a b", t=TT, a=16)
        diag = x_f[:, 0:2048].rearrange("p (a b) -> p a b", a=16)
        gain_b = x_f[:, 2048:4096]
        tk = slots_f[:, TOPK0 * T:64 * T]
        tk_s, tk_if = tk[:, 0:256], tk[:, 256:512]
        tk_iu = tk[:, 512:768].bitcast(U32)
        tk_cand, tk_best = tk[:, 768:1024], tk[:, 1024:1152]
        tk_pos, tk_hi, tk_lo = (tk[:, 1152 + 128 * n:1280 + 128 * n].bitcast(U32) for n in range(3))
        tk_hif, tk_lof, tk_e1, tk_e2 = (tk[:, 1536 + 128 * n:1664 + 128 * n] for n in range(4))
        picks = tk[:, 2048:2304].bitcast(U32)
        gates, dots, pick_w = tk[:, 2304:2560], tk[:, 2560:2816], tk[:, 2816:3072]
        iota16 = tk[:, 3072:3088]
        zero_row = tk[:, 3088:3600]
        onehot = norm_ws[:, :]
        rows = [w_raw[:, n, :] for n in range(SBUF2)] + [slots_f[:, n * D:(n + 1) * D] for n in range(6)]
        ROWS = len(rows)
        ROUNDS = PICKS // ROWS
        PE_ROWS = 5

        ps_p = ps[:, 0:PSLOTS, 0:T]
        ps_m = ps[:, 2:4, :]
        ps_n, ps_s, ps_pt, ps_o = ps[:, 4, :], ps[:, 5, 0:384], ps[:, 6, 0:384], ps[:, 7, 0:T]
        ps_v = ps[:, 0:4, :]

        x_in = [sem(f"x_in{t}") for t in range(TT)]
        raw_landed = [sem(f"raw_landed{b}") for b in range(SBUF2)]
        hi_ready, lo_ready = sem("hi_ready"), sem("lo_ready")
        a_hi_ready, a_lo_ready = sem("a_hi_ready"), sem("a_lo_ready")
        vec_in, ssm_in, b_in, c_in, subk_in, gain_in = (sem(n) for n in ("vec_in", "ssm_in", "b_in", "c_in", "subk_in", "gain_in"))
        consts_ready, cdiag_cleared, mask_ready = sem("consts_ready"), sem("cdiag_cleared"), sem("mask_ready")
        consts_set, mask_set = sem("consts_set"), sem("mask_set")
        eps_ready = sem("eps_ready")
        proj_done, proj_freed = sem("proj_done"), sem("proj_freed")
        misc_done, misc_freed = sem("misc_done"), sem("misc_freed")
        squared, sq_summed, acc_summed = sem("squared"), sem("sq_summed"), sem("acc_summed")
        rooted, rstd_ready, h_scaled = sem("rooted"), sem("rstd_ready"), sem("h_scaled")
        dve_step = sem("dve_step")
        ssm_coef, bdiag_ready, powers_ready = sem("ssm_coef"), sem("bdiag_ready"), sem("powers_ready")
        head_squared, head_summed, qk_ready, v_copied, v_turned, v_ready = (
            sem(n) for n in ("head_squared", "head_summed", "qk_ready", "v_copied", "v_turned", "v_ready"))
        scores_done, nmax_ready, exp_ready, probs_ready, probs_turned, pt_ready, out_done, out_ready = (
            sem(n) for n in ("scores_done", "nmax_ready", "exp_ready", "probs_ready", "probs_turned", "pt_ready",
                             "out_done", "out_ready"))
        za_silu, yconv_raw, y_final = sem("za_silu"), sem("yconv_raw"), sem("y_final")
        scanned, ssm_sum, z_ready, glu_ready, conv_done, centred, ln_scaled, conv_act = (
            sem(n) for n in ("scanned", "ssm_sum", "z_ready", "glu_ready", "conv_done", "centred", "ln_scaled", "conv_act"))
        val_gated, merged = sem("val_gated"), sem("merged")
        picks_ready, best_ready, best_exp, dots_ready, gelu_ready, w_ready, diag_ready = (
            sem(n) for n in ("picks_ready", "best_ready", "best_exp", "dots_ready", "gelu_ready", "w_ready", "diag_ready"))
        staged, zero_ready = [sem(f"staged{half}") for half in range(2)], sem("zero_ready")
        gathered = [sem(f"gathered{n}") for n in range(ROWS)]
        row_free = [sem(f"row_free{n}") for n in range(ROWS)]
        v_summed, v_read, y_ready, out_squared, out_rooted, normed, stored = (
            sem(n) for n in ("v_summed", "v_read", "y_ready", "out_squared", "out_rooted", "normed", "stored"))

        def freed(n):
            return n + PSLOTS

        M_X = 0
        M_VEC = M_X + 8
        M_LAM = M_VEC + 1
        M_BC = M_LAM + 1
        M_BU = [M_BC + 8, M_BC + 8 + 20]
        M_CY = [M_BU[0] + 16, M_BU[1] + 16]
        M_SUB = M_CY[1] + 4
        M_TOK = M_SUB + 4
        M_S = M_TOK + 16

        block = ctx.enter_context(nc.Block())

        @block.sync
        def _(sp):
            for t in range(TT):
                sp.dma_start(x_tok0[:, t, :], d["x"][0, t * P:(t + 1) * P, :]).then_inc(x_in[t], 16)
            w_in = d["w_in"][0].rearrange("(k p) n -> p k n", p=P)
            w_out = d["w_out"][0].rearrange("(k p) n -> p k n", p=P)
            w_in2 = d["w_in_2"][0].rearrange("(k p) n -> p k n", p=P)
            w_val = d["ssm_w_val_2"][0].rearrange("(k p) n -> p k n", p=P)
            w_gate = d["ssm_w_gate_2"][0].rearrange("(k p) n -> p k n", p=P)
            w_cv = d["conv_w_out_2"][0].rearrange("(k p) n -> p k n", p=P)
            w_out2 = d["w_out_2"][0].rearrange("(k p) n -> p k n", p=P)
            w_q = d["peer_w_q_2"][0].rearrange("(k p) n -> p k n", p=P)

            def load(b, w, col, n, used):
                if used is not None:
                    sp.wait_ge(lo_ready, used)
                src = w[:, :, col:col + n] if isinstance(col, int) else w[:, :, bass.ds(col, n)]
                sp.dma_start(w_raw[:, b, :].rearrange("p (k n) -> p k n", n=n), src).then_inc(raw_landed[b], 16)

            def load_pairs(w, slab0, first, last, col0, n=P):
                with sp.Fori((slab0 + first) // 2, (slab0 + last) // 2) as j:
                    for b in range(2):
                        load(b, w, j * (2 * n) + (col0 + n * (b - slab0)), n, j * 4 + (2 * b - 2))

            for b in range(2):
                load(b, w_in, 4 * HALF + P * b, P, None)
            load_pairs(w_in, SLAB_IN, 2, 32, 4 * HALF)
            load_pairs(w_in, SLAB_IN, 32, 64, -4 * HALF)
            load_pairs(w_out, SLAB_OUT, 0, 16, 0)
            load_pairs(w_in2, SLAB_IN2, 0, 8, 2 * HALF)
            load_pairs(w_in2, SLAB_IN2, 8, 24, -KH * P)
            load_pairs(w_in2, SLAB_IN2, 24, 56, 0)
            with sp.Fori(0, 4) as g:
                for m, w in enumerate((w_val, w_gate)):
                    for b in range(2):
                        load(b, w, g * 512 + 256 * b, 256, g * 8 + 2 * (SLAB_VG + 2 * m + b - 1))
            load_pairs(w_cv, SLAB_CV, 0, 8, 0, 256)
            load_pairs(w_out2, SLAB_OUT2, 0, 4, 0)
            sp.wait_ge(merged, KD)
            sp.dma_start(subk, d["peer_sub_keys_2"][0].rearrange("h c n e -> n (h c) e")).then_inc(subk_in, 16)
            load_pairs(w_out2, SLAB_OUT2, 4, 16, 0)
            load_pairs(w_q, SLAB_WQ, 0, 16, 0)
            sp.wait_ge(picks_ready, len(HEAD_PARTS) + 1)
            sp.dma_start(gain_b, d["norm_final_2"].partition_broadcast(P)).then_inc(gain_in, 16)
            for t in range(TT):
                for half in range(2):
                    cols = slice(half * HALF, (half + 1) * HALF)
                    sp.wait_ge(normed, 2 * t + half + 1)
                    sp.dma_start(d["out"][0, t * P:(t + 1) * P, cols], y_tok[:, t, cols]).then_inc(stored, 16)
            sp.wait_ge(stored, 16 * 2 * TT)

        @block.gpsimd
        def _(pool):
            nc.gpsimd.memset(ident[:, :], 0.0).then_inc(consts_set, 1)
            nc.gpsimd.memset(ones[:, :], 1.0).then_inc(consts_ready, 1)
            pool.wait_ge(consts_set, 1)
            nc.gpsimd.affine_select(out=ident[:, :], in_=ident[:, :], compare_op=ALU.not_equal, fill=1.0, base=0,
                                    pattern=[[-1, P]], channel_multiplier=1).then_inc(consts_ready, 1)
            nc.gpsimd.memset(c_diag, 0.0).then_inc(cdiag_cleared, 1)

            def low_parts(first, last):
                with pool.Fori(first // 2, last // 2) as j:
                    for b in range(2):
                        for half in range(2):
                            at = slice(half * SLAB // 2, (half + 1) * SLAB // 2)
                            pool.wait_ge(hi_ready, j * 4 + (2 * b + half + 1))
                            nc.gpsimd.tensor_tensor(w_lo[:, b, at], w_raw[:, b, at], w_hi[:, b, at].bitcast(F32),
                                                    ALU.subtract).then_inc(lo_ready, 1)

            low_parts(0, 4)
            pool.wait_ge(misc_done, M_X + 8)
            nc.gpsimd.memset(mask, 0.0).then_inc(mask_set, 1)
            pool.wait_ge(mask_set, 1)
            for lo in (0, 2 * P):
                nc.gpsimd.affine_select(out=mask[:, lo:lo + P], in_=mask[:, lo:lo + P], compare_op=ALU.is_ge,
                                        fill=-3.0e38, base=0, pattern=[[-1, P]],
                                        channel_multiplier=1).then_inc(mask_ready, 1)

            low_parts(4, SLAB_WQ)
            pool.wait_ge(merged, KD)
            nc.gpsimd.iota(iota16, pattern=[[1, 16]], base=0, channel_multiplier=0,
                           allow_small_or_imprecise_dtypes=True).then_inc(zero_ready, 1)
            nc.gpsimd.memset(zero_row, 0.0).then_inc(zero_ready, 1)
            low_parts(SLAB_WQ, SLABS)

            def gather(rnd, col0, ready, table):
                for half in range(2):
                    mine = range(half * ROWS // 2, (half + 1) * ROWS // 2)
                    for n in mine:
                        pool.wait_ge(row_free[n], rnd + 1)
                    nc.gpsimd.tensor_copy(pick_stage[:, mine[0]:mine[-1] + 1],
                                          picks[:, bass.ds(col0 + mine[0], len(mine))]).then_inc(staged[half], 1)
                    pool.wait_ge(picks_ready, ready)
                    pool.wait_ge(staged[half], rnd + 1)
                    for n in mine:
                        nc.gpsimd.indirect_dma_start(
                            rows[n], None, table, bass.IndirectOffsetOnAxis(ap=pick_stage[:, n:n + 1], axis=0),
                        ).then_inc(gathered[n], 16)

            for n in range(ROWS):
                pool.sem_inc(row_free[n], 1)
            pool.wait_ge(misc_done, M_S + PEER_H)
            pool.wait_ge(lo_ready, 2 * SLABS)
            per_head = PEER_K // ROWS
            for t in range(TT):
                for v, table in ((0, d["peer_u_2"][0]), (1, d["peer_v_2"][0])):
                    parts = [(*heads, n + 1) for n, heads in enumerate(HEAD_PARTS)] if t == v == 0 \
                        else [(0, PEER_H, len(HEAD_PARTS) + t)]
                    for first, last, ready in parts:
                        pool.wait_ge(picks_ready, ready)
                        with pool.Fori(first * per_head, last * per_head) as i:
                            gather(i + (2 * t + v) * ROUNDS, i * ROWS + t * PICKS, ready, table)

        @block.tensor
        def _(pe):
            def tile(slab0, tile0, t, kts, k0=0, order=None, ready=None):
                per = SLAB // kts // P
                b, n = (t // per) % SBUF2, t % per
                if n == 0:
                    pe.wait_ge(hi_ready, slab0 * 2 + (2 * (t // per) + 2))
                pe.wait_ge(proj_freed, tile0 + (t + 1))
                hi, lo = (w[:, b, :].rearrange("p (k n) -> p k n", k=kts)[:, :, n * P:(n + 1) * P] for w in (w_hi, w_lo))
                out = ps_p[:, t % PSLOTS, :]
                order = list(range(kts)) if order is None else order
                for k in order:
                    if ready is not None:
                        pe.wait_ge(a_lo_ready, ready(k) + 1)
                    nc.tensor.matmul(out, hi[:, k, :], a_hi[:, k0 + k, :], start=(k == order[0]), stop=False)
                    nc.tensor.matmul(out, hi[:, k, :], a_lo[:, k0 + k, :], start=False, stop=False)
                if n == 0:
                    pe.wait_ge(lo_ready, slab0 * 2 + (2 * (t // per) + 2))
                for k in order:
                    mm = nc.tensor.matmul(out, lo[:, k, :], a_hi[:, k0 + k, :], start=False, stop=(k == order[-1]))
                mm.then_inc(proj_done, 1)

            def misc_bank(m, first):
                pe.wait_ge(misc_freed, m if first else m - 1)
                return ps_m[:, m % 2, :]

            def sum_square(n, count, q0, r):
                if n == 0 and r > 1:
                    pe.wait_ge(rooted, r - 1)
                pe.wait_ge(squared, q0 + n + 1)
                nc.tensor.matmul(ps_n[:, 0:T], ones[:, :], sq[:, n % SQ, :], start=(n == 0),
                                 stop=(n == count - 1), skip_group_check=True).then_inc(sq_summed, 1)

            def sum_residual(q0, r):
                pe.wait_ge(rooted, r - 1)
                pe.wait_ge(sq_summed, q0 + KD)
                nc.tensor.matmul(ps_n[:, 0:T], ones[:, :], sq_acc, start=True, stop=True).then_inc(acc_summed, 1)

            pe.wait_ge(consts_ready, 2)
            for g in range(4):
                for t in range(TT):
                    m = M_X + TT * g + t
                    if g == 0:
                        pe.wait_ge(x_in[t], 16)
                    bank = misc_bank(m, m == 0) if m >= 2 else ps_m[:, m % 2, :]
                    for j in range(4):
                        k = 4 * g + j
                        tr = nc.tensor.transpose(bank[:, j * P:(j + 1) * P], x_tok0[:, t, k * P:(k + 1) * P], ident[:, :])
                    tr.then_inc(misc_done, 1)
            pe.wait_ge(vec_in, 16 * 14)
            bank = misc_bank(M_VEC, True)
            for j, n in enumerate((90, 64, 124, 124)):
                tr = nc.tensor.transpose(bank[:, j * P:j * P + n], vec[0:n, j, :], ident[0:n, 0:n])
            tr.then_inc(misc_done, 1)
            for n in range(KD):
                sum_square(n, KD, 0, 1)

            with pe.Fori(0, 3) as i:
                for t in range(8):
                    tile(i * 8, i * 8, t, KD, ready=(lambda k: G_IN + k // 2) if t == 0 else None)
            pe.wait_ge(ssm_coef, 1)
            bank = misc_bank(M_LAM, True)
            for j in range(4):
                tr = nc.tensor.transpose(bank[:, j * P:j * P + PAIRS], slot(56 + j // 2)[0:PAIRS, (j % 2) * P:(j % 2 + 1) * P],
                                         ident[0:PAIRS, 0:PAIRS])
            tr.then_inc(misc_done, 1)

            with pe.Fori(0, 4) as i:
                for e in range(2):
                    head = i * 2 + e
                    pe.wait_ge(rooted, head + 1)
                    pe.wait_ge(head_squared, head * 2 + 2)
                    nc.tensor.matmul(ps_n, ones[:, :], norm_ws[:, 1024:1536], start=True, stop=True).then_inc(head_summed, 1)
                    for t in range(2):
                        tile(i * 8 + 24, i * 8 + 24, 4 * e + t, KD)
                    pe.wait_ge(v_copied, head + 1)
                    pe.wait_ge(out_ready, head + 1)
                    for j in range(2):
                        tr = nc.tensor.transpose(ps_o[:, j * P:(j + 1) * P], att_v[:, j * P:(j + 1) * P], ident[:, :])
                    tr.then_inc(v_turned, 1)
                    pe.wait_ge(qk_ready, head * 2 + 2)
                    nc.tensor.matmul(ps_s[:, 0:P], att_qk[:, 0:P], att_qk[:, T:T + P], start=True, stop=True)
                    nc.tensor.matmul(ps_s[:, P:3 * P], att_qk[:, P:T], att_qk[:, T:2 * T], start=True,
                                     stop=True).then_inc(scores_done, 1)
                    tile(i * 8 + 24, i * 8 + 24, 4 * e + 2, KD)
                    pe.wait_ge(probs_ready, head * 2 + 2)
                    for j in range(3):
                        tr = nc.tensor.transpose(ps_pt[:, j * P:(j + 1) * P], att_p[:, j * P:(j + 1) * P], ident[:, :])
                    tr.then_inc(probs_turned, 1)
                    tile(i * 8 + 24, i * 8 + 24, 4 * e + 3, KD)
                    pe.wait_ge(pt_ready, head + 1)
                    pe.wait_ge(v_ready, head + 1)
                    nc.tensor.matmul(ps_o, att_vtok[:, 0, :], att_pt[:, 0:T], start=True, stop=False)
                    nc.tensor.matmul(ps_o[:, P:T], att_vtok[:, 1, :], att_pt[:, T:T + P], start=False,
                                     stop=True).then_inc(out_done, 1)

            for t in range(8):
                tile(56, 56, t, KD)
                for n in range(4):
                    if t < 2:
                        sum_square(4 * t + n, KH, 16, 10)
                    elif t in (4, 5):
                        sum_square(4 * (t - 4) + n, KH, 24, 11)

            for t in range(16):
                if t == 0:
                    pe.wait_ge(proj_freed, freed(TILE_OUT))
                tile(SLAB_OUT, TILE_OUT, t, KD, order=[*range(KH, KD), *range(KH)],
                     ready=(lambda k: G_MIX + (k // 4 + 2) % 4) if t == 0 else None)
                if t == 4:
                    pe.wait_ge(bdiag_ready, 1)
                    pe.wait_ge(c_in, 16 * 16)
                for u in range(2 * (t - 4), 2 * (t - 3)) if 4 <= t < 8 else ():
                    bank = misc_bank(M_BC + u, u == 0)
                    c, half = (u // 2) % 2, u % 2
                    for j in range(4):
                        a = 4 * half + j
                        src = b_diag[:, c, 4 * a:4 * a + 4, :].rearrange("p r h -> p (r h)") if u < 4 else c_diag[:, c, a, :]
                        tr = nc.tensor.transpose(bank[:, j * P:(j + 1) * P], src, ident[:, :])
                    tr.then_inc(misc_done, 1)
            sum_residual(32, 12)

            pe.wait_ge(proj_freed, freed(TILE_IN2))
            for t in range(8):
                tile(SLAB_IN2, TILE_IN2, t, KD, ready=(lambda k: G_IN2 + k // 2) if t == 0 else None)

            def ssm_inputs(half):
                pe.wait_ge(proj_freed, freed(TILE_IN2 + 8))
                for n in range(HPAIRS):
                    pr = HPAIRS * half + n
                    a, j = pr // 4, pr % 4
                    bank = misc_bank(M_BU[half] + n, n == 0)
                    for c in range(2):
                        mm = nc.tensor.matmul(bank[:, c * T:(c + 1) * T], bt[32 * j:32 * j + 32, c, a, :],
                                              slot(SSM0 + a)[32 * j:32 * j + 32, :], start=True, stop=True)
                    mm.then_inc(misc_done, 1)

            def ssm_outputs(half):
                pe.wait_ge(scanned, half + 1)
                for n in range(4):
                    a = 4 * half + n
                    bank = misc_bank(M_CY[half] + n, n == 0)
                    for j in range(4):
                        for c in range(2):
                            mm = nc.tensor.matmul(bank[32 * j:32 * j + 32, 0:T], ct[:, c, a, 32 * j:32 * j + 32],
                                                  xs[:, c, 4 * n + j, :], start=(c == 0), stop=(c == 1))
                    mm.then_inc(misc_done, 1)

            pe.wait_ge(misc_freed, M_BC + 8)
            ssm_inputs(0)

            def rounds(first, last):
                with pe.Fori(first, last) as i:
                    for t in range(4):
                        tile(i * 4 + SLAB_IN2, i * 4 + TILE_IN2, t, KD)

            rounds(2, 7)
            ssm_outputs(0)
            ssm_inputs(1)
            rounds(7, 12)
            ssm_outputs(1)
            rounds(12, 14)

            for t in range(32):
                tile(SLAB_VG, TILE_VG, t, KH, ready=(lambda k: G_Z + k // 4) if t == 0 else None)
                if t == LN_MEAN:
                    pe.wait_ge(conv_done, 1)
                    pe.wait_ge(rooted, 12)
                    for n in range(KH):
                        mm = nc.tensor.matmul(ps_n[:, 0:T], ones[:, :], slot(CONV0 + n), start=(n == 0), stop=(n == KH - 1))
                    mm.then_inc(centred, 1)
                if t == LN_VAR:
                    for n in range(KH):
                        sum_square(n, KH, 48, 14)

            pe.wait_ge(proj_freed, freed(TILE_CV))
            for t in range(16):
                tile(SLAB_CV, TILE_CV, t, KH, k0=KH, ready=(lambda k: G_CV + k // 2) if t == 0 else None)

            for t in range(16):
                tile(SLAB_OUT2, TILE_OUT2, t, KD, ready=(lambda k: G_MERGE + k // 2) if t == 0 else None)
                if 11 <= t < 15:
                    u = t - 11
                    if u == 0:
                        pe.wait_ge(subk_in, 16)
                    bank = misc_bank(M_SUB + u, u == 0)
                    for j in range(4):
                        tr = nc.tensor.transpose(bank[:, j * P:(j + 1) * P], subk[:, 4 * u + j, :], ident[:, :])
                    tr.then_inc(misc_done, 1)
            sum_residual(56, 15)

            def head_scores(h):
                pe.wait_ge(proj_freed, freed(TILE_WQ + 2 * h + 2))
                bank = misc_bank(M_S + h, h == 0)
                for t in range(TT):
                    for c in range(2):
                        mm = nc.tensor.matmul(bank[:, (2 * t + c) * P:(2 * t + c + 1) * P],
                                              slot(2 * h + c)[:, t * P:(t + 1) * P], subt[:, 2 * h + c, :], start=True, stop=True)
                mm.then_inc(misc_done, 1)

            pe.wait_ge(proj_freed, freed(TILE_WQ))
            for n in range(16):
                tile(SLAB_WQ, TILE_WQ, n, KD, ready=(lambda k: G_Q + k // 2) if n == 0 else None)
                for u in range(4 * n, 4 * n + 4 if n < 4 else 4 * n):
                    bank = misc_bank(M_TOK + u, u == 0)
                    src, t, g = (x_t, h_t)[u // 8], (u // 4) % 2, u % 4
                    for j in range(4):
                        tr = nc.tensor.transpose(bank[:, j * P:(j + 1) * P], src[:, 4 * g + j, t * P:(t + 1) * P], ident[:, :])
                    tr.then_inc(misc_done, 1)
                if n in SCORE_AFTER:
                    head_scores(SCORE_AFTER.index(n))

            pe.wait_ge(zero_ready, 2)
            pe.wait_ge(misc_freed, M_S + 8)
            for t in range(TT):
                if t > 0:
                    pe.wait_ge(v_read, t)
                for c in range(4):
                    nc.tensor.matmul(ps_v[:, c, :], zero_row[:, 0:P], zero_row, start=True, stop=False, skip_group_check=True)
                with pe.Fori(0, ROUNDS) as i:
                    for n in range(PE_ROWS):
                        pe.wait_ge(diag_ready, i * PE_ROWS + (ROUNDS * PE_ROWS * t + n + 1))
                        pe.wait_ge(gathered[n], (i + ((2 * t + 1) * ROUNDS + 1)) * 16)
                        for c in range(4):
                            mm = nc.tensor.matmul(ps_v[:, c, :], diag[:, n, :], rows[n][:, c * 512:(c + 1) * 512],
                                                  start=False, stop=False, skip_group_check=True)
                        mm.then_inc(row_free[n], 1)
                for c in range(4):
                    mm = nc.tensor.matmul(ps_v[:, c, 0:8], zero_row[:, 0:P], zero_row[:, 0:8], start=False, stop=True,
                                          skip_group_check=True)
                mm.then_inc(v_summed, 1)

        @block.scalar
        def _(act):
            def act_copy(dst, src):
                return nc.scalar.activation(dst, src, ACT.Copy)

            def row(j, r, src, n):
                act.dma_start(vec[r:r + n, j, :], src).then_inc(vec_in, 16)

            def rows_of(name, pat="(k p) -> k p"):
                return d[name][0].rearrange(pat, p=P)

            row(0, C_NORM, rows_of("norm_gain"), KD)
            row(0, C_MIX, rows_of("norm_mix_2"), KD)
            row(0, C_FFN, rows_of("norm_ffn_2"), KD)
            row(0, C_COUT, rows_of("conv_out_gain"), KH)
            row(0, C_AOUT, rows_of("attn_out_gain"), KH)
            row(0, C_CONV, rows_of("conv_w", "t (k p) -> (t k) p"), 3 * KH)
            row(0, C_QG, d["q_norm_gain"], 1)
            row(0, C_KG, d["k_norm_gain"], 1)
            row(1, 0, rows_of("b_gate_2"), 32)
            row(1, 32, rows_of("conv_b_dw_2"), KH)
            row(1, 40, rows_of("conv_ln_g_2"), KH)
            row(1, 48, rows_of("conv_ln_b_2"), KH)
            row(1, 56, rows_of("ssm_d_2"), KH)
            taps = rows_of("conv_w_dw_2", "t (k p) -> (t k) p")
            act.dma_start(vec[0:124, 2:4, :], taps.rearrange("(j r) p -> r j p", j=2)).then_inc(vec_in, 16)
            act.dma_start(slot(59)[0:PAIRS, 0:P], d["ssm_a_re_2"][0].rearrange("(r s) p -> r (s p)", s=2)).then_inc(ssm_in, 16)
            act.dma_start(slot(59)[0:PAIRS, P:T], d["ssm_a_im_2"][0].rearrange("(r s) p -> r (s p)", s=2)).then_inc(ssm_in, 16)
            act.dma_start(slot(62)[0:PAIRS, 0:2], d["ssm_log_dt_2"][0].rearrange("(r s) -> r s", s=2)).then_inc(ssm_in, 16)
            act.wait_ge(eps_ready, 2)

            def square(n, q0, src):
                if q0 + n >= SQ:
                    act.wait_ge(sq_summed, q0 if n < SQ else q0 + n - SQ + 1)
                nc.scalar.activation(sq[:, n % SQ, :], src, ACT.Square).then_inc(squared, 1)

            def root(r, q_end, width, eps=eps_c, summed=sq_summed):
                act.wait_ge(summed, q_end)
                if r > 1:
                    act.wait_ge(rstd_ready, r - 1)
                nc.scalar.activation(sdev[:, 0:T], ps_n[:, 0:T], ACT.Sqrt, bias=eps, scale=1.0 / width).then_inc(rooted, 1)

            def read_out(tile0, n, dst, func=ACT.Copy, **kw):
                act.wait_ge(proj_done, tile0 + (n + 1))
                return nc.scalar.activation(dst, ps_p[:, n % PSLOTS, :], func, **kw).then_inc(proj_freed, 1)

            def high_part(slab, b, done=None):
                if done is not None:
                    act.wait_ge(proj_done, done)
                act.wait_ge(raw_landed[b], slab * 8 + (16 - 8 * b))
                for half in range(2):
                    at = slice(half * SLAB // 2, (half + 1) * SLAB // 2)
                    act_copy(w_hi[:, b, at], w_raw[:, b, at]).then_inc(hi_ready, 1)

            def next_high(slab0, tile0, n):
                per = 2 if isinstance(slab0, int) and SLAB_VG <= slab0 < SLAB_OUT2 else 1
                if not (isinstance(slab0, int) and slab0 + n // per + 2 >= SLABS):
                    high_part(slab0 + (n // per + 2), (n // per) % SBUF2, tile0 + (n + 1))

            def operand_high(k, src, n=2):
                act_copy(a_hi[:, k:k + n, :], src).then_inc(a_hi_ready, 1)

            def normed_high(q0):
                for g in range(KD // 2):
                    act.wait_ge(h_scaled, q0 + 2 * g + 2)
                    operand_high(2 * g, h_t[:, 2 * g:2 * g + 2, :])

            for n in range(KD):
                act.wait_ge(misc_freed, M_X + TT * (n // 4 + 1))
                square(n, 0, x_t[:, n, :])
            root(1, KD, D)
            high_part(0, 0)
            normed_high(0)
            high_part(1, 1)
            act.wait_ge(cdiag_cleared, 1)
            for c, name in enumerate(("ssm_c_re_2", "ssm_c_im_2")):
                src = d[name][0].rearrange("(a g) h p -> g h a p", g=8)
                for g in range(8):
                    act.dma_start(c_diag[GCH * g:GCH * g + GCH, c, :, STATE * (g % 2):STATE * (g % 2) + STATE],
                                  src[g]).then_inc(c_in, 16)
            act.wait_ge(misc_done, M_X + 8)
            for c, name in enumerate(("ssm_b_re_2", "ssm_b_im_2")):
                act.dma_start(b_nat[:, c, :, :], d[name][0].rearrange("(r s) p h -> (s p) r h", s=2)).then_inc(b_in, 16)

            with act.Fori(0, 3) as i:
                for t in range(8):
                    next_high(i * 8, i * 8, t)
                    read_out(i * 8, t, slot(i * 8 + t))
            act.wait_ge(proj_freed, freed(24))

            def head_inputs(head):
                act.wait_ge(sq_summed, KD)
                nc.scalar.activation(sq[:, 0, :], slot(head + Q0), ACT.Square).then_inc(head_squared, 1)
                nc.scalar.activation(sq[:, 1, :], slot(head + K0), ACT.Square).then_inc(head_squared, 1)
                act_copy(att_v, slot(head + V0)).then_inc(v_copied, 1)

            def two_heads(i, last):
                for e in range(2):
                    head = i * 2 + e
                    act.wait_ge(head_summed, head + 1)
                    act.wait_ge(rstd_ready, head + 1)
                    nc.scalar.activation(sdev, ps_n, ACT.Sqrt, bias=eps_c, scale=1.0 / HEAD_DIM).then_inc(rooted, 1)
                    for t in range(4 * e, 4 * e + 2):
                        next_high(i * 8 + 24, i * 8 + 24, t)
                        read_out(i * 8 + 24, t, slot(i * 8 + (24 + t)))
                    for j, (lo, hi) in enumerate(((0, P), (P, 3 * P))):
                        act.wait_ge(nmax_ready, head + 1)
                        nc.scalar.activation(att_p[:, lo:hi], att_s[:, lo:hi], ACT.Exp, bias=att_nmax[:, j:j + 1],
                                             scale=HEAD_DIM ** -0.5, accum_out=att_sum[:, j:j + 1]).then_inc(exp_ready, 1)
                    next_high(i * 8 + 24, i * 8 + 24, 4 * e + 2)
                    read_out(i * 8 + 24, 4 * e + 2, slot(i * 8 + (26 + 4 * e)))
                    act.wait_ge(probs_turned, head + 1)
                    act_copy(att_pt, ps_pt).then_inc(pt_ready, 1)
                    if not (last and e == 1):
                        head_inputs(head + 1)
                    next_high(i * 8 + 24, i * 8 + 24, 4 * e + 3)
                    read_out(i * 8 + 24, 4 * e + 3, slot(i * 8 + (27 + 4 * e)))
                    act.wait_ge(proj_freed, freed(24))
                    act.wait_ge(out_done, head + 1)
                    act_copy(slot(head + Q0), ps_o).then_inc(out_ready, 1)

            head_inputs(0)
            with act.Fori(0, HEADS // 2 - 1) as i:
                two_heads(i, False)
            two_heads(HEADS // 2 - 1, True)
            act.wait_ge(proj_freed, freed(32))
            act.wait_ge(out_ready, HEADS + 1)
            for t in range(8):
                if t == 4:
                    act.wait_ge(yconv_raw, 1)
                for n in range(4):
                    if t < 2:
                        square(4 * t + n, 16, slot(Q0 + 4 * t + n))
                    elif t in (4, 5):
                        square(4 * (t - 4) + n, 24, slot(HC0 + 4 * (t - 4) + n))
                next_high(56, 56, t)
                read_out(56, t, slot(ZC0 + t), ACT.Silu)
                if t == 1:
                    root(10, 24, HALF)
                elif t == 2:
                    nc.scalar.activation(slot(ZA0, KH), slot(ZA0, KH), ACT.Silu).then_inc(za_silu, 1)
                elif t == 5:
                    root(11, 32, HALF)
            act.wait_ge(proj_done, TILE_OUT)
            for s0, k, done in MIX:
                act.wait_ge(y_final, done)
                operand_high(k, slots[:, s0:s0 + 4, :], 4)

            def out_squares(slab0, tile0, q0, first, per, first_bank, bank_out):
                for n in range(KD):
                    if n < KD - 1:
                        next_high(slab0, tile0, n)
                    else:
                        nc.scalar.activation(small[:, 52:53], eps_c, ACT.Sqrt)
                    act.wait_ge(proj_freed, freed(tile0 + n + 1))
                    square(n, q0, x_t[:, n, :])
                    for u in range(per * (n - first), per * (n - first + 1)) if first <= n < first + 4 else ():
                        act.wait_ge(misc_done, first_bank + u + 1)
                        dst, scale = bank_out(u)
                        nc.scalar.activation(dst, ps_m[:, (first_bank + u) % 2, :], ACT.Copy, scale=scale).then_inc(misc_freed, 1)

            def ssm_matrix(u):
                c, half = (u // 2) % 2, u % 2
                dst = (bt if u < 4 else ct)[:, c, 4 * half:4 * half + 4, :].rearrange("p a b -> p (a b)")
                return dst, (-1.0 if u >= 4 and c == 1 else 1.0)

            out_squares(SLAB_OUT, TILE_OUT, 32, 4, 2, M_BC, ssm_matrix)
            root(12, 1, D, summed=acc_summed)
            next_high(SLAB_OUT, TILE_OUT, KD - 1)
            normed_high(KD)

            for t in range(8):
                next_high(SLAB_IN2, TILE_IN2, t)
                read_out(TILE_IN2, t, slot(SSM0 + t))

            def ssm_inputs(half):
                for n in range(HPAIRS):
                    m = M_BU[half] + n
                    act.wait_ge(misc_done, m + 1)
                    act_copy(xs[:, :, n, :], ps_m[:, m % 2, :].rearrange("p (c t) -> p c t", c=2)).then_inc(misc_freed, 1)

            def ssm_gelu(half):
                for n in range(4):
                    act.wait_ge(ssm_sum, 4 * half + n + 1)
                    nc.scalar.activation(slot(SSM0 + 4 * half + n), slot(SSM0 + 4 * half + n),
                                         ACT.Gelu_apprx_tanh).then_inc(z_ready, 1)

            ssm_inputs(0)
            for t in range(8):
                next_high(SLAB_IN2 + 8, TILE_IN2 + 8, t)
                read_out(TILE_IN2 + 8, t, slot(GLU0 + t))
            for t in range(8):
                next_high(SLAB_IN2 + 16, TILE_IN2 + 16, t)
                read_out(TILE_IN2 + 16, t, slot(SIG0 + t), ACT.Sigmoid)

            def gate_tiles(first, last):
                with act.Fori(first // 4, last // 4) as i:
                    for t in range(4):
                        next_high(i * 4 + (SLAB_IN2 + 24), i * 4 + (TILE_IN2 + 24), t)
                        read_out(i * 4 + (TILE_IN2 + 24), t, slot(i * 4 + (GA0 + t)), ACT.Sigmoid,
                                 bias=params[:, bass.ds(i * 4 + (C_GATE + t), 1)])

            gate_tiles(0, 4)
            ssm_inputs(1)
            ssm_gelu(0)
            gate_tiles(4, 24)
            ssm_gelu(1)
            gate_tiles(24, 32)
            act.wait_ge(z_ready, KH)
            for g in range(2):
                operand_high(4 * g, slots[:, SSM0 + 4 * g:SSM0 + 4 * g + 4, :], 4)

            for n in range(32):
                g, t = n // 8, n % 8
                if t == 0 and g > 1:
                    act.wait_ge(val_gated, g - 1)
                if n == 0:
                    act.wait_ge(glu_ready, 1)
                if n % 2:
                    next_high(SLAB_VG, TILE_VG, n)
                read_out(TILE_VG, n, slot(VAL0 * (1 - g % 2) + t), ACT.Copy if t < 4 else ACT.Sigmoid)
                if n == LN_MEAN:
                    act.wait_ge(centred, 1)
                    act.wait_ge(rstd_ready, 12)
                    nc.scalar.activation(sdev[:, 0:T], ps_n[:, 0:T], ACT.Copy, scale=1.0 / HALF).then_inc(rooted, 1)
                elif n == LN_VAR - 1:
                    act.wait_ge(centred, 2)
                    for k in range(KH):
                        square(k, 48, slot(CONV0 + k))
                elif n == LN_VAR:
                    root(14, 56, HALF, ln_eps_c)
                elif n == LN_OUT:
                    for k in range(KH):
                        act.wait_ge(ln_scaled, k + 1)
                        nc.scalar.activation(slot(CONV0 + k), slot(CONV0 + k), ACT.Silu,
                                             bias=params[:, C_LNB + k:C_LNB + k + 1]).then_inc(conv_act, 1)
                        if k % 2:
                            act.wait_ge(conv_act, k + 1)
                            operand_high(KH + k - 1, slots[:, CONV0 + k - 1:CONV0 + k + 1, :])
            for g in range(KD // 2):
                next_high(SLAB_CV, TILE_CV, 2 * g + 1)
                if g < KH // 2:
                    act.wait_ge(merged, 2 * g + 2)
                    operand_high(2 * g, slots[:, GA0 + 2 * g:GA0 + 2 * g + 2, :])
            for g in range(KH // 2, KD // 2):
                act.wait_ge(merged, 2 * g + 2)
                operand_high(2 * g, slots[:, GA0 + 2 * g:GA0 + 2 * g + 2, :])

            def keys_out(u):
                return subt[:, 4 * u:4 * u + 4, :].rearrange("p a b -> p (a b)"), 1.0

            out_squares(SLAB_OUT2, TILE_OUT2, 56, 11, 1, M_SUB, keys_out)
            root(15, 2, D, summed=acc_summed)
            next_high(SLAB_OUT2, TILE_OUT2, KD - 1)
            normed_high(2 * KD)

            def scores_out(h):
                m = M_S + h
                act.wait_ge(misc_done, m + 1)
                act_copy(x_f.rearrange("p (t a) -> p t a", t=TT)[:, :, 2 * h * KEYS:2 * (h + 1) * KEYS],
                         ps_m[:, m % 2, :].rearrange("p (t a) -> p t a", t=TT)).then_inc(misc_freed, 1)

            for n in range(16):
                next_high(SLAB_WQ, TILE_WQ, n)
                read_out(TILE_WQ, n, slot(n))
                for u in range(4 * n, 4 * n + 4 if n < 4 else 4 * n):
                    act.wait_ge(misc_done, M_TOK + u + 1)
                    dst, t, g = (y_tok, h_tok)[u // 8], (u // 4) % 2, u % 4
                    act_copy(dst[:, t, 512 * g:512 * g + 512], ps_m[:, (M_TOK + u) % 2, :]).then_inc(misc_freed, 1)
                if n in SCORE_AFTER:
                    scores_out(SCORE_AFTER.index(n))

            def softmax_exp(t):
                act.wait_ge(best_ready, t + 1)
                nc.scalar.activation(gates[:, t * P:(t + 1) * P], gates[:, t * P:(t + 1) * P], ACT.Exp).then_inc(best_exp, 1)

            softmax_exp(0)
            for t in range(TT):
                act.wait_ge(dots_ready, (t + 1) * PICKS)
                nc.scalar.activation(pick_w[:, t * P:(t + 1) * P], dots[:, t * P:(t + 1) * P], ACT.Gelu_apprx_tanh).then_inc(gelu_ready, 1)
                act.wait_ge(w_ready, t + 1)
                with act.Fori(0, ROUNDS) as i:
                    for n in range(PE_ROWS):
                        act.wait_ge(row_free[n], i + ((2 * t + 1) * ROUNDS + 1))
                        nc.scalar.activation(diag[:, n, :], ident[:, :], ACT.Copy,
                                             scale=pick_w[:, bass.ds(i * ROWS + (t * P + n), 1)]).then_inc(diag_ready, 1)
                if t == 0:
                    softmax_exp(1)
                nc.scalar.activation(small[:, 52:53], eps_c, ACT.Sqrt)
                act.wait_ge(y_ready, t + 1)
                nc.scalar.activation(onehot, y_tok[:, t, :], ACT.Square, accum_out=out_ss[:, t:t + 1]).then_inc(out_squared, 1)
                act.wait_ge(out_squared, t + 1)
                nc.scalar.activation(out_sd[:, t:t + 1], out_ss[:, t:t + 1], ACT.Sqrt, bias=eps_c, scale=1.0 / D).then_inc(out_rooted, 1)

        @block.vector
        def _(dve):
            own = Chain(dve, dve_step)
            v = nc.vector
            v.memset(eps_c, EPS).then_inc(eps_ready, 1)
            v.memset(ln_eps_c, LN_EPS).then_inc(eps_ready, 1)
            v.memset(ps_p, 0.0).then_inc(proj_freed, PSLOTS)
            v.memset(ps_o, 0.0).then_inc(out_ready, 1)

            for g in range(4):
                for t in range(TT):
                    m = M_X + TT * g + t
                    dve.wait_ge(misc_done, m + 1)
                    v.tensor_copy(x_t[:, 4 * g:4 * g + 4, t * P:(t + 1) * P],
                                  ps_m[:, m % 2, :].rearrange("p (a b) -> p a b", a=4)).then_inc(misc_freed, 1)
            dve.wait_ge(misc_done, M_VEC + 1)
            bank = ps_m[:, M_VEC % 2, :]
            own.step(v.tensor_copy(params[:, 0:90], bank[:, 0:90]))
            own.step(v.tensor_copy(params[:, 128:192], bank[:, 128:192]))
            own.step(v.tensor_copy(params[:, C_TAP:C_TAP + 124], bank[:, 256:380]))
            v.tensor_copy(params[:, C_TAP + 124:C_TAP + 248], bank[:, 384:508]).then_inc(misc_freed, 1)
            dve.wait_ge(misc_freed, M_VEC + 1)

            def invert_root(r):
                dve.wait_ge(rooted, r)
                v.reciprocal(rstd[:, 0:T], sdev[:, 0:T]).then_inc(rstd_ready, 1)
                dve.wait_ge(rstd_ready, r)

            def operand_low(group, k, src, n=2):
                dve.wait_ge(a_hi_ready, group + 1)
                v.tensor_tensor(a_lo[:, k:k + n, :], src, a_hi[:, k:k + n, :].bitcast(F32), ALU.subtract).then_inc(a_lo_ready, 1)

            def scale_residual(r, c0, group):
                invert_root(r)
                for g in range(KD // 2 + 1):
                    for k in range(2 * g, 2 * g + 2 if g < KD // 2 else 2 * g):
                        v.scalar_tensor_tensor(out=h_t[:, k, :], in0=x_t[:, k, :], scalar=params[:, k + c0:k + c0 + 1],
                                               in1=rstd[:, 0:T], op0=ALU.mult, op1=ALU.mult).then_inc(h_scaled, 1)
                    if g > 0:
                        operand_low(group + g - 1, 2 * g - 2, h_t[:, 2 * g - 2:2 * g, :])

            scale_residual(1, C_NORM, G_IN)

            dve.wait_ge(ssm_in, 16 * 3)
            buf = slots_f[0:PAIRS, 56 * T:63 * T].rearrange("p (a b) -> p a b", b=P)
            lam_re, lam_im, fac_re, fac_im = (buf[:, n, :] for n in range(4))
            a_re, a_im, t0, t1, t2, t3 = (buf[:, n, :] for n in (6, 7, 4, 5, 8, 9))
            t4, t5 = buf[:, 10, :], buf[:, 11, :]
            log_dt, dt = buf[:, 12, 0:2], buf[:, 12, 2:4]
            u0, u1, u2, u3 = (buf[:, 12, 8 + 8 * n:10 + 8 * n] for n in range(4))

            def scal(out, in0, s1, s2, op0, op1):
                own.do(v.tensor_scalar(out, in0, s1, s2, op0, op1))

            def stt(out, in0, s, in1, op0, op1):
                own.do(v.scalar_tensor_tensor(out=out, in0=in0, scalar=s, in1=in1, op0=op0, op1=op1))

            def tt(out, a, b, op):
                own.do(v.tensor_tensor(out, a, b, op))

            def exp(x, n, r, p, s):
                scal(r, x, -174.0, 176.0, ALU.max, ALU.min)
                scal(n, r, 1.4426950408889634, MAGIC, ALU.mult, ALU.add)
                scal(n, n, -MAGIC, None, ALU.add, ALU.bypass)
                stt(r, n, -0.693359375, r, ALU.mult, ALU.add)
                stt(r, n, 2.12194440e-4, r, ALU.mult, ALU.add)
                scal(p, r, 1.0 / 5040, None, ALU.mult, ALU.bypass)
                for c in (1.0 / 720, 1.0 / 120, 1.0 / 24, 1.0 / 6, 0.5, 1.0):
                    stt(p, p, c, r, ALU.add, ALU.mult)
                scal(p, p, 1.0, None, ALU.add, ALU.bypass)
                scal(r, n, 0.5, MAGIC, ALU.mult, ALU.add)
                scal(r, r, -MAGIC, None, ALU.add, ALU.bypass)
                tt(n, n, r, ALU.subtract)
                for half in (r, n):
                    scal(s.bitcast(I32), half, 127.0, 8388608.0, ALU.add, ALU.mult)
                    tt(p, p, s, ALU.mult)

            exp(log_dt, u0, u1, dt, u2)
            for s in range(2):
                own.do(v.tensor_scalar(t0[:, s * STATE:(s + 1) * STATE], a_re[:, s * STATE:(s + 1) * STATE],
                                       dt[:, s:s + 1], None, ALU.mult))
            exp(t0, t1, t2, t3, t4)
            for s in range(2):
                own.do(v.tensor_scalar(t0[:, s * STATE:(s + 1) * STATE], a_im[:, s * STATE:(s + 1) * STATE],
                                       dt[:, s:s + 1], None, ALU.mult))
            scal(t1, t0, 0.6366197723675814, MAGIC, ALU.mult, ALU.add)
            scal(t1, t1, -MAGIC, None, ALU.add, ALU.bypass)
            for c in (1.5703125, 4.837512969970703e-4, 7.549789948768648e-8):
                stt(t0, t1, -c, t0, ALU.mult, ALU.add)
            scal(t2, t1, 0.25, -0.375, ALU.mult, ALU.add)
            scal(t2, t2, MAGIC, None, ALU.add, ALU.bypass)
            scal(t2, t2, -MAGIC, None, ALU.add, ALU.bypass)
            stt(t1, t2, -4.0, t1, ALU.mult, ALU.add)
            tt(t2, t0, t0, ALU.mult)
            scal(t4, t2, 1.0 / 362880, None, ALU.mult, ALU.bypass)
            for c in (-1.0 / 5040, 1.0 / 120, -1.0 / 6):
                stt(t4, t4, c, t2, ALU.add, ALU.mult)
            stt(t4, t4, 1.0, t0, ALU.add, ALU.mult)
            scal(t5, t2, -1.0 / 3628800, None, ALU.mult, ALU.bypass)
            for c in (1.0 / 40320, -1.0 / 720, 1.0 / 24, -0.5):
                stt(t5, t5, c, t2, ALU.add, ALU.mult)
            scal(t5, t5, 1.0, None, ALU.add, ALU.bypass)
            scal(t0, t1, 1.0, None, ALU.is_equal, ALU.bypass)
            stt(t0, t1, 3.0, t0, ALU.is_equal, ALU.add)
            scal(t2, t0, -1.0, 1.0, ALU.mult, ALU.add)
            tt(lam_re, t0, t4, ALU.mult)
            tt(fac_re, t2, t5, ALU.mult)
            tt(lam_re, lam_re, fac_re, ALU.add)
            tt(lam_im, t0, t5, ALU.mult)
            tt(fac_im, t2, t4, ALU.mult)
            tt(lam_im, lam_im, fac_im, ALU.add)
            scal(t2, t1, 2.0, None, ALU.is_ge, ALU.bypass)
            scal(t2, t2, -2.0, 1.0, ALU.mult, ALU.add)
            tt(lam_im, lam_im, t2, ALU.mult)
            scal(t2, t1, 1.0, None, ALU.is_equal, ALU.bypass)
            stt(t2, t1, 2.0, t2, ALU.is_equal, ALU.add)
            scal(t2, t2, -2.0, 1.0, ALU.mult, ALU.add)
            tt(lam_re, lam_re, t2, ALU.mult)
            tt(lam_re, lam_re, t3, ALU.mult)
            tt(lam_im, lam_im, t3, ALU.mult)
            tt(t0, a_re, a_re, ALU.mult)
            tt(t1, a_im, a_im, ALU.mult)
            tt(t0, t0, t1, ALU.add)
            own.do(v.reciprocal(t1, t0))
            scal(t2, lam_re, -1.0, None, ALU.add, ALU.bypass)
            tt(t3, t2, a_re, ALU.mult)
            tt(t4, lam_im, a_im, ALU.mult)
            tt(t3, t3, t4, ALU.add)
            tt(fac_re, t3, t1, ALU.mult)
            tt(t3, lam_im, a_re, ALU.mult)
            tt(t4, t2, a_im, ALU.mult)
            tt(t3, t3, t4, ALU.subtract)
            v.tensor_tensor(fac_im, t3, t1, ALU.mult).then_inc(ssm_coef, 1)

            dve.wait_ge(misc_done, M_LAM + 1)
            v.tensor_copy(lam_f[:, :, :], ps_m[:, M_LAM % 2, :].rearrange("p (a b) -> p a b", a=4)[:, :, 0:PAIRS]).then_inc(misc_freed, 1)
            dve.wait_ge(misc_freed, M_LAM + 1)
            pw = att_qk[:, 0:256], att_qk[:, 256:512]
            dve.wait_ge(misc_done, M_X + 8)
            for c in range(2):
                own.step(v.tensor_copy(powers[:, c, 0, :], lam_f[:, c, :]))
            own.wait()
            n = 1
            while n < CHUNK:
                re, im = powers[:, 0, 0:n, :], powers[:, 1, 0:n, :]
                by_re, by_im = (powers[:, c, n - 1, :].unsqueeze(1).broadcast_to([P, n, PAIRS]) for c in range(2))
                s0, s1 = (p[:, 0:n * PAIRS].rearrange("p (a b) -> p a b", a=n) for p in pw)
                for c, (p, q, op) in enumerate(((by_re, by_im, ALU.subtract), (by_im, by_re, ALU.add))):
                    own.step(v.tensor_tensor(s0, re, p, ALU.mult))
                    own.do(v.tensor_tensor(s1, im, q, ALU.mult))
                    own.do(v.tensor_tensor(powers[:, c, n:2 * n, :], s0, s1, op))
                n *= 2
            dve.wait_ge(b_in, 32)
            own.do(v.memset(b_diag, 0.0))
            f_re, f_im = (lam_f[:, 2 + c, :].unsqueeze(2).broadcast_to([P, PAIRS, GCH]) for c in range(2))
            pw3 = att_qk.rearrange("p (a b) -> p a b", b=GCH)
            pw4 = work[:, 1024:1536].rearrange("p (a b) -> p a b", b=GCH)
            for c, (p, q, op) in enumerate(((f_re, f_im, ALU.subtract), (f_im, f_re, ALU.add))):
                own.step(v.tensor_tensor(pw3, b_nat[:, 0, :, :], p, ALU.mult))
                own.do(v.tensor_tensor(pw4, b_nat[:, 1, :, :], q, ALU.mult))
                for s in range(2):
                    half = slice(s * STATE, (s + 1) * STATE)
                    own.step(v.tensor_tensor(b_diag[half, c, :, s * GCH:(s + 1) * GCH], pw3[half], pw4[half], op))
                own.wait()
            v.tensor_copy(small[:, 40:41], small[:, 0:1]).then_inc(bdiag_ready, 1)

            dve.wait_ge(mask_ready, 2)
            with dve.Fori(0, 4) as i:
                for e in range(2):
                    head = i * 2 + e
                    dve.wait_ge(rooted, head + 2)
                    v.reciprocal(rstd, sdev).then_inc(rstd_ready, 1)
                    dve.wait_ge(rstd_ready, head + 2)
                    for c, (s0, gain) in enumerate(((Q0, C_QG), (K0, C_KG))):
                        v.scalar_tensor_tensor(out=att_qk[:, c * T:(c + 1) * T], in0=slot(head + s0),
                                               scalar=params[:, gain:gain + 1], in1=rstd[:, c * T:(c + 1) * T],
                                               op0=ALU.mult, op1=ALU.mult).then_inc(qk_ready, 1)
                    dve.wait_ge(v_turned, head + 1)
                    v.tensor_copy(att_vtok, ps_o.rearrange("p (a b) -> p a b", a=2)).then_inc(v_ready, 1)
                    dve.wait_ge(scores_done, head + 1)
                    own_at = head * 4 + own.n
                    v.tensor_tensor(att_s, ps_s, mask, ALU.add).then_inc(dve_step, 1)
                    dve.wait_ge(dve_step, own_at + 1)
                    v.tensor_reduce(att_max[:, 0:1], att_s[:, 0:P], AX_X, ALU.max).then_inc(dve_step, 1)
                    v.tensor_reduce(att_max[:, 1:2], att_s[:, P:3 * P], AX_X, ALU.max).then_inc(dve_step, 1)
                    dve.wait_ge(dve_step, own_at + 3)
                    v.tensor_scalar(att_nmax, att_max, -HEAD_DIM ** -0.5, None, ALU.mult).then_inc(nmax_ready, 1)
                    dve.wait_ge(exp_ready, head * 2 + 2)
                    v.reciprocal(att_rsum, att_sum).then_inc(dve_step, 1)
                    dve.wait_ge(dve_step, own_at + 4)
                    for j, (lo, hi) in enumerate(((0, P), (P, 3 * P))):
                        v.tensor_scalar(att_p[:, lo:hi], att_p[:, lo:hi], att_rsum[:, j:j + 1], None,
                                        ALU.mult).then_inc(probs_ready, 1)
            own.n += 4 * HEADS

            dve.wait_ge(proj_freed, freed(56))
            own.do(v.tensor_tensor(slot(CG0, KH), slot(CG0, KH), slot(HC0, KH), ALU.mult))
            for tap in (2, 1, 0):
                lag = 2 - tap
                for n in range(KH):
                    w = params[:, C_CONV + tap * KH + n:C_CONV + tap * KH + n + 1]
                    u, y = slot(CG0 + n), slot(HC0 + n)
                    if lag == 0:
                        ins = v.tensor_scalar(y, u, w, None, ALU.mult)
                    else:
                        ins = v.scalar_tensor_tensor(out=y[:, lag:T], in0=u[:, 0:T - lag], scalar=w, in1=y[:, lag:T],
                                                     op0=ALU.mult, op1=ALU.add)
                    own.step(ins)
                own.wait()
            v.tensor_tensor(slot(HC0, KH), slot(HC0, KH), slot(BG0, KH), ALU.mult).then_inc(yconv_raw, 1)

            def norm_branch(r, s0, c0):
                invert_root(r)
                for n in range(KH):
                    own.step(v.scalar_tensor_tensor(out=slot(s0 + n), in0=slot(s0 + n), scalar=params[:, c0 + n:c0 + n + 1],
                                                    in1=rstd[:, 0:T], op0=ALU.mult, op1=ALU.mult))
                own.wait()

            norm_branch(10, Q0, C_AOUT)
            dve.wait_ge(za_silu, 1)
            v.tensor_tensor(slot(Q0, KH), slot(Q0, KH), slot(ZA0, KH), ALU.mult).then_inc(y_final, 1)
            norm_branch(11, HC0, C_COUT)
            for n in range(KH):
                dve.wait_ge(proj_freed, freed(56 + n + 1))
                v.tensor_tensor(slot(HC0 + n), slot(HC0 + n), slot(ZC0 + n), ALU.mult).then_inc(y_final, 1)
            for g, (s0, k, done) in enumerate(MIX):
                dve.wait_ge(y_final, done)
                operand_low(G_MIX + g, k, slots[:, s0:s0 + 4, :], 4)

            def add_residual(tile0, q0):
                for n in range(KD + 2):
                    if n < KD:
                        dve.wait_ge(proj_done, tile0 + n + 1)
                        v.tensor_tensor(x_t[:, n, :], x_t[:, n, :], ps_p[:, n % PSLOTS, :], ALU.add).then_inc(proj_freed, 1)
                    if n == 3:
                        dve.wait_ge(squared, q0 + 2)
                        v.tensor_tensor(sq_acc, sq[:, 0, :], sq[:, 1, :], ALU.add).then_inc(sq_summed, 2)
                    elif n > 3:
                        dve.wait_ge(squared, q0 + n - 1)
                        dve.wait_ge(sq_summed, q0 + n - 2)
                        v.tensor_tensor(sq_acc, sq_acc, sq[:, (n - 2) % SQ, :], ALU.add).then_inc(sq_summed, 1)

            add_residual(TILE_OUT, 32)
            scale_residual(12, C_MIX, G_IN2)

            prod = [norm_ws[:, 1024 + 256 * n:1280 + 256 * n] for n in range(4)]

            def rotate(here, before, lam, width):
                p0, p1, p2, p3 = (p[:, 0:HPAIRS * width].rearrange("p (r k) -> p r k", r=HPAIRS) for p in prod)
                (re, im), (b_re, b_im), (l_re, l_im) = here, before, lam
                own.wait(1)
                own.step(v.tensor_tensor(p0, b_re, l_re, ALU.mult))
                own.step(v.tensor_tensor(p1, b_re, l_im, ALU.mult))
                own.wait(2)
                own.step(v.tensor_tensor(p2, b_im, l_im, ALU.mult))
                own.step(v.tensor_tensor(p3, b_im, l_re, ALU.mult))
                own.wait(3)
                own.step(v.tensor_tensor(re, re, p0, ALU.add))
                own.wait(3)
                own.step(v.tensor_tensor(im, im, p1, ALU.add))
                own.wait(1)
                own.step(v.tensor_tensor(re, re, p2, ALU.subtract))
                own.wait(1)
                own.step(v.tensor_tensor(im, im, p3, ALU.add))

            def scan(half):
                dve.wait_ge(misc_freed, M_BU[half] + 16)
                pairs = slice(HPAIRS * half, HPAIRS * half + HPAIRS)

                def power(j, width):
                    if isinstance(j, int):
                        p = [powers[:, c, j, pairs] for c in range(2)]
                    else:
                        p = [powers[:, c, bass.ds(j, 1), pairs].rearrange("p o r -> p (o r)") for c in range(2)]
                    return [x.unsqueeze(2).broadcast_to([P, HPAIRS, width]) for x in p]

                def token(j):
                    x = xs_j[:, :, bass.ds(j, 1)].rearrange("p (c r k) o -> p c r (k o)", c=2, r=HPAIRS)
                    return x[:, 0], x[:, 1]

                lam1 = power(0, CHUNKS)
                own.wait()
                with own.loop(1, CHUNK, 8) as j:
                    rotate(token(j), token(j - 1), lam1, CHUNKS)
                own.wait()
                lam16 = [powers[:, c, CHUNK - 1, pairs].unsqueeze(1).unsqueeze(3).broadcast_to([P, 2, HPAIRS, 1]) for c in range(2)]
                w1, w2 = (p[:, 0:2 * HPAIRS].rearrange("p (c r k) -> p c r k", c=2, r=HPAIRS) for p in prod[0:2])
                flat = lambda w: w.rearrange("p c r k -> p (c r k)")
                with own.loop(1, CHUNKS, 5) as k:
                    before = xs_cj[:, :, bass.ds(k - 1, 1), CHUNK - 1:CHUNK].rearrange("p (c r) k j -> p c r (k j)", c=2)
                    here = xs_cj[:, :, bass.ds(k, 1), CHUNK - 1:CHUNK].rearrange("p a k j -> p (a k j)")
                    n = HPAIRS
                    own.step(v.tensor_tensor(w1, before, lam16[0], ALU.mult))
                    own.do(v.tensor_tensor(w2, before, lam16[1], ALU.mult))
                    own.do(v.tensor_tensor(here, here, flat(w1), ALU.add))
                    own.step(v.tensor_tensor(here[:, 0:n], here[:, 0:n], flat(w2)[:, n:2 * n], ALU.subtract))
                    own.do(v.tensor_tensor(here[:, n:2 * n], here[:, n:2 * n], flat(w2)[:, 0:n], ALU.add))
                carry = xs_cj[:, :, 0:CHUNKS - 1, CHUNK - 1].rearrange("p (c r) k -> p c r k", c=2)
                with own.loop(0, CHUNK - 1, 8) as j:
                    here = xs_cj[:, :, 1:CHUNKS, bass.ds(j, 1)].rearrange("p (c r) k o -> p c r (k o)", c=2)
                    rotate((here[:, 0], here[:, 1]), (carry[:, 0], carry[:, 1]), power(j, CHUNKS - 1), CHUNKS - 1)
                own.wait()
                v.tensor_copy(small[:, 41 + half:42 + half], small[:, 0:1]).then_inc(scanned, 1)

            def skip_sum(half):
                for n in range(4):
                    a, m = 4 * half + n, M_CY[half] + n
                    dve.wait_ge(misc_done, m + 1)
                    own.do(v.scalar_tensor_tensor(out=slot(SSM0 + a), in0=slot(SSM0 + a), scalar=params[:, C_SKIP + a:C_SKIP + a + 1],
                                                  in1=ps_m[:, m % 2, 0:T], op0=ALU.mult, op1=ALU.add))
                    v.tensor_copy(small[:, 44:45], small[:, 0:1]).then_inc(ssm_sum, 1)
                    v.tensor_copy(small[:, 45:46], small[:, 0:1]).then_inc(misc_freed, 1)

            scan(0)
            skip_sum(0)
            scan(1)
            skip_sum(1)

            dve.wait_ge(misc_done, M_CY[1] + 4)
            dve.wait_ge(proj_freed, freed(TILE_IN2 + 24))
            own.step(v.memset(glu_pad[:, :, 0:TAPS2 - 1], 0.0))
            own.do(v.tensor_tensor(glu_pad[:, :, TAPS2 - 1:], slots[:, GLU0:GLU0 + KH, :], slots[:, SIG0:SIG0 + KH, :], ALU.mult))
            v.tensor_copy(small[:, 51:52], small[:, 0:1]).then_inc(glu_ready, 1)
            for n in range(KH):
                last = TAPS2 - 1
                w = params[:, C_TAP + last * KH + n:C_TAP + last * KH + n + 1]
                own.step(v.tensor_scalar(slot(CONV0 + n), glu_pad[:, n, last:last + T], w, params[:, C_CB + n:C_CB + n + 1],
                                         ALU.mult, ALU.add))

            def taps(first, last):
                with own.loop(first, last, KH) as tap:
                    for n in range(KH):
                        own.wait(KH - 1)
                        own.step(v.scalar_tensor_tensor(out=slot(CONV0 + n), in0=glu_pad[:, n, bass.ds(tap, T)],
                                                        scalar=params[:, bass.ds(tap * KH + (C_TAP + n), 1)], in1=slot(CONV0 + n),
                                                        op0=ALU.mult, op1=ALU.add))

            def gate_values(g):
                dve.wait_ge(proj_freed, freed(TILE_VG + 8 * g + 8))
                val = VAL0 * (1 - g % 2)
                own.do(v.tensor_tensor(slot(val, 4), slot(val, 4), slot(val + 4, 4), ALU.mult))
                v.tensor_tensor(slot(GB0 + 4 * g, 4), slot(GB0 + 4 * g, 4), slot(val, 4), ALU.mult).then_inc(val_gated, 1)

            taps(0, 10)
            for g in range(2):
                operand_low(G_Z + g, 4 * g, slots[:, SSM0 + 4 * g:SSM0 + 4 * g + 4, :], 4)
            taps(10, 17)
            gate_values(0)
            taps(17, 23)
            gate_values(1)
            taps(23, TAPS2 - 1)
            own.wait()
            v.tensor_copy(small[:, 43:44], small[:, 0:1]).then_inc(conv_done, 1)
            dve.wait_ge(rooted, 13)
            conv = slots[:, CONV0:CONV0 + KH, :]
            own.do(v.tensor_tensor(conv, conv, sdev[:, 0:T].unsqueeze(1).broadcast_to([P, KH, T]), ALU.subtract))
            v.tensor_copy(small[:, 46:47], small[:, 0:1]).then_inc(centred, 1)
            v.tensor_copy(small[:, 47:48], small[:, 0:1]).then_inc(rstd_ready, 1)
            gate_values(2)
            invert_root(14)
            for n in range(KH):
                v.scalar_tensor_tensor(out=slot(CONV0 + n), in0=slot(CONV0 + n), scalar=params[:, C_LNG + n:C_LNG + n + 1],
                                       in1=rstd[:, 0:T], op0=ALU.mult, op1=ALU.mult).then_inc(ln_scaled, 1)
            for g in range(KH // 2):
                operand_low(G_CV + g, KH + 2 * g, slots[:, CONV0 + 2 * g:CONV0 + 2 * g + 2, :])
            gate_values(3)
            dve.wait_ge(val_gated, 4)
            for n in range(KD):
                dve.wait_ge(proj_done, TILE_CV + n + 1)
                v.tensor_tensor(slot(GA0 + n), slot(GA0 + n), ps_p[:, n % PSLOTS, :], ALU.mult).then_inc(proj_freed, 1)
                dve.wait_ge(proj_freed, freed(TILE_CV + n + 1))
                v.tensor_tensor(slot(GA0 + n), slot(GA0 + n), slot(GB0 + n), ALU.add).then_inc(merged, 1)
                if n % 2 and 2 < n < KH + 2:
                    operand_low(G_MERGE + n // 2 - 1, n - 3, slots[:, GA0 + n - 3:GA0 + n - 1, :])
            for g in range(KH // 2, KD // 2):
                operand_low(G_MERGE + g, 2 * g, slots[:, GA0 + 2 * g:GA0 + 2 * g + 2, :])

            add_residual(TILE_OUT2, 56)
            scale_residual(15, C_FFN, G_Q)

            s4 = tk_s.rearrange("p (h c k) -> p h c k", h=PEER_H, c=2)

            def best16(src, val, idx):
                n = range(len(src))
                for half in range(2):
                    at = slice(8 * half, 8 * half + 8)
                    for m in n:
                        own.step(v.max(val[m][:, at], src[m]))
                    own.wait()
                    for m in n:
                        own.step(v.max_index(idx[m][:, at], val[m][:, at], src[m]))
                    if half == 0:
                        for m in n:
                            own.step(v.match_replace(src[m], val[m][:, at], src[m], -3.0e38))
                    own.wait()

            def head_picks(t, h):
                dve.wait_ge(misc_freed, M_S + h + 1)
                own.wait()
                two = range(2)
                best16([key_s[:, t, 2 * h + c, :] for c in two], [tk_s[:, (2 * h + c) * 16:(2 * h + c + 1) * 16] for c in two],
                       [tk_iu[:, (2 * h + c) * 16:(2 * h + c + 1) * 16] for c in two])
                own.do(v.tensor_tensor(tk_cand.rearrange("p (a b) -> p a b", a=16),
                                       s4[:, h, 0, :].unsqueeze(2).broadcast_to([P, 16, 16]),
                                       s4[:, h, 1, :].unsqueeze(1).broadcast_to([P, 16, 16]), ALU.add))
                best16([tk_cand], [tk_best[:, h * 16:(h + 1) * 16]], [tk_pos[:, h * 16:(h + 1) * 16]])

            def experts(t, first, last):
                own.wait()
                dve.wait_ge(zero_ready, 1)
                n, at = (last - first) * PEER_K, slice(first * PEER_K, last * PEER_K)
                keys = slice(first * 2 * PEER_K, last * 2 * PEER_K)
                own.step(v.tensor_scalar(tk_hi[:, at], tk_pos[:, at], 4, None, ALU.logical_shift_right))
                own.step(v.tensor_scalar(tk_lo[:, at], tk_pos[:, at], 15, None, ALU.bitwise_and))
                own.do(v.tensor_copy(tk_if[:, keys], tk_iu[:, keys]))
                own.step(v.tensor_copy(tk_hif[:, at], tk_hi[:, at]))
                own.do(v.tensor_copy(tk_lof[:, at], tk_lo[:, at]))
                i4 = tk_if[:, keys].rearrange("p (h c k) -> p h c k", h=last - first, c=2)
                hot = onehot[:, 0:n * 16].rearrange("p (n a) -> p n a", a=16)
                hot4 = onehot[:, 0:n * 16].rearrange("p (h k a) -> p h k a", h=last - first, k=PEER_K)
                for c, (pos, e) in enumerate(((tk_hif, tk_e1), (tk_lof, tk_e2))):
                    own.do(v.tensor_tensor(hot, pos[:, at].unsqueeze(2).broadcast_to([P, n, 16]),
                                           iota16.unsqueeze(1).broadcast_to([P, n, 16]), ALU.is_equal))
                    own.do(v.tensor_tensor(hot4, hot4, i4[:, :, c, :].unsqueeze(2).broadcast_to([P, last - first, PEER_K, 16]), ALU.mult))
                    own.do(v.tensor_reduce(e[:, at], hot, AX_X, ALU.add))
                ids = picks[:, t * P + first * PEER_K:t * P + last * PEER_K]
                ins = v.scalar_tensor_tensor(out=ids, in0=tk_e1[:, at], scalar=float(KEYS), in1=tk_e2[:, at], op0=ALU.mult, op1=ALU.add)
                ins.then_inc(picks_ready, 1)

            def softmax(t):
                g, best = (a.rearrange("p (h k) -> p h k", h=PEER_H) for a in (gates[:, t * P:(t + 1) * P], tk_best))
                own.wait()
                v.tensor_tensor(g, best, best[:, :, 0:1].broadcast_to([P, PEER_H, PEER_K]), ALU.subtract).then_inc(best_ready, 1)
                dve.wait_ge(best_exp, t + 1)
                own.do(v.tensor_reduce(head_sum, g, AX_X, ALU.add))
                own.do(v.reciprocal(head_rs, head_sum))
                own.do(v.tensor_tensor(g, g, head_rs.unsqueeze(2).broadcast_to([P, PEER_H, PEER_K]), ALU.mult))

            for h in range(PEER_H):
                head_picks(0, h)
                for first, last in HEAD_PARTS:
                    if h == last - 1:
                        experts(0, first, last)
            softmax(0)

            def dot_rows(t):
                with dve.Fori(0, ROUNDS) as i:
                    for n in range(ROWS):
                        dve.wait_ge(gathered[n], (i + (2 * t * ROUNDS + 1)) * 16)
                        v.scalar_tensor_tensor(out=rows[n], in0=rows[n], scalar=1.0, in1=h_tok[:, t, :], op0=ALU.mult,
                                               op1=ALU.mult, accum_out=dots[:, bass.ds(i * ROWS + (t * P + n), 1)]).then_inc(row_free[n], 1)
                for n in range(ROWS):
                    dve.wait_ge(row_free[n], (2 * t + 1) * ROUNDS + 1)
                v.tensor_copy(small[:, 48:49], small[:, 0:1]).then_inc(dots_ready, PICKS)
                dve.wait_ge(gelu_ready, t + 1)
                cols = slice(t * P, (t + 1) * P)
                v.tensor_tensor(pick_w[:, cols], pick_w[:, cols], gates[:, cols], ALU.mult).then_inc(w_ready, 1)
                dve.wait_ge(w_ready, t + 1)

            def add_rows(t, i):
                for n in range(PE_ROWS, ROWS):
                    dve.wait_ge(gathered[n], (i + ((2 * t + 1) * ROUNDS + 1)) * 16)
                    at = i * ROWS + (t * P + n)
                    w = pick_w[:, at:at + 1] if isinstance(at, int) else pick_w[:, bass.ds(at, 1)]
                    v.scalar_tensor_tensor(out=y_tok[:, t, :], in0=rows[n], scalar=w, in1=y_tok[:, t, :],
                                           op0=ALU.mult, op1=ALU.add).then_inc(row_free[n], 1)
                    dve.wait_ge(row_free[n], i + ((2 * t + 1) * ROUNDS + 2))

            def add_sums(t):
                dve.wait_ge(v_summed, t + 1)
                own.do(v.tensor_tensor(y_tok[:, t, :].rearrange("p (c n) -> p c n", c=4), y_tok[:, t, :].rearrange("p (c n) -> p c n", c=4),
                                       ps_v, ALU.add))
                v.tensor_copy(small[:, 49:50], small[:, 0:1]).then_inc(v_read, 1)

            def finish(t):
                v.tensor_copy(small[:, 50:51], small[:, 0:1]).then_inc(y_ready, 1)
                dve.wait_ge(out_rooted, t + 1)
                own.do(v.reciprocal(out_rs[:, t:t + 1], out_sd[:, t:t + 1]))
                dve.wait_ge(gain_in, 16)
                for half in range(2):
                    cols = slice(half * HALF, (half + 1) * HALF)
                    v.scalar_tensor_tensor(out=y_tok[:, t, cols], in0=y_tok[:, t, cols], scalar=out_rs[:, t:t + 1],
                                           in1=gain_b[:, cols], op0=ALU.mult, op1=ALU.mult).then_inc(normed, 1)

            dve.wait_ge(misc_freed, M_S + 8)
            dot_rows(0)
            for i in range(ROUNDS):
                if i == ROUNDS - 1:
                    experts(1, 0, PEER_H)
                    softmax(1)
                if i < PEER_H:
                    head_picks(1, i)
                add_rows(0, i)
            add_sums(0)
            finish(0)
            dot_rows(1)
            with dve.Fori(0, ROUNDS) as i:
                add_rows(1, i)
            add_sums(1)
            finish(1)


_INPUTS = [
    "x", "norm_gain", "w_in", "conv_w", "q_norm_gain", "k_norm_gain", "conv_out_gain", "attn_out_gain", "w_out",
    "norm_mix_2", "w_in_2", "b_gate_2", "conv_w_dw_2", "conv_b_dw_2", "conv_ln_g_2", "conv_ln_b_2", "conv_w_out_2",
    "ssm_a_re_2", "ssm_a_im_2", "ssm_log_dt_2", "ssm_b_re_2", "ssm_b_im_2", "ssm_c_re_2", "ssm_c_im_2", "ssm_d_2",
    "ssm_w_val_2", "ssm_w_gate_2", "w_out_2", "norm_ffn_2", "peer_w_q_2", "peer_sub_keys_2", "peer_u_2", "peer_v_2",
    "norm_final_2",
]


def kernel(**inputs):
    import numpy as np
    import concourse.bacc as bacc
    from concourse.bass_utils import run_bass_kernel_spmd

    nc = bacc.Bacc("TRN2", target_bir_lowering=False, num_devices=1)
    arrays, aps = {}, {}
    for name in _INPUTS:
        a = np.ascontiguousarray(inputs[name])
        arrays[f"in_{name}"] = a
        aps[name] = nc.dram_tensor(f"in_{name}", a.shape, mybir.dt.from_np(a.dtype), kind="ExternalInput").ap()
    aps["out"] = nc.dram_tensor("out_y", (1, T, D), F32, kind="ExternalOutput").ap()
    build(nc, aps)
    result = run_bass_kernel_spmd(nc, [arrays], core_ids=[0])
    return result.results[0]["out_y"]
```
